# Optimizing a Trainium2 kernel written in Bass

```python
import jax, jax.numpy as jnp
from jax import lax
import numpy as np
import math

D_MODEL = 2048
BATCH = 1
SEQ = 256
DEPTH = 2

GRID_W = 64
CTX_LEN = 256

HEAD_DIM = 128
N_Q_HEADS = 8
N_KV_HEADS = 2
Q_PER_KV = N_Q_HEADS // N_KV_HEADS
ATTN_W = N_Q_HEADS * HEAD_DIM
KV_W = N_KV_HEADS * HEAD_DIM
Q_BLOCK = 128
ATTN_SCALE = HEAD_DIM ** -0.5
ROPE_THETA = 10000.0
AXIS_DIM = HEAD_DIM // 2
N_FREQ = AXIS_DIM // 2

CONV_CH = 1024
CONV_WIDTH = 31

CHUNK = 128
SGU_W = D_MODEL
SGU_GROUPS = 8
SGU_GW = SGU_W // SGU_GROUPS

EV_SPLITS = [KV_W, 2 * KV_W, 2 * KV_W + ATTN_W, 2 * KV_W + 2 * ATTN_W,
             2 * KV_W + 2 * ATTN_W + 2 * CONV_CH]
EV_IN = 2 * KV_W + 2 * ATTN_W + 3 * CONV_CH
EV_MIX = ATTN_W + CONV_CH
OD_IN = 3 * SGU_W

N_EVEN = (DEPTH + 1) // 2
N_ODD = DEPTH // 2
EPS = 1e-6


def rmsnorm(x, g):
    xf = x.astype(jnp.float32)
    y = xf * lax.rsqrt(jnp.mean(xf * xf, axis=-1, keepdims=True) + EPS)
    return (y * g.astype(jnp.float32)).astype(x.dtype)

def layernorm(x, g, b):
    xf = x.astype(jnp.float32)
    mu = jnp.mean(xf, axis=-1, keepdims=True)
    var = jnp.mean(jnp.square(xf - mu), axis=-1, keepdims=True)
    y = (xf - mu) * lax.rsqrt(var + EPS)
    return (y * g.astype(jnp.float32) + b.astype(jnp.float32)).astype(x.dtype)

def modulate(h, shift, scale):
    return h * (1.0 + scale) + shift

def axial_rope_tables(n):
    rows = n // GRID_W
    row = jnp.repeat(jnp.arange(rows, dtype=jnp.float32), GRID_W)
    col = jnp.tile(jnp.arange(GRID_W, dtype=jnp.float32), rows)
    inv = jnp.power(ROPE_THETA, jnp.arange(N_FREQ, dtype=jnp.float32) * (-2.0 / AXIS_DIM))
    ang = jnp.concatenate([row[:, None] * inv, col[:, None] * inv], axis=-1)
    return jnp.cos(ang), jnp.sin(ang)

def apply_rope(x, cos, sin):
    shp = x.shape
    xf = x.astype(jnp.float32).reshape(shp[:-1] + (HEAD_DIM // 2, 2))
    x1, x2 = xf[..., 0], xf[..., 1]
    cs, sn = cos[None, :, None, :], sin[None, :, None, :]
    out = jnp.stack([x1 * cs - x2 * sn, x1 * sn + x2 * cs], axis=-1)
    return out.reshape(shp).astype(x.dtype)

def latent_attention(q, k_lat, v_lat, k_ctx, v_ctx):
    bsz, n = q.shape[:2]
    k_all = jnp.concatenate([k_lat, k_ctx], axis=1)
    v_all = jnp.concatenate([v_lat, v_ctx], axis=1)
    nb = n // Q_BLOCK
    qb = q.reshape(bsz, nb, Q_BLOCK, N_KV_HEADS, Q_PER_KV, HEAD_DIM).transpose(1, 0, 2, 3, 4, 5)

    def block(qi):
        s = jnp.einsum('bqhgd,bkhd->bhgqk', qi, k_all).astype(jnp.float32) * ATTN_SCALE
        p = jax.nn.softmax(s, axis=-1)
        return jnp.einsum('bhgqk,bkhd->bqhgd', p.astype(v_all.dtype), v_all)

    out = lax.map(block, qb)
    return out.transpose(1, 0, 2, 3, 4, 5).reshape(bsz, n, ATTN_W)

def context_attention(q, k, v):
    bsz, l = q.shape[:2]
    qg = q.reshape(bsz, l, N_KV_HEADS, Q_PER_KV, HEAD_DIM)
    s = jnp.einsum('bqhgd,bkhd->bhgqk', qg, k).astype(jnp.float32) * ATTN_SCALE
    p = jax.nn.softmax(s, axis=-1)
    o = jnp.einsum('bhgqk,bkhd->bqhgd', p.astype(v.dtype), v)
    return o.reshape(bsz, l, ATTN_W)

def conformer_conv(pair, dw_w, dw_b, ln_g, ln_b):
    a, b = jnp.split(pair, 2, axis=-1)
    y = a * jax.nn.sigmoid(b)
    y = lax.conv_general_dilated(
        y, dw_w[:, None, :], window_strides=(1,),
        padding=[(CONV_WIDTH // 2, CONV_WIDTH // 2)],
        dimension_numbers=('NWC', 'WIO', 'NWC'),
        feature_group_count=CONV_CH) + dw_b
    return jax.nn.silu(layernorm(y, ln_g, ln_b))

def spatial_gating(uv, ln_g, ln_b, ws, bs):
    bsz, n = uv.shape[:2]
    u, v = jnp.split(jax.nn.gelu(uv), 2, axis=-1)
    v = layernorm(v, ln_g, ln_b).reshape(bsz, n // CHUNK, CHUNK, SGU_GROUPS, SGU_GW)
    mixed = jnp.einsum('gij,bcjgd->bcigd', ws, v) + bs.T[None, None, :, :, None]
    return u * mixed.reshape(bsz, n, SGU_W)

def first_inputs(seed: int = 0) -> dict:
    key = jax.random.key(seed)
    ks = iter(jax.random.split(key, 32))

    def nrm(shape, scale):
        return jax.random.normal(next(ks), shape, jnp.float32) * scale

    d = D_MODEL
    return {
        "x": nrm((BATCH, SEQ, d), 1.0),
        "c": nrm((BATCH, d), 1.0),
        "ctx": nrm((BATCH, CTX_LEN, d), 1.0),
        "c_ctx": nrm((d,), 1.0),
        "ada_w": nrm((DEPTH, d, 3 * d), 0.5 * d ** -0.5),
        "ada_b": nrm((DEPTH, 3 * d), 0.02),
        "norm_g": 1.0 + nrm((DEPTH, d), 0.02),
        "ev_w_in": nrm((N_EVEN, d, EV_IN), d ** -0.5),
        "ev_q_norm": 1.0 + nrm((N_EVEN, HEAD_DIM), 0.02),
        "ev_k_norm": 1.0 + nrm((N_EVEN, HEAD_DIM), 0.02),
        "ev_dw_w": nrm((N_EVEN, CONV_WIDTH, CONV_CH), CONV_WIDTH ** -0.5),
        "ev_dw_b": nrm((N_EVEN, CONV_CH), 0.02),
        "ev_ln_g": 1.0 + nrm((N_EVEN, CONV_CH), 0.02),
        "ev_ln_b": nrm((N_EVEN, CONV_CH), 0.02),
        "ev_w_out": nrm((N_EVEN, EV_MIX, d), EV_MIX ** -0.5),
        "od_w_in": nrm((N_ODD, d, OD_IN), d ** -0.5),
        "od_ln_g": 1.0 + nrm((N_ODD, SGU_W), 0.02),
        "od_ln_b": nrm((N_ODD, SGU_W), 0.02),
        "od_ws": nrm((N_ODD, SGU_GROUPS, CHUNK, CHUNK), CHUNK ** -0.5),
        "od_bs": 1.0 + nrm((N_ODD, SGU_GROUPS, CHUNK), 0.02),
        "od_w_out": nrm((N_ODD, SGU_W, d), SGU_W ** -0.5),
        "final_g": 1.0 + nrm((d,), 0.02),
    }

def first_block(x, c, ctx, c_ctx, ada_w, ada_b, norm_g, ev_w_in, ev_q_norm, ev_k_norm,
              ev_dw_w, ev_dw_b, ev_ln_g, ev_ln_b, ev_w_out, od_w_in, od_ln_g, od_ln_b,
              od_ws, od_bs, od_w_out, final_g):
    bsz, n, _ = x.shape
    cos, sin = axial_rope_tables(n)
    sc = jax.nn.silu(c)
    scc = jax.nn.silu(c_ctx)
    xc = ctx
    lc = ctx.shape[1]
    for layer in range(DEPTH):
        ctx_needed = any(j % 2 == 0 for j in range(layer + 1, DEPTH))
        is_even = layer % 2 == 0
        mod = sc @ ada_w[layer] + ada_b[layer]
        shift, scale, gate = jnp.split(mod[:, None, :], 3, axis=-1)
        h = modulate(rmsnorm(x, norm_g[layer]), shift, scale)
        if is_even or ctx_needed:
            n_mod = 3 * D_MODEL if ctx_needed else 2 * D_MODEL
            mod_c = (scc @ ada_w[layer][:, :n_mod] + ada_b[layer][:n_mod])[None, None, :]
            hc = modulate(rmsnorm(xc, norm_g[layer]),
                          mod_c[..., :D_MODEL], mod_c[..., D_MODEL:2 * D_MODEL])
        if is_even:
            e = layer // 2
            w_in = ev_w_in[e]
            k, v, q, za, glu, zb = jnp.split(h @ w_in, EV_SPLITS, axis=-1)
            q = apply_rope(rmsnorm(q.reshape(bsz, n, N_Q_HEADS, HEAD_DIM), ev_q_norm[e]), cos, sin)
            k = apply_rope(rmsnorm(k.reshape(bsz, n, N_KV_HEADS, HEAD_DIM), ev_k_norm[e]), cos, sin)
            v = v.reshape(bsz, n, N_KV_HEADS, HEAD_DIM)
            if ctx_needed:
                kc, vc, qc, zac, gluc, zbc = jnp.split(hc @ w_in, EV_SPLITS, axis=-1)
            else:
                kc, vc = jnp.split(hc @ w_in[:, :2 * KV_W], 2, axis=-1)
            kc = rmsnorm(kc.reshape(bsz, lc, N_KV_HEADS, HEAD_DIM), ev_k_norm[e])
            vc = vc.reshape(bsz, lc, N_KV_HEADS, HEAD_DIM)
            attn = latent_attention(q, k, v, kc, vc)
            conv = conformer_conv(glu, ev_dw_w[e], ev_dw_b[e], ev_ln_g[e], ev_ln_b[e])
            mix = jnp.concatenate([attn * jax.nn.silu(za), conv * jax.nn.silu(zb)], axis=-1)
            x_new = x + gate * (mix @ ev_w_out[e])
            if ctx_needed:
                qc = rmsnorm(qc.reshape(bsz, lc, N_Q_HEADS, HEAD_DIM), ev_q_norm[e])
                attn_c = context_attention(qc, kc, vc)
                conv_c = conformer_conv(gluc, ev_dw_w[e], ev_dw_b[e], ev_ln_g[e], ev_ln_b[e])
                mix_c = jnp.concatenate([attn_c * jax.nn.silu(zac), conv_c * jax.nn.silu(zbc)], axis=-1)
                xc = xc + mod_c[..., 2 * D_MODEL:] * (mix_c @ ev_w_out[e])
            x = x_new
        else:
            o = layer // 2
            p = h @ od_w_in[o]
            mixed = spatial_gating(p[..., :2 * SGU_W], od_ln_g[o], od_ln_b[o], od_ws[o], od_bs[o])
            mixed = mixed * jax.nn.silu(p[..., 2 * SGU_W:])
            x_new = x + gate * (mixed @ od_w_out[o])
            if ctx_needed:
                pc = hc @ od_w_in[o]
                mixed_c = spatial_gating(pc[..., :2 * SGU_W], od_ln_g[o], od_ln_b[o], od_ws[o], od_bs[o])
                mixed_c = mixed_c * jax.nn.silu(pc[..., 2 * SGU_W:])
                xc = xc + mod_c[..., 2 * D_MODEL:] * (mixed_c @ od_w_out[o])
            x = x_new
    return rmsnorm(x, final_g)


_first_inputs = first_inputs


def first_inputs(seed=0):
    import zlib

    import numpy as np

    out = dict(_first_inputs(seed))
    spreads = {}
    factors = {'ctx': 7.352,
     'c_ctx': 2.859,
     'ada_b': 3.279,
     'norm_g': 8.0,
     'ev_q_norm': 8.0,
     'ev_k_norm': 8.0,
     'ev_dw_b': 8.0,
     'ev_ln_g': 26.966,
     'ev_ln_b': 25.689,
     'od_ln_g': 34.172,
     'od_ln_b': 32.6,
     'od_bs': 33.573,
     'final_g': 7.606}
    for name, (base, spread) in spreads.items():
        noise = np.random.default_rng([zlib.crc32(name.encode()), seed]).standard_normal(out[name].shape)
        drawn = base * np.exp(spread * noise) if base else spread * noise
        out[name] = __import__('jax').numpy.asarray(drawn.astype(out[name].dtype))
    for name, factor in factors.items():
        out[name] = (out[name] * factor).astype(out[name].dtype)
    return out


_narrow_inputs = first_inputs


def first_inputs(seed=0):

    out = dict(_narrow_inputs(seed))
    wider = {'od_ln_g': 4.7, 'od_ln_b': 4.69, 'od_bs': 4.7, 'final_g': 3.11}
    for name, times in wider.items():
        mean = out[name].mean()
        out[name] = (mean + times * (out[name] - mean)).astype(out[name].dtype)
    return out


DEPTH_2 = 1

ATTN_HEADS = 8
ATTN_HEAD_DIM = 128
ATTN_WIDTH = ATTN_HEADS * ATTN_HEAD_DIM
SSM_WIDTH = D_MODEL // 4
SSM_GROUP = 16
SSM_GROUPS = SSM_WIDTH // SSM_GROUP
SSM_STATE = 64
DT_MIN = 1e-3
DT_MAX = 1e-1
N_BRANCHES = 2
PEER_HEADS = 8
PEER_N_KEYS = 128
PEER_N_EXPERTS = PEER_N_KEYS * PEER_N_KEYS
PEER_QUERY_DIM = 256
PEER_HALF_DIM = PEER_QUERY_DIM // 2
PEER_TOPK = 16
PEER_CHUNK = 128
N_MOD = 6
RMS_EPS = 1e-6
NEG_INF = -1e30

IN_SIZES = (ATTN_WIDTH, ATTN_WIDTH, ATTN_WIDTH, ATTN_HEADS, SSM_WIDTH, D_MODEL, D_MODEL)
IN_WIDTH = sum(IN_SIZES)
IN_SPLIT_POINTS = tuple(int(v) for v in np.cumsum(IN_SIZES)[:-1])


def rms_norm(x, w):
    xf = x.astype(jnp.float32)
    xf = xf * lax.rsqrt(jnp.mean(xf * xf, axis=-1, keepdims=True) + RMS_EPS)
    return xf.astype(x.dtype) * w

def modulate_2(h, shift, scale):
    return h * (1.0 + scale[:, None, :]) + shift[:, None, :]

def _ssm_combine(e_i, e_j):
    ar_i, ai_i, br_i, bi_i = e_i
    ar_j, ai_j, br_j, bi_j = e_j
    ar = ar_j * ar_i - ai_j * ai_i
    ai = ar_j * ai_i + ai_j * ar_i
    br = ar_j * br_i - ai_j * bi_i + br_j
    bi = ar_j * bi_i + ai_j * br_i + bi_j
    return (ar, ai, br, bi)

def s5_mixer(u, A_re, A_im, log_dt, B_re, B_im, C_re, C_im, D_skip):
    bsz, seq, _ = u.shape
    f32 = jnp.float32
    uf = u.astype(f32).reshape(bsz, seq, SSM_GROUPS, SSM_GROUP)
    lam_re = A_re.astype(f32)
    lam_im = A_im.astype(f32)
    dt = jnp.exp(log_dt.astype(f32))[:, None]
    mag = jnp.exp(lam_re * dt)
    ab_re = mag * jnp.cos(lam_im * dt)
    ab_im = mag * jnp.sin(lam_im * dt)
    den = lam_re * lam_re + lam_im * lam_im
    nr = ab_re - 1.0
    coef_re = (nr * lam_re + ab_im * lam_im) / den
    coef_im = (ab_im * lam_re - nr * lam_im) / den
    b_re = B_re.astype(f32)
    b_im = B_im.astype(f32)
    bb_re = coef_re[..., None] * b_re - coef_im[..., None] * b_im
    bb_im = coef_re[..., None] * b_im + coef_im[..., None] * b_re
    bu_re = jnp.einsum('bsgc,gpc->bsgp', uf, bb_re)
    bu_im = jnp.einsum('bsgc,gpc->bsgp', uf, bb_im)
    a_re = jnp.broadcast_to(ab_re, (1, seq, SSM_GROUPS, SSM_STATE))
    a_im = jnp.broadcast_to(ab_im, (1, seq, SSM_GROUPS, SSM_STATE))
    _, _, st_re, st_im = lax.associative_scan(_ssm_combine, (a_re, a_im, bu_re, bu_im), axis=1)
    y = (jnp.einsum('gcp,bsgp->bsgc', C_re.astype(f32), st_re)
         - jnp.einsum('gcp,bsgp->bsgc', C_im.astype(f32), st_im)
         + D_skip.astype(f32) * uf)
    return y.reshape(bsz, seq, SSM_WIDTH).astype(u.dtype)

def half_glu(y, w_glu, b_glu):
    g = jax.nn.gelu(y, approximate=False)
    return g * jax.nn.sigmoid(g @ w_glu + b_glu)

def head_rms(t, w):
    tf = t.astype(jnp.float32)
    tf = tf * lax.rsqrt(jnp.mean(tf * tf, axis=-1, keepdims=True) + RMS_EPS)
    return tf.astype(t.dtype) * w

def fox_attention(q, k, v, f_logit, b_forget, q_norm_w, k_norm_w):
    bsz, seq, _ = q.shape
    q = head_rms(q.reshape(bsz, seq, ATTN_HEADS, ATTN_HEAD_DIM), q_norm_w) * (ATTN_HEAD_DIM ** -0.5)
    k = head_rms(k.reshape(bsz, seq, ATTN_HEADS, ATTN_HEAD_DIM), k_norm_w)
    v = v.reshape(bsz, seq, ATTN_HEADS, ATTN_HEAD_DIM)
    log_f = jax.nn.log_sigmoid((f_logit + b_forget).astype(jnp.float32))
    cum = jnp.cumsum(log_f, axis=1).transpose(0, 2, 1)
    nb = seq // Q_BLOCK
    q_blocks = q.reshape(bsz, nb, Q_BLOCK, ATTN_HEADS, ATTN_HEAD_DIM).transpose(1, 0, 2, 3, 4)
    cum_blocks = cum.reshape(bsz, ATTN_HEADS, nb, Q_BLOCK).transpose(2, 0, 1, 3)
    kpos = jnp.arange(seq)

    def block(args):
        qb, cq, bi = args
        s = (jnp.einsum('bqhd,bkhd->bhqk', qb, k).astype(jnp.float32)
             + cq[..., None] - cum[:, :, None, :])
        qpos = bi * Q_BLOCK + jnp.arange(Q_BLOCK)
        s = jnp.where(kpos[None, :] <= qpos[:, None], s, NEG_INF)
        p = jax.nn.softmax(s, axis=-1).astype(v.dtype)
        return jnp.einsum('bhqk,bkhd->bqhd', p, v)

    o = lax.map(block, (q_blocks, cum_blocks, jnp.arange(nb)))
    return o.transpose(1, 0, 2, 3, 4).reshape(bsz, seq, ATTN_WIDTH)

def peer_ffn(h, w_q, sub_keys, expert_u, expert_v):
    bsz, seq, d = h.shape
    q = (h @ w_q).reshape(bsz, seq, PEER_HEADS, 2, PEER_HALF_DIM)
    scores = jnp.einsum('bshpd,hpnd->bshpn', q, sub_keys).astype(jnp.float32)
    sv, si = lax.top_k(scores, PEER_TOPK)
    cand = (sv[..., 0, :, None] + sv[..., 1, None, :]).reshape(bsz, seq, PEER_HEADS, PEER_TOPK * PEER_TOPK)
    cidx = (si[..., 0, :, None] * PEER_N_KEYS + si[..., 1, None, :]).reshape(bsz, seq, PEER_HEADS, PEER_TOPK * PEER_TOPK)
    tv, tp = lax.top_k(cand, PEER_TOPK)
    eidx = jnp.take_along_axis(cidx, tp, axis=-1)
    gw = jax.nn.softmax(tv, axis=-1).astype(h.dtype)
    n_sel = PEER_HEADS * PEER_TOPK
    nc = (bsz * seq) // PEER_CHUNK
    xs = h.reshape(nc, PEER_CHUNK, d)
    ids = eidx.reshape(nc, PEER_CHUNK, n_sel)
    ws = gw.reshape(nc, PEER_CHUNK, n_sel)

    def chunk(args):
        xc, ic, wc = args
        a = jnp.einsum('td,ted->te', xc, expert_u[ic])
        a = jax.nn.gelu(a, approximate=False) * wc
        return jnp.einsum('te,ted->td', a, expert_v[ic])

    out = lax.map(chunk, (xs, ids, ws))
    return out.reshape(bsz, seq, d)

def second_inputs(seed: int = 0) -> dict:
    key = jax.random.key(seed)
    ks = jax.random.split(key, 32)
    f32 = jnp.float32
    L = DEPTH_2
    nrm = lambda k, shape, s: (jax.random.normal(k, shape, f32) * s)
    n_idx = jnp.arange(SSM_STATE, dtype=f32)
    A_re = -0.5 * jnp.exp(nrm(ks[9], (L, SSM_GROUPS, SSM_STATE), 0.05))
    A_im = math.pi * n_idx[None, None, :] + nrm(ks[10], (L, SSM_GROUPS, SSM_STATE), 0.01)
    log_dt = jax.random.uniform(ks[11], (L, SSM_GROUPS), f32, math.log(DT_MIN), math.log(DT_MAX))
    return {
        "x": nrm(ks[0], (BATCH, SEQ, D_MODEL), 1.0),
        "c": nrm(ks[1], (BATCH, D_MODEL), 1.0),
        "w_ada": nrm(ks[2], (L, D_MODEL, N_MOD * D_MODEL), 0.02),
        "b_ada": nrm(ks[3], (L, N_MOD * D_MODEL), 0.01),
        "norm1_w": 1.0 + nrm(ks[4], (L, D_MODEL), 0.02),
        "w_in": nrm(ks[5], (L, D_MODEL, IN_WIDTH), D_MODEL ** -0.5),
        "b_forget": jax.random.uniform(ks[6], (L, ATTN_HEADS), f32, 1.0, 3.0),
        "q_norm_w": 1.0 + nrm(ks[7], (L, ATTN_HEAD_DIM), 0.02),
        "k_norm_w": 1.0 + nrm(ks[8], (L, ATTN_HEAD_DIM), 0.02),
        "ssm_A_re": A_re,
        "ssm_A_im": A_im,
        "ssm_log_dt": log_dt,
        "ssm_B_re": nrm(ks[12], (L, SSM_GROUPS, SSM_STATE, SSM_GROUP), (2.0 * SSM_GROUP) ** -0.5),
        "ssm_B_im": nrm(ks[13], (L, SSM_GROUPS, SSM_STATE, SSM_GROUP), (2.0 * SSM_GROUP) ** -0.5),
        "ssm_C_re": nrm(ks[14], (L, SSM_GROUPS, SSM_GROUP, SSM_STATE), (2.0 * SSM_STATE) ** -0.5),
        "ssm_C_im": nrm(ks[15], (L, SSM_GROUPS, SSM_GROUP, SSM_STATE), (2.0 * SSM_STATE) ** -0.5),
        "ssm_D": 1.0 + nrm(ks[16], (L, SSM_GROUPS, SSM_GROUP), 0.1),
        "w_glu": nrm(ks[17], (L, SSM_WIDTH, SSM_WIDTH), SSM_WIDTH ** -0.5),
        "b_glu": nrm(ks[18], (L, SSM_WIDTH), 0.01),
        "w_ssm_up": nrm(ks[19], (L, SSM_WIDTH, D_MODEL), SSM_WIDTH ** -0.5),
        "w_attn_up": nrm(ks[20], (L, ATTN_WIDTH, D_MODEL), ATTN_WIDTH ** -0.5),
        "w_out": nrm(ks[21], (L, D_MODEL, D_MODEL), D_MODEL ** -0.5),
        "norm2_w": 1.0 + nrm(ks[22], (L, D_MODEL), 0.02),
        "w_peer_q": nrm(ks[23], (L, D_MODEL, PEER_HEADS * PEER_QUERY_DIM), D_MODEL ** -0.5),
        "peer_sub_keys": nrm(ks[24], (L, PEER_HEADS, 2, PEER_N_KEYS, PEER_HALF_DIM), PEER_HALF_DIM ** -0.5),
        "peer_u": nrm(ks[25], (L, PEER_N_EXPERTS, D_MODEL), D_MODEL ** -0.5),
        "peer_v": nrm(ks[26], (L, PEER_N_EXPERTS, D_MODEL), 0.25),
    }

def second_block(x, c, w_ada, b_ada, norm1_w, w_in, b_forget, q_norm_w, k_norm_w,
              ssm_A_re, ssm_A_im, ssm_log_dt, ssm_B_re, ssm_B_im, ssm_C_re, ssm_C_im, ssm_D,
              w_glu, b_glu, w_ssm_up, w_attn_up, w_out, norm2_w, w_peer_q, peer_sub_keys,
              peer_u, peer_v):
    cond = jax.nn.silu(c)
    for l in range(DEPTH_2):
        mod = cond @ w_ada[l] + b_ada[l]
        sh1, sc1, g1, sh2, sc2, g2 = jnp.split(mod, N_MOD, axis=-1)
        h = modulate_2(rms_norm(x, norm1_w[l]), sh1, sc1)
        proj = h @ w_in[l]
        q, k, v, f_logit, u, gate_s, gate_a = jnp.split(proj, IN_SPLIT_POINTS, axis=-1)
        y_ssm = s5_mixer(u, ssm_A_re[l], ssm_A_im[l], ssm_log_dt[l], ssm_B_re[l], ssm_B_im[l],
                         ssm_C_re[l], ssm_C_im[l], ssm_D[l])
        y_ssm = half_glu(y_ssm, w_glu[l], b_glu[l])
        y_attn = fox_attention(q, k, v, f_logit, b_forget[l], q_norm_w[l], k_norm_w[l])
        merged = (jax.nn.sigmoid(gate_s) * (y_ssm @ w_ssm_up[l])
                  + jax.nn.sigmoid(gate_a) * (y_attn @ w_attn_up[l]))
        x = x + g1[:, None, :] * (merged @ w_out[l])
        h2 = modulate_2(rms_norm(x, norm2_w[l]), sh2, sc2)
        x = x + g2[:, None, :] * peer_ffn(h2, w_peer_q[l], peer_sub_keys[l], peer_u[l], peer_v[l])
    return x


def setup_inputs(seed=0):
    out = dict(first_inputs(seed))
    for name, value in second_inputs(seed + 1).items():
        if name != "x":
            out[name + "_2"] = value
    return out


def reference(
    x, c, ctx, c_ctx, ada_w, ada_b, norm_g, ev_w_in, ev_q_norm, ev_k_norm, ev_dw_w, ev_dw_b,
    ev_ln_g, ev_ln_b, ev_w_out, od_w_in, od_ln_g, od_ln_b, od_ws, od_bs, od_w_out, final_g, c_2,
    w_ada_2, b_ada_2, norm1_w_2, w_in_2, b_forget_2, q_norm_w_2, k_norm_w_2, ssm_A_re_2,
    ssm_A_im_2, ssm_log_dt_2, ssm_B_re_2, ssm_B_im_2, ssm_C_re_2, ssm_C_im_2, ssm_D_2, w_glu_2,
    b_glu_2, w_ssm_up_2, w_attn_up_2, w_out_2, norm2_w_2, w_peer_q_2, peer_sub_keys_2, peer_u_2,
    peer_v_2,
):
    x = first_block(
        x, c, ctx, c_ctx, ada_w, ada_b, norm_g, ev_w_in, ev_q_norm, ev_k_norm, ev_dw_w, ev_dw_b,
        ev_ln_g, ev_ln_b, ev_w_out, od_w_in, od_ln_g, od_ln_b, od_ws, od_bs, od_w_out, final_g,
    )
    return second_block(
        x, c_2, w_ada_2, b_ada_2, norm1_w_2, w_in_2, b_forget_2, q_norm_w_2, k_norm_w_2,
        ssm_A_re_2, ssm_A_im_2, ssm_log_dt_2, ssm_B_re_2, ssm_B_im_2, ssm_C_re_2, ssm_C_im_2,
        ssm_D_2, w_glu_2, b_glu_2, w_ssm_up_2, w_attn_up_2, w_out_2, norm2_w_2, w_peer_q_2,
        peer_sub_keys_2, peer_u_2, peer_v_2,
    )


_drawn_inputs = setup_inputs


def setup_inputs(seed=0):
    import zlib

    import numpy as np

    out = dict(_drawn_inputs(seed))
    spreads = {}
    factors = {'b_ada_2': 8.0,
     'norm1_w_2': 8.0,
     'b_forget_2': 8.0,
     'q_norm_w_2': 8.0,
     'k_norm_w_2': 8.0,
     'ssm_A_re_2': 64.0,
     'ssm_A_im_2': 64.0,
     'ssm_log_dt_2': 64.0,
     'ssm_B_re_2': 64.0,
     'ssm_B_im_2': 64.0,
     'ssm_C_re_2': 64.0,
     'ssm_C_im_2': 64.0,
     'ssm_D_2': 8.0,
     'w_glu_2': 8.0,
     'b_glu_2': 8.0,
     'w_ssm_up_2': 3.148,
     'norm2_w_2': 8.0,
     'w_peer_q_2': 4.836,
     'peer_sub_keys_2': 4.858,
     'peer_u_2': 5.439,
     'peer_v_2': 4.847}
    for name, (base, spread) in spreads.items():
        noise = np.random.default_rng([zlib.crc32(name.encode()), seed]).standard_normal(out[name].shape)
        drawn = base * np.exp(spread * noise) if base else spread * noise
        out[name] = __import__('jax').numpy.asarray(drawn.astype(out[name].dtype))
    for name, factor in factors.items():
        out[name] = (out[name] * factor).astype(out[name].dtype)
    return out
```

```python
from contextlib import ExitStack

import concourse.bass as bass
from concourse import mybir
from concourse.alu_op_type import AluOpType as ALU
import numpy as np

F32 = mybir.dt.float32
U32 = mybir.dt.uint32
ACT = mybir.ActivationFunctionType
AX = mybir.AxisListType.X

P = 128
TOK = 256
D = 2048
DT = D // P
EPS = 1e-6
CHUNK = 2048
SLOTS = 4
HEADS = 8
HD = 128
KV = 2
CONV_T = 8
CONV_W = 31
PADW = TOK + CONV_W - 1
SEL = 16
NSLOT = HEADS * SEL
NEG = -1e30
LOWEST = -3.0e38
_hi = float(np.float32(np.floor(2 * np.pi * 2.0 ** 8) / 2.0 ** 8))
_mid = float(np.floor((2 * np.pi - _hi) * 2.0 ** 20) / 2.0 ** 20)
TURN = (_hi, _mid, 2 * np.pi - _hi - _mid)
HALF_TURN = 3.1415925
ROUND = 1.5 * 2.0 ** 23

STREAM = [("kv", 4, 2), ("ev", 40, 1), ("ev_out", 16, 1), ("od", 48, 1), ("od_out", 16, 1), ("w_in", 28, 1),
          ("glu", 1, 4), ("ssm_up", 4, 4), ("attn_up", 8, 2), ("gates", 32, 1), ("w_out", 16, 1), ("peer_q", 16, 1)]
CHUNK0, UNIT0 = {}, {}
_c = _u = 0
for _n, _k, _g in STREAM:
    CHUNK0[_n], UNIT0[_n] = _c, _u
    _c += _k
    _u += _k * _g
NCHUNK = _c
NUNIT = _u
UNITS_THROUGH = []
for _n, _k, _g in STREAM:
    for _i in range(_k):
        UNITS_THROUGH.append(UNIT0[_n] + (_i + 1) * _g)

PRE_GROUPS = 2
ADA = ["gate0", "shift1", "scale1", "gate1", "shift2", "scale2", "gate2", "shift3", "scale3", "gate3"]
COND = {"gate0": 0, "shift1": 0, "scale1": 0, "gate1": 0}
NADA = 16 * (PRE_GROUPS + len(ADA))
MOD = {"shift0": 0, "scale0": 1, "shift0c": 2, "scale0c": 3}
MOD.update({n: 4 + i for i, n in enumerate(ADA)})

CONST = {}
_at = 0
for _n, _w in (("ident", 128), ("ones", 128), ("rot", 128), ("cos", TOK), ("sin", TOK), ("mask", 2 * TOK),
               ("gmask", 32), ("iota", 16)):
    CONST[_n] = (_at, _w)
    _at += _w
NCONST = _at
VEC = {}
_at = 0
for _n, _w in (("cond", 48), ("ada_b", 192), ("norm_g0", 16), ("norm_g1", 16), ("final_g", 16), ("norm1_w", 16),
               ("norm2_w", 16), ("q_norm", 1), ("k_norm", 1), ("q_norm_2", 1), ("k_norm_2", 1),
               ("dw_w", CONV_T * CONV_W), ("dw_b", 8), ("ln_g", 8), ("ln_b", 8), ("od_g", 16), ("od_b", 16),
               ("A_re", 16), ("A_im", 16), ("log_dt", 16), ("ssm_D", 4), ("b_glu", 4), ("b_forget", 1),
               ("B_re", 256), ("B_im", 256), ("C_re", 256), ("C_im", 256), ("w_f", 128)):
    VEC[_n] = (_at, _w)
    _at += _w
NVEC = _at


def constants():
    t = np.zeros((P, NCONST), np.float32)

    def put(name, a):
        a0, w = CONST[name]
        t[:, a0:a0 + w] = a

    put("ident", np.eye(P))
    put("ones", 1.0)
    rot = np.zeros((P, P))
    for i in range(HD // 2):
        rot[2 * i + 1, 2 * i] = -1.0
        rot[2 * i, 2 * i + 1] = 1.0
    put("rot", rot)
    f = np.float32
    pos = np.arange(TOK)
    inv = np.power(f(10000.0), np.arange(32, dtype=f) * f(-2.0 / 64)).astype(f)
    ang = np.concatenate([(pos // 64).astype(f)[:, None] * inv, (pos % 64).astype(f)[:, None] * inv], 1)
    ang = np.repeat(ang, 2, axis=1).T
    put("cos", np.cos(ang))
    put("sin", np.sin(ang))
    qpos = np.arange(2)[None, :, None] * P + np.arange(P)[:, None, None]
    put("mask", np.where(np.arange(TOK)[None, None, :] <= qpos, 0.0, NEG).reshape(P, -1))
    g = np.zeros((P, 4, 8))
    for p in range(P):
        for j in range(4):
            g[p, j, 2 * j + p // 64] = 1.0
    put("gmask", g.reshape(P, 32))
    put("iota", np.arange(16.0)[None, :])
    return t


def build(nc, xT, ctxT, consts, vecs, weights, ada, keysT, wsT, bs, g3_bias, peer_u, peer_v, out):
    with ExitStack() as ctx:
        def sb(name, shape, dt=F32):
            return ctx.enter_context(nc.sbuf_tensor(name, shape, dt))

        def sem(name):
            return ctx.enter_context(nc.semaphore(name))

        x = sb("x", [P, DT, TOK])
        h = sb("h", [P, DT, TOK])
        ring = sb("ring", [P, SLOTS, CHUNK])
        aring = sb("aring", [P, SLOTS, CHUNK])
        proj = sb("proj", [P, 48, TOK])
        acc = sb("acc", [P, 2, CHUNK])
        sq = sb("sq", [P, DT * TOK])
        att = sb("att", [P, CONV_T * PADW])
        cst = sb("cst", [P, NCONST])
        vec = sb("vec", [P, NVEC])
        mods = sb("mods", [P, 14 * 16])
        gs = sb("gs", [P, 16])
        cond = sb("cond", [P, 48])
        rstd = sb("rstd", [P, TOK])
        small = sb("small", [P, 192])
        powers = sb("powers", [P, 8, 2, 16])
        idx = sb("idx", [P, SLOTS], U32)
        dots = sb("dots", [P, 3 * SLOTS])

        M = ctx.enter_context(nc.psum_tensor("M", [P, 2048], F32))
        G = [ctx.enter_context(nc.psum_tensor(f"G{i}", [P, 512], F32)) for i in range(2)]
        B6 = ctx.enter_context(nc.psum_tensor("B6", [P, 512], F32))
        B7 = ctx.enter_context(nc.psum_tensor("B7", [P, 512], F32))
        O = [B6, B7]

        def C(name):
            a, w = CONST[name]
            return cst[:, a:a + w]

        def V(name):
            a, w = VEC[name]
            return vec[:, a:a + w]

        def mod(name):
            return mods[:, 16 * MOD[name]:16 * MOD[name] + 16]

        def flat(ap):
            return ap.rearrange("p a b -> p (a b)")

        def tiles(ap, n):
            return ap.rearrange("p (n t) -> p n t", n=n)

        def over_tiles(ap, n):
            return ap.unsqueeze(1).to_broadcast([P, n, ap.shape[-1]])

        ident, ones = C("ident"), C("ones")
        hc = proj[:, 32:48, :]
        craw = proj[:, 16:32, :]
        kv_keys = sq[:, 0:1024].rearrange("p (g k) -> p g k", g=2)
        kv_vals = sq[:, 1024:2048].rearrange("p (g k) -> p g k", g=2)
        head_sq_at = sq[:, 2048:4096]
        eps = small[:, 8:9]
        cum, ncum = att[0:8, 1024:1280], att[0:8, 1280:1536]
        f_min, f_exp_row = att[0:8, 1536:1792], att[0:8, 1792:2048]
        turn_cos, turn_sin = proj[:, 28:32, :], proj[:, 32:36, :]
        w_re, w_im, tmp4 = proj[:, 36:40, :], proj[:, 40:44, :], proj[:, 44:48, :]
        z_re, z_im = sq[:, 2048:3072], sq[:, 3072:4096]

        consts_in, vecs_in, x_in, ctx_in = sem("consts_in"), sem("vecs_in"), sem("x_in"), sem("ctx_in")
        spatial_in, bs_in, keys_in, g3b_in = sem("spatial_in"), sem("bs_in"), sem("keys_in"), sem("g3b_in")
        w_in = [sem(f"w_in{s}") for s in range(SLOTS)]
        ada_in = [sem(f"ada_in{s}") for s in range(SLOTS)]
        unit_done, unit_evac = sem("unit_done"), sem("unit_evac")
        ada_pe_used, ada_dve_used = sem("ada_pe_used"), sem("ada_dve_used")
        cond_ready, pre_rows, pre_cols = sem("cond_ready"), sem("pre_rows"), sem("pre_cols")
        mod_sums, mod_copied, mods_ready = sem("mod_sums"), sem("mod_copied"), sem("mods_ready")
        dve_step, act_step, pool_step = sem("dve_step"), sem("act_step"), sem("pool_step")
        sum_in, sum_done, std_ready = sem("sum_in"), sem("sum_done"), sem("std_ready")
        h_ready, out_merged = sem("h_ready"), sem("out_merged")
        head_sq, head_sums, head_std = sem("head_sq"), sem("head_sums"), sem("head_std")
        rot_in, rot_done, qk_ready = sem("rot_in"), sem("rot_done"), sem("qk_ready")
        v_turned, v_ready = sem("v_turned"), sem("v_ready")
        s_done, nmax_ready, exp_done, p_ready = sem("s_done"), sem("nmax_ready"), sem("exp_done"), sem("p_ready")
        pt_done, pt_copied, pv_done, o_read = sem("pt_done"), sem("pt_copied"), sem("pv_done"), sem("o_read")
        conv_normed, conv_act, mix_ready = sem("conv_normed"), sem("conv_act"), sem("mix_ready")
        gate_v_ready, vt_done, vt_copied = sem("gate_v_ready"), sem("vt_done"), sem("vt_copied")
        sgu_done, sgu_read, sgu_ready = sem("sgu_done"), sem("sgu_read"), sem("sgu_ready")
        f_done, f_exp_in, f_exp, f_ln_in, f_ln, cum_ready = (sem("f_done"), sem("f_exp_in"), sem("f_exp"),
                                                             sem("f_ln_in"), sem("f_ln"), sem("cum_ready"))
        trig_in, trig_out = sem("trig_in"), sem("trig_out")
        ssm_bc, ssm_bt, ssm_btc = sem("ssm_bc"), sem("ssm_bt"), sem("ssm_btc")
        ssm_bu, ssm_s, ssm_y, ssm_yd, ssm_g = (sem("ssm_bu"), sem("ssm_s"), sem("ssm_y"), sem("ssm_yd"), sem("ssm_g"))
        glu_ready, merged = sem("glu_ready"), sem("merged")
        g3_done, g3_ready = sem("g3_done"), sem("g3_ready")
        sc_done, sc_copied = sem("sc_done"), sem("sc_copied")
        ht_done, ht_copied = sem("ht_done"), sem("ht_copied")
        gexp_in, gexp_out, picks_ready = sem("gexp_in"), sem("gexp_out"), sem("picks_ready")
        u_in = [sem(f"u_in{s}") for s in range(SLOTS)]
        v_in = [sem(f"v_in{s}") for s in range(SLOTS)]
        gathers_begun = sem("gathers_begun")
        idx_set, dot_done, gelu_done, coef_ready, v_added = (sem("idx_set"), sem("dot_done"), sem("gelu_done"),
                                                             sem("coef_ready"), sem("v_added"))
        tile_step, conv_step = sem("tile_step"), sem("conv_step")
        out_ready, stored = sem("out_ready"), sem("stored")

        block = ctx.enter_context(nc.Block())

        @block.sync
        def _(sp):
            sp.dma_start(vec[:, :], vecs).then_inc(vecs_in, 16)
            sp.dma_start(flat(x[:, :, :]), xT).then_inc(x_in, 16)
            sp.dma_start(flat(craw), ctxT).then_inc(ctx_in, 16)
            sp.dma_start(cst[:, :], consts).then_inc(consts_in, 16)

            def load(c, slot, units_before):
                if units_before is not None:
                    sp.wait_ge(unit_done, units_before)
                sp.dma_start(ring[:, slot, :], weights[c]).then_inc(w_in[slot], 16)

            def straight(a, b):
                for c in range(a, b):
                    load(c, c % SLOTS, UNITS_THROUGH[c - SLOTS] if c >= SLOTS else None)

            def looped(a, b):
                with sp.Fori(0, (b - a) // SLOTS) as i:
                    for j in range(SLOTS):
                        load(a + j + SLOTS * i, (a + j) % SLOTS, UNITS_THROUGH[a + j - SLOTS] + SLOTS * i)

            glu, gates = CHUNK0["glu"], CHUNK0["gates"]
            straight(0, 8)
            looped(8, glu)
            straight(glu, gates + SLOTS)
            looped(gates + SLOTS, NCHUNK - SLOTS)
            straight(NCHUNK - SLOTS, NCHUNK)
            for tt in range(2):
                sp.wait_ge(out_ready, tt + 1)
                sp.dma_start(out[tt * P:(tt + 1) * P, :], flat(h[:, :, :])[:, tt * D:(tt + 1) * D]).then_inc(stored, 16)
            sp.wait_ge(stored, 32)

        @block.gpsimd
        def _(pool):
            def load(a, slot):
                pool.dma_start(aring[:, slot, :], ada[a]).then_inc(ada_in[slot], 16)

            for a in range(SLOTS):
                load(a, a)
            with pool.Fori(1, 16 * PRE_GROUPS // SLOTS) as i:
                for s in range(SLOTS):
                    pool.wait_ge(ada_pe_used, SLOTS * i + s - SLOTS + 1)
                    load(SLOTS * i + s, s)
            for s in range(SLOTS):
                pool.wait_ge(ada_pe_used, 16 * PRE_GROUPS - SLOTS + s + 1)
                load(16 * PRE_GROUPS + s, s)
            with pool.Fori(1, 16 * len(ADA) // SLOTS) as i:
                for s in range(SLOTS):
                    pool.wait_ge(ada_dve_used, SLOTS * i + s - SLOTS + 1)
                    load(16 * PRE_GROUPS + SLOTS * i + s, s)

            pool.wait_ge(pt_done, 16)
            pool.wait_ge(s_done, 16)
            pool.dma_start(att[:, 0:D], g3_bias.partition_broadcast(P)).then_inc(g3b_in, 16)

            pool.wait_ge(picks_ready, 2)
            pool.wait_ge(unit_done, NUNIT)
            pool.wait_ge(ada_dve_used, 16 * len(ADA))
            picks = flat(proj[:, 40:41, :]).bitcast(U32)

            def gather(n, s, before):
                if before is not None:
                    pool.wait_ge(dot_done, before)
                    pool.wait_ge(v_added, before)
                nc.gpsimd.tensor_copy(idx[:, s:s + 1], picks[:, bass.ds(n, 1)]).then_inc(idx_set, 1)
                pool.wait_ge(idx_set, n + 1)
                pool.sem_inc(gathers_begun, 1)
                where = bass.IndirectOffsetOnAxis(idx[:, s:s + 1], 0)
                pool.indirect_dma_start(ring[:, s, :], None, peer_u, where).then_inc(u_in[s], 16)
                pool.indirect_dma_start(aring[:, s, :], None, peer_v, where).then_inc(v_in[s], 16)

            for s in range(SLOTS):
                gather(s, s, None)
            with pool.Fori(1, 2 * NSLOT // SLOTS) as i:
                for s in range(SLOTS):
                    gather(SLOTS * i + s, s, SLOTS * i + s - SLOTS + 1)

        @block.tensor
        def _(pe):
            unit_bank = lambda u: G[u % 2]

            def unit(slot, weights_at, k, rhs, u, bank):
                for t in range(k):
                    mm = nc.tensor.matmul(bank[:, 0:TOK], lhsT=ring[:, slot, weights_at + t * P:weights_at + (t + 1) * P],
                                          rhs=rhs[:, t, :], start=(t == 0), stop=(t == k - 1))
                mm.then_inc(unit_done, 1)

            def dense(name, rhss, k=DT, first=0, count=None):
                per = len(rhss)
                n = dict((a, b) for a, b, _ in STREAM)[name]
                count = n if count is None else count
                c0, u0 = CHUNK0[name] + first, UNIT0[name] + first * per

                def chunk(j, i):
                    c = c0 + j
                    pe.wait_ge(w_in[c % SLOTS], 16 * (c // SLOTS + 1) + 16 * i)
                    for e in range(per):
                        u = u0 + j * per + e
                        if u >= 2:
                            pe.wait_ge(unit_evac, u - 1 + i * SLOTS * per)
                        unit(c % SLOTS, e * k * P if per * k == DT else 0, k, rhss[e], u, unit_bank(u))

                whole = count // SLOTS
                if whole >= 2 and u0 >= 2 and (SLOTS * per) % 2 == 0:
                    with pe.Fori(0, whole) as i:
                        for j in range(SLOTS):
                            chunk(j, i)
                    for j in range(whole * SLOTS, count):
                        chunk(j, 0)
                else:
                    for j in range(count):
                        chunk(j, 0)

            sums = [0]

            def feature_sum(src, n):
                sums[0] += 1
                pe.wait_ge(sum_in, sums[0])
                for t in range(n):
                    mm = nc.tensor.matmul(B7[:, 0:TOK], lhsT=ones, rhs=src[:, t * TOK:(t + 1) * TOK],
                                          start=(t == 0), stop=(t == n - 1))
                mm.then_inc(sum_done, 1)

            heads_n = [0]

            def head_sum(n):
                heads_n[0] += 1
                pe.wait_ge(head_sq, heads_n[0])
                for j in range(n // 2):
                    mm = nc.tensor.matmul(M[:, j * 512:(j + 1) * 512], lhsT=ones, rhs=head_sq_at[:, j * 512:(j + 1) * 512],
                                          start=True, stop=True)
                mm.then_inc(head_sums, 1)

            rots = [0]

            def rotate(srcs):
                rots[0] += 1
                pe.wait_ge(rot_in, rots[0])
                for j, s in enumerate(srcs):
                    w = s.shape[-1]
                    mm = nc.tensor.matmul(M[:, j * w:(j + 1) * w], lhsT=C("rot"), rhs=s, start=True, stop=True)
                mm.then_inc(rot_done, 1)

            def mod_sum(g, units):
                pe.wait_ge(ada_dve_used, 16 * (g + 1))
                pe.wait_ge(unit_evac, units)
                for m in range(DT):
                    mm = nc.tensor.matmul(G[0][:, m:m + 1], lhsT=acc[:, g % 2, m * P:(m + 1) * P],
                                          rhs=ones[:, 0:1], start=True, stop=True)
                mm.then_inc(mod_sums, 1)
                pe.wait_ge(mod_copied, g + 1)

            def attention(base, nk, q_of, k_of, v_of, pt, extra):
                w = nk * P

                def scores(hh):
                    if hh > 0:
                        pe.wait_ge(exp_done, 2 * (base + hh))
                    for qt in range(2):
                        o = M[:, qt * w:(qt + 1) * w]
                        mm = nc.tensor.matmul(o, lhsT=q_of(hh)[:, qt * P:(qt + 1) * P], rhs=k_of(hh),
                                              start=True, stop=not extra)
                        if extra:
                            nc.tensor.matmul(o, lhsT=cum[:, qt * P:(qt + 1) * P], rhs=pick_rows(hh),
                                             start=False, stop=False)
                            mm = nc.tensor.matmul(o, lhsT=pick_rows(hh)[:, 0:P], rhs=ncum, start=False, stop=True)
                    mm.then_inc(s_done, 1)

                scores(0)
                for hh in range(HEADS):
                    if hh + 1 < HEADS:
                        scores(hh + 1)
                    pe.wait_ge(p_ready, base + hh + 1)
                    if base + hh > 0:
                        pe.wait_ge(pt_copied, base + hh)
                    for kt in range(nk):
                        for qt in range(2):
                            mm = nc.tensor.transpose(M[:, 1024 + kt * 256 + qt * P:1024 + kt * 256 + (qt + 1) * P],
                                                     att[:, qt * w + kt * P:qt * w + (kt + 1) * P], ident)
                    mm.then_inc(pt_done, 1)
                    pe.wait_ge(pt_copied, base + hh + 1)
                    if base + hh >= 2:
                        pe.wait_ge(o_read, base + hh - 1)
                    for kt in range(nk):
                        mm = nc.tensor.matmul(O[hh % 2][:, 0:TOK], lhsT=v_of(hh, kt),
                                              rhs=pt[:, kt * 256:(kt + 1) * 256], start=(kt == 0), stop=(kt == nk - 1))
                    mm.then_inc(pv_done, 1)

            pe.wait_ge(cond_ready, 1)
            cond_v = cond[:, :].rearrange("p (v t) -> p v t", v=3)
            for g in range(PRE_GROUPS):
                if g > 0:
                    pe.wait_ge(pre_rows, g)
                for t in range(DT):
                    pe.wait_ge(ada_in[t % SLOTS], 16 * (4 * g + t // SLOTS + 1))
                    for nb in range(4):
                        mm = nc.tensor.matmul(M[0:2, nb * 512:(nb + 1) * 512], lhsT=cond_v[:, 0:2, t],
                                              rhs=aring[:, t % SLOTS, nb * 512:(nb + 1) * 512],
                                              start=(t == 0), stop=(t == DT - 1))
                    mm.then_inc(ada_pe_used, 1)
                if g == 0:
                    pe.wait_ge(consts_in, 16)
                pe.wait_ge(pre_rows, g + 1)
                for m in range(DT):
                    mm = nc.tensor.matmul(B6[:, g * 32 + 2 * m:g * 32 + 2 * m + 2], lhsT=acc[0:2, g, m * P:(m + 1) * P],
                                          rhs=ident[0:2, 0:2], start=True, stop=True)
                mm.then_inc(pre_cols, 1)

            feature_sum(sq, DT)
            feature_sum(sq, DT)
            pe.wait_ge(h_ready, 1)
            dense("kv", [h, hc])
            dense("ev", [h], first=0, count=8)
            head_sum(4)
            dense("ev", [h], first=8, count=8)
            rotate([kv_keys[:, g, 0:TOK] for g in range(2)])
            dense("ev", [h], first=16, count=8)
            head_sum(8)
            dense("ev", [h], first=24, count=8)
            rotate([flat(proj[:, 0:8, :])[:, j * 512:(j + 1) * 512] for j in range(4)])
            mod_sum(0, UNIT0["ev"] + 32)
            dense("ev", [h], first=32, count=8)
            mod_sum(1, UNIT0["ev_out"])
            pe.wait_ge(qk_ready, 1)
            for g in range(KV):
                for kt in range(4):
                    mm = nc.tensor.transpose(M[:, 1024 + kt * 256 + g * P:1024 + kt * 256 + (g + 1) * P],
                                             kv_vals[:, g, kt * P:(kt + 1) * P], ident)
            mm.then_inc(v_turned, 1)
            pe.wait_ge(v_ready, 1)
            vtok = sq[:, 3072:4096]
            attention(0, 4, lambda hh: proj[:, hh, :], lambda hh: kv_keys[:, hh // 4, :],
                      lambda hh, kt: vtok[:, kt * 256 + (hh // 4) * P:kt * 256 + (hh // 4 + 1) * P],
                      sq[:, 2048:3072], False)
            feature_sum(flat(proj[:, 8:16, :]), CONV_T)
            feature_sum(sq, CONV_T)
            pe.wait_ge(mix_ready, 1)
            dense("ev_out", [proj])
            mod_sum(2, UNIT0["od"])

            feature_sum(sq, DT)
            pe.wait_ge(h_ready, 2)
            dense("od", [h], first=0, count=16)
            pe.wait_ge(unit_evac, UNIT0["od"] + 16)
            for t in range(DT):
                mm = nc.tensor.matmul(B7[:, 0:TOK], lhsT=ones, rhs=proj[:, t, :], start=(t == 0), stop=(t == DT - 1))
            mm.then_inc(sum_done, 1)
            mod_sum(3, UNIT0["od"] + 16)
            dense("od", [h], first=16, count=16)
            feature_sum(sq, DT)
            mod_sum(4, UNIT0["od"] + 32)
            dense("od", [h], first=32, count=16)
            pe.wait_ge(gate_v_ready, 1)
            for b in range(4):
                half = (b % 2) * 1024
                if b >= 2:
                    pe.wait_ge(vt_copied, b - 1)
                for j in range(8):
                    n, c = (b % 2) * 8 + j, b // 2
                    mm = nc.tensor.transpose(M[:, half + j * P:half + (j + 1) * P], proj[:, n, c * P:(c + 1) * P], ident)
                mm.then_inc(vt_done, 1)
            pe.wait_ge(spatial_in, 16)
            for b in range(4):
                half = (b % 2) * 1024
                pe.wait_ge(vt_copied, 4 if b < 2 else 4)
                if b >= 2:
                    pe.wait_ge(sgu_read, b - 1)
                for j in range(4):
                    n = 4 * b + j
                    for c in range(2):
                        mm = nc.tensor.matmul(M[:, half + j * TOK + c * P:half + j * TOK + (c + 1) * P],
                                              lhsT=sq[:, c * D + n * P:c * D + (n + 1) * P],
                                              rhs=att[:, (n // 2) * P:(n // 2 + 1) * P], start=True, stop=True)
                mm.then_inc(sgu_done, 1)
            mod_sum(5, UNIT0["od_out"])
            pe.wait_ge(sgu_ready, 1)
            dense("od_out", [proj])
            mod_sum(6, UNIT0["w_in"])

            feature_sum(sq, DT)
            feature_sum(sq, DT)
            pe.wait_ge(h_ready, 3)
            dense("w_in", [h], first=0, count=4)
            for t in range(DT):
                mm = nc.tensor.matmul(B7[0:8, 0:TOK], lhsT=V("w_f")[:, t * 8:(t + 1) * 8], rhs=h[:, t, :],
                                      start=(t == 0), stop=(t == DT - 1))
            mm.then_inc(f_done, 1)

            def turn_b(q):
                pe.wait_ge(ssm_bc, q + 1)
                for part in range(2):
                    for j in range(4):
                        o = M[:, 1024 * part + j * P:1024 * part + (j + 1) * P]
                        mm = nc.tensor.transpose(o, att[:, part * 512 + j * P:part * 512 + (j + 1) * P], ident)
                mm.then_inc(ssm_bt, 1)

            def inputs_of_states(q):
                pe.wait_ge(ssm_btc, q + 1)
                for part in range(2):
                    for j in range(4):
                        mm = nc.tensor.matmul(M[:, 1024 * part + j * TOK:1024 * part + (j + 1) * TOK],
                                              lhsT=sq[:, part * 512 + j * P:part * 512 + (j + 1) * P],
                                              rhs=proj[:, q, :], start=True, stop=True)
                mm.then_inc(ssm_bu, 1)

            def outputs_of_states(q):
                pe.wait_ge(ssm_s, q + 1)
                for part in range(2):
                    for j in range(4):
                        mm = nc.tensor.matmul(B6[:, 0:TOK], lhsT=sq[:, 1024 + part * 512 + j * P:1024 + part * 512 + (j + 1) * P],
                                              rhs=ssm_w[part][:, j * TOK:(j + 1) * TOK],
                                              start=(part == 0 and j == 0), stop=(part == 1 and j == 3))
                mm.then_inc(ssm_y, 1)

            ssm_w = [flat(w_re), flat(w_im)]
            turn_b(0)
            dense("w_in", [h], first=4, count=4)
            inputs_of_states(0)
            dense("w_in", [h], first=8, count=4)
            for q in range(1, 4):
                outputs_of_states(q - 1)
                turn_b(q)
                inputs_of_states(q)
                dense("w_in", [h], first=8 + 4 * q, count=4)
            outputs_of_states(3)
            dense("w_in", [h], first=24, count=4)
            head_sum(8)
            head_sum(8)
            pe.wait_ge(ssm_g, 4)
            dense("glu", [proj, proj, proj, proj], k=4)
            pe.wait_ge(qk_ready, 2)
            for hh in range(HEADS):
                for kt in range(2):
                    mm = nc.tensor.transpose(M[:, kt * 1024 + hh * P:kt * 1024 + (hh + 1) * P],
                                             proj[:, 20 + hh, kt * P:(kt + 1) * P], ident)
            mm.then_inc(v_turned, 1)
            pe.wait_ge(v_ready, 2)
            pe.wait_ge(cum_ready, 1)
            vtok2 = flat(proj[:, 36:44, :])

            def pick_rows(hh):
                return ident[0:8, hh:hh + 1].to_broadcast([8, TOK])

            attention(8, 2, lambda hh: proj[:, 12 + hh, :], lambda hh: proj[:, 4 + hh, :],
                      lambda hh, kt: vtok2[:, kt * 1024 + hh * P:kt * 1024 + (hh + 1) * P], sq[:, 2048:2560], True)
            mod_sum(7, UNIT0["ssm_up"])
            pe.wait_ge(glu_ready, 1)
            dense("ssm_up", [proj, proj, proj, proj], k=4)
            pe.wait_ge(o_read, 16)
            dense("attn_up", [proj[:, 12:20, :], proj[:, 12:20, :]], k=8)
            mod_sum(8, UNIT0["gates"])
            dense("gates", [h])
            pe.wait_ge(merged, 1)
            dense("w_out", [proj[:, 32:48, :]])
            pe.wait_ge(ada_dve_used, 16 * len(ADA))
            for nb in range(4):
                mm = nc.tensor.matmul(M[:, nb * 512:(nb + 1) * 512], lhsT=ones, rhs=acc[:, 1, nb * 512:(nb + 1) * 512],
                                      start=True, stop=True)
            mm.then_inc(g3_done, 1)
            feature_sum(sq, DT)
            pe.wait_ge(h_ready, 4)

            def turn_to_tokens(src, first):
                for b in range(4):
                    half = (b % 2) * 1024
                    if first + b >= 2:
                        pe.wait_ge(ht_copied, first + b - 1)
                    for j in range(8):
                        n, c = (b % 2) * 8 + j, b // 2
                        mm = nc.tensor.transpose(M[:, half + j * P:half + (j + 1) * P], src[:, n, c * P:(c + 1) * P], ident)
                    mm.then_inc(ht_done, 1)

            pe.wait_ge(g3_ready, 1)
            turn_to_tokens(h, 0)
            turn_to_tokens(x, 4)
            dense("peer_q", [h])
            pe.wait_ge(unit_evac, NUNIT)
            pe.wait_ge(keys_in, 16)
            pe.wait_ge(ht_copied, 8)
            for tt in range(2):
                if tt > 0:
                    pe.wait_ge(sc_copied, tt)
                for r in range(16):
                    mm = nc.tensor.matmul(M[:, r * P:(r + 1) * P], lhsT=proj[:, r, tt * P:(tt + 1) * P],
                                          rhs=flat(proj[:, 40:48, :])[:, r * P:(r + 1) * P], start=True, stop=True)
                mm.then_inc(sc_done, 1)

        @block.scalar
        def _(act):
            def leave(u, dst, func, i=0, per=0, scale=1.0, bias=0.0):
                act.wait_ge(unit_done, u + 1 + i)
                nc.scalar.activation(dst, G[u % 2][:, 0:TOK], func, bias=bias, scale=scale).then_inc(unit_evac, 1)

            def leave_many(u0, tile0, n, func):
                if n >= 8:
                    with act.Fori(0, n // 4) as i:
                        for j in range(4):
                            leave(u0 + j, flat(proj[:, :, :])[:, bass.ds((tile0 + j) * TOK + i * (4 * TOK), TOK)], func, i=4 * i)
                else:
                    for j in range(n):
                        leave(u0 + j, proj[:, tile0 + j, :], func)

            def leave_gated(u0, gate):
                for n in range(DT):
                    leave(u0 + n, h[:, n, :], ACT.Identity, scale=gate[:, n:n + 1])

            def mod_out(g):
                act.wait_ge(mod_sums, g + 1)
                nc.scalar.activation(mods[:, 16 * (4 + g):16 * (5 + g)], G[0][:, 0:16], ACT.Copy).then_inc(mod_copied, 1)

            sums = [0]

            def std(n, count=1):
                sums[0] += count
                act.wait_ge(sum_done, sums[0])
                nc.scalar.activation(rstd[:, :], B7[:, 0:TOK], ACT.Sqrt, bias=eps, scale=1.0 / n).then_inc(std_ready, 1)

            hn = [0]

            def head_stds(n):
                hn[0] += 1
                act.wait_ge(head_sums, hn[0])
                nc.scalar.activation(head_sq_at[:, 0:n * TOK], M[:, 0:n * TOK], ACT.Sqrt, bias=eps, scale=1.0 / HD).then_inc(head_std, 1)

            def softmax_steps(base, nk, pt, scale):
                w = nk * P

                def exps(hh):
                    act.wait_ge(nmax_ready, base + hh + 1)
                    if base == 0 and hh > 0:
                        act.wait_ge(pt_done, base + hh)
                    for qt in range(2):
                        src = M[:, qt * w:(qt + 1) * w] if nk == 4 else att[:, qt * w:(qt + 1) * w]
                        nc.scalar.activation(att[:, qt * w:(qt + 1) * w], src, ACT.Exp, bias=small[:, 2 + qt:3 + qt],
                                                 scale=scale, accum_out=small[:, 4 + qt:5 + qt]).then_inc(exp_done, 1)

                exps(0)
                for hh in range(HEADS):
                    act.wait_ge(pt_done, base + hh + 1)
                    if hh > 0:
                        act.wait_ge(pv_done, base + hh)
                    nc.scalar.activation(pt, M[:, 1024:1024 + nk * 256], ACT.Copy).then_inc(pt_copied, 1)
                    if hh + 1 < HEADS:
                        exps(hh + 1)

            act.wait_ge(vecs_in, 16)
            act.wait_ge(dve_step, 1)
            nc.scalar.activation(cond[:, :], V("cond"), ACT.Silu).then_inc(cond_ready, 1)
            nc.scalar.activation(small[:, 16:32], V("log_dt"), ACT.Exp).then_inc(trig_out, 1)
            act.wait_ge(trig_in, 1)
            nc.scalar.activation(small[:, 32:48], small[:, 32:48], ACT.Exp).then_inc(trig_out, 1)
            act.wait_ge(trig_in, 2)
            nc.scalar.activation(small[:, 64:96], small[:, 64:96], ACT.Sin).then_inc(trig_out, 1)
            for g in range(PRE_GROUPS):
                act.wait_ge(ada_pe_used, 16 * (g + 1))
                nc.scalar.activation(acc[0:2, g, :], M[0:2, :], ACT.Copy).then_inc(pre_rows, 1)
            std(D)
            std(D)
            for t in range(4):
                dst = (kv_keys if t < 2 else kv_vals)[:, t % 2, :]
                if t == 0:
                    act.wait_ge(h_ready, 1)
                leave(2 * t, dst[:, 0:TOK], ACT.Copy)
                leave(2 * t + 1, dst[:, TOK:2 * TOK], ACT.Copy)
            u = UNIT0["ev"]
            leave_many(u, 0, 8, ACT.Copy)
            head_stds(4)
            leave_many(u + 8, 8, 8, ACT.Copy)
            leave_many(u + 16, 16, 8, ACT.Sigmoid)
            head_stds(8)
            leave_many(u + 24, 24, 8, ACT.Silu)
            mod_out(0)
            leave_many(u + 32, 32, 8, ACT.Silu)
            mod_out(1)
            act.wait_ge(v_turned, 1)
            nc.scalar.activation(sq[:, 3072:4096], M[:, 1024:2048], ACT.Copy).then_inc(v_ready, 1)
            softmax_steps(0, 4, sq[:, 2048:3072], HD ** -0.5)
            std(CONV_T * P, count=2)
            act.wait_ge(conv_normed, 1)
            for t in range(CONV_T):
                nc.scalar.activation(proj[:, 8 + t, :], proj[:, 8 + t, :], ACT.Silu, bias=V("ln_b")[:, t:t + 1],
                                     scale=V("ln_g")[:, t:t + 1]).then_inc(conv_act, 1)
            act.dma_start(att[:, 0:1024], wsT).then_inc(spatial_in, 16)
            act.dma_start(att[:, 1024:2048], bs.partition_broadcast(P)).then_inc(bs_in, 16)
            act.wait_ge(mods_ready, 1)
            leave_gated(UNIT0["ev_out"], mod("gate0"))
            mod_out(2)
            std(D)
            u = UNIT0["od"]
            leave_many(u, 0, 16, ACT.Gelu_apprx_tanh)
            mod_out(3)
            leave_many(u + 16, 16, 16, ACT.Gelu_apprx_tanh)
            std(D, count=2)
            mod_out(4)
            leave_many(u + 32, 32, 16, ACT.Silu)
            for b in range(4):
                act.wait_ge(vt_done, b + 1)
                half = (b % 2) * 1024
                nc.scalar.activation(sq[:, (b // 2) * D + (b % 2) * 1024:(b // 2) * D + (b % 2) * 1024 + 1024],
                                     M[:, half:half + 1024], ACT.Copy).then_inc(vt_copied, 1)
            mod_out(5)
            act.wait_ge(mods_ready, 4)
            leave_gated(UNIT0["od_out"], mod("gate1"))
            mod_out(6)
            std(D)
            std(D)
            u = UNIT0["w_in"]
            leave_many(u, 0, 4, ACT.Copy)
            act.wait_ge(f_exp_in, 1)
            nc.scalar.activation(f_exp_row, f_exp_row, ACT.Exp).then_inc(f_exp, 1)
            act.wait_ge(f_ln_in, 1)
            nc.scalar.activation(f_exp_row, f_exp_row, ACT.Ln).then_inc(f_ln, 1)

            def copy_b(q):
                act.wait_ge(ssm_bt, q + 1)
                nc.scalar.activation(sq[:, 0:1024].rearrange("p (a b) -> p a b", a=2),
                                     M[:, :].rearrange("p (a b) -> p a b", a=2)[:, :, 0:512], ACT.Copy).then_inc(ssm_btc, 1)

            def gelu_y(q):
                act.wait_ge(ssm_yd, q + 1)
                nc.scalar.activation(proj[:, q, :], proj[:, q, :], ACT.Gelu).then_inc(ssm_g, 1)

            copy_b(0)
            leave_many(u + 4, 4, 4, ACT.Copy)
            leave_many(u + 8, 8, 4, ACT.Copy)
            for q in range(1, 4):
                copy_b(q)
                leave_many(u + 8 + 4 * q, 8 + 4 * q, 4, ACT.Copy)
                gelu_y(q - 1)
            leave_many(u + 24, 24, 4, ACT.Copy)
            gelu_y(3)
            head_stds(8)
            head_stds(8)
            for t in range(4):
                leave(UNIT0["glu"] + t, proj[:, 28 + t, :], ACT.Sigmoid, bias=V("b_glu")[:, t:t + 1])
            act.wait_ge(v_turned, 2)
            nc.scalar.activation(flat(proj[:, 36:44, :]), M[:, :], ACT.Copy).then_inc(v_ready, 1)
            softmax_steps(8, 2, sq[:, 2048:2560], 1.0)
            mod_out(7)
            act.wait_ge(pv_done, 16)
            leave_many(UNIT0["ssm_up"], 32, 16, ACT.Copy)
            for n in range(DT):
                leave(UNIT0["attn_up"] + n, sq[:, n * TOK:(n + 1) * TOK], ACT.Copy)
            mod_out(8)
            act.wait_ge(unit_done, UNIT0["gates"])
            leave_many(UNIT0["gates"], 0, 32, ACT.Sigmoid)
            act.wait_ge(mods_ready, 7)
            leave_gated(UNIT0["w_out"], mod("gate2"))
            act.dma_start(flat(proj[:, 40:48, :]), keysT).then_inc(keys_in, 16)
            std(D)

            def to_tokens(dst, first):
                for b in range(4):
                    act.wait_ge(ht_done, first + b + 1)
                    half = (b % 2) * 1024
                    nc.scalar.activation(dst[:, (b // 2) * D + half:(b // 2) * D + half + 1024], M[:, half:half + 1024],
                                         ACT.Copy).then_inc(ht_copied, 1)

            to_tokens(sq, 0)
            to_tokens(flat(acc[:, :, :]), 4)
            leave_many(UNIT0["peer_q"], 0, 16, ACT.Copy)
            for tt in range(2):
                act.wait_ge(sc_done, tt + 1)
                nc.scalar.activation(flat(proj[:, 16 + 8 * tt:24 + 8 * tt, :]), M[:, :], ACT.Copy).then_inc(sc_copied, 1)
            for tt in range(2):
                act.wait_ge(gexp_in, tt + 1)
                g = flat(proj[:, 41:42, :])[:, tt * P:(tt + 1) * P]
                nc.scalar.activation(g, g, ACT.Exp).then_inc(gexp_out, 1)
            gw = flat(proj[:, 41:42, :])
            act.wait_ge(picks_ready, 2)
            with act.Fori(0, 2 * NSLOT // SLOTS) as i:
                for s in range(SLOTS):
                    act.wait_ge(dot_done, SLOTS * i + s + 1)
                    nc.scalar.activation(dots[:, SLOTS + s:SLOTS + s + 1], dots[:, s:s + 1], ACT.Gelu).then_inc(gelu_done, 1)
                    act.wait_ge(gelu_done, SLOTS * i + s + 1)
                    nc.scalar.activation(dots[:, 2 * SLOTS + s:2 * SLOTS + s + 1], gw[:, bass.ds(SLOTS * i + s, 1)],
                                         ACT.Copy, scale=dots[:, SLOTS + s:SLOTS + s + 1]).then_inc(coef_ready, 1)

        @block.vector
        def _(dve):
            V_ = nc.vector
            counts = {}

            def step(ins, on=None):
                s, key = (dve_step, "step") if on is None else (on, on.name)
                counts[key] = counts.get(key, 0) + 1
                ins.then_inc(s, 1)
                dve.wait_ge(s, counts[key])

            tt = V_.tensor_tensor
            loop_count = [0]

            def affine(buf, n, mul, add=None):
                base = loop_count[0]
                loop_count[0] += n
                with dve.Fori(0, n // 4) as i:
                    for j in range(4):
                        t = buf[:, bass.ds(j * TOK + i * (4 * TOK), TOK)]
                        m = mul[:, bass.ds(4 * i + j, 1)]
                        a = None if add is None else add[:, bass.ds(4 * i + j, 1)]
                        V_.tensor_scalar(t, t, m, a, ALU.mult, *([] if add is None else [ALU.add])).then_inc(tile_step, 1)
                dve.wait_ge(tile_step, base + n)

            sums = {"sum": 0, "std": 0}

            def square_sum(src3, n, dst=None):
                s = flat(src3)
                step(tt(sq[:, 0:n * TOK], s, s, ALU.mult), on=sum_in)

            def root():
                sums["std"] += 1
                dve.wait_ge(std_ready, sums["std"])
                step(V_.reciprocal(rstd[:, :], rstd[:, :]))

            def scaled(dst3, src3, n):
                step(tt(dst3, src3, over_tiles(rstd[:, :], n), ALU.mult))

            def centre(t3, n, nth):
                dve.wait_ge(sum_done, nth)
                step(V_.scalar_tensor_tensor(out=t3, in0=over_tiles(B7[:, 0:TOK], n), scalar=-1.0 / (n * P), in1=t3,
                                             op0=ALU.mult, op1=ALU.add))

            def ada_group(g):
                if g < 2:
                    dve.wait_ge(pre_cols, 2)
                else:
                    dve.wait_ge(mod_sums, g - 1)
                v = 0 if g < 4 else 32
                a = acc[:, g % 2, :]

                def chunk(k, i):
                    s = k % SLOTS
                    dve.wait_ge(ada_in[s], 16 * (4 * (PRE_GROUPS + g) + 1 + i))
                    c = cond[:, bass.ds(v + s + SLOTS * i, 1)]
                    if k == 0 and isinstance(i, int):
                        V_.tensor_scalar(a, aring[:, s, :], c, None, ALU.mult).then_inc(ada_dve_used, 1)
                    else:
                        dve.wait_ge(ada_dve_used, 16 * g + s + SLOTS * i)
                        V_.scalar_tensor_tensor(out=a, in0=aring[:, s, :], scalar=c, in1=a, op0=ALU.mult,
                                                op1=ALU.add).then_inc(ada_dve_used, 1)

                for k in range(SLOTS):
                    chunk(k, 0)
                with dve.Fori(1, 16 // SLOTS) as i:
                    for k in range(SLOTS):
                        chunk(k, i)

            def mods_from(g):
                dve.wait_ge(mod_copied, g + 1)
                m = mods[:, 16 * (4 + g):16 * (5 + g)]
                step(tt(m, m, V("ada_b")[:, 16 * (2 + g):16 * (3 + g)], ALU.add), on=mods_ready)

            def modulated(buf3, norm, scale, shift):
                step(V_.scalar_tensor_tensor(out=gs[:, :], in0=scale, scalar=1.0, in1=norm, op0=ALU.add, op1=ALU.mult))
                affine(flat(buf3), DT, gs, shift)

            def head_norm(src, n, weight):
                step(tt(head_sq_at[:, 0:n * TOK], src, src, ALU.mult), on=head_sq)
                counts["head"] = counts.get("head", 0) + 1
                dve.wait_ge(head_std, counts["head"])
                step(V_.reciprocal(head_sq_at[:, 0:n * TOK], head_sq_at[:, 0:n * TOK]))
                return V_.scalar_tensor_tensor(out=src, in0=src, scalar=weight, in1=head_sq_at[:, 0:n * TOK],
                                               op0=ALU.mult, op1=ALU.mult)

            def rope(src3, n, nth):
                dve.wait_ge(rot_done, nth)
                t = tiles(head_sq_at[:, 0:n * TOK], n)
                step(tt(t, tiles(M[:, 0:n * TOK], n), over_tiles(C("sin"), n), ALU.mult))
                step(tt(src3, src3, over_tiles(C("cos"), n), ALU.mult))
                return tt(src3, src3, t, ALU.add)

            def softmax(base, nk, scale, finish):
                w = nk * P
                probs = att[:, 0:2 * w].rearrange("p (a b) -> p a b", a=2)

                def maxima(hh):
                    dve.wait_ge(s_done, base + hh + 1)
                    s = M[:, 0:2 * w].rearrange("p (a b) -> p a b", a=2)
                    if base:
                        if hh:
                            dve.wait_ge(pt_done, base + hh)
                        step(tt(probs, s, C("mask").rearrange("p (a b) -> p a b", a=2), ALU.add))
                        s = probs
                    step(V_.tensor_reduce(small[:, 0:2], s, AX, ALU.max))
                    step(V_.tensor_scalar(small[:, 2:4], small[:, 0:2], -scale, None, ALU.mult), on=nmax_ready)

                maxima(0)
                for hh in range(HEADS):
                    dve.wait_ge(exp_done, 2 * (base + hh + 1))
                    step(V_.reciprocal(small[:, 6:8], small[:, 4:6]))
                    step(V_.tensor_scalar(probs[:, 0, :], probs[:, 0, :], small[:, 6:7], None, ALU.mult))
                    step(V_.tensor_scalar(probs[:, 1, :], probs[:, 1, :], small[:, 7:8], None, ALU.mult), on=p_ready)
                    if hh + 1 < HEADS:
                        maxima(hh + 1)
                    dve.wait_ge(pv_done, base + hh + 1)
                    finish(hh, O[hh % 2][:, 0:TOK])

            step(V_.memset(eps, EPS))
            dve.wait_ge(trig_out, 1)
            S = lambda a: small[:, a:a + 16]
            dt, mag, theta, sin_, cos_, k_, t0, t1 = S(16), S(32), S(48), S(64), S(80), S(96), S(112), S(128)
            cr, ci = S(144), S(160)
            step(tt(mag, V("A_re"), dt, ALU.mult))
            step(tt(theta, V("A_im"), dt, ALU.mult), on=trig_in)
            step(V_.tensor_scalar(k_, theta, 1.0 / (2 * np.pi), ROUND, ALU.mult, ALU.add))
            step(V_.tensor_scalar(k_, k_, ROUND, None, ALU.subtract))
            step(V_.scalar_tensor_tensor(out=t0, in0=k_, scalar=-TURN[0], in1=theta, op0=ALU.mult, op1=ALU.add))
            step(V_.scalar_tensor_tensor(out=t1, in0=k_, scalar=-TURN[1], in1=t0, op0=ALU.mult, op1=ALU.add))
            step(V_.scalar_tensor_tensor(out=t0, in0=k_, scalar=-TURN[2], in1=t1, op0=ALU.mult, op1=ALU.add))
            step(V_.tensor_scalar(sin_, t0, HALF_TURN, -HALF_TURN, ALU.min, ALU.max))
            step(V_.scalar_tensor_tensor(out=t1, in0=sin_, scalar=-1.0, in1=sin_, op0=ALU.mult, op1=ALU.max))
            step(V_.tensor_scalar(cos_, t1, -1.0, float(np.pi / 2), ALU.mult, ALU.add), on=trig_in)
            dve.wait_ge(trig_out, 3)
            step(V_.tensor_copy(powers[:, 0, 0, :], cos_))
            step(V_.tensor_copy(powers[:, 0, 1, :], sin_))
            for k in range(7):
                c, s_ = powers[:, k, 0, :], powers[:, k, 1, :]
                step(tt(t0, c, c, ALU.mult))
                step(tt(t1, s_, s_, ALU.mult))
                step(tt(powers[:, k + 1, 0, :], t0, t1, ALU.subtract))
                step(V_.scalar_tensor_tensor(out=powers[:, k + 1, 1, :], in0=c, scalar=2.0, in1=s_, op0=ALU.mult,
                                             op1=ALU.mult))
            a_re, a_im, den = cos_, sin_, k_
            step(tt(a_re, mag, cos_, ALU.mult))
            step(tt(a_im, mag, sin_, ALU.mult))
            step(V_.tensor_scalar(a_re, a_re, 1.0, None, ALU.subtract))
            step(tt(t0, V("A_re"), V("A_re"), ALU.mult))
            step(tt(t1, V("A_im"), V("A_im"), ALU.mult))
            step(tt(den, t0, t1, ALU.add))
            step(V_.reciprocal(den, den))
            for out_, p_, q_, op in ((cr, (a_re, "A_re"), (a_im, "A_im"), ALU.add),
                                     (ci, (a_im, "A_re"), (a_re, "A_im"), ALU.subtract)):
                step(tt(t0, p_[0], V(p_[1]), ALU.mult))
                step(tt(t1, q_[0], V(q_[1]), ALU.mult))
                step(tt(t0, t0, t1, op))
                step(tt(out_, t0, den, ALU.mult))
            wide = lambda ap: ap.unsqueeze(2).to_broadcast([P, 16, 16])
            square = lambda ap: ap.rearrange("p (a b) -> p a b", a=16)
            b_re, b_im = square(V("B_re")), square(V("B_im"))
            x0, x1, x2 = (square(att[:, 256 * i:256 * (i + 1)]) for i in range(3))
            step(tt(x0, b_re, wide(cr), ALU.mult))
            step(tt(x1, b_im, wide(ci), ALU.mult))
            step(tt(x2, b_re, wide(ci), ALU.mult))
            step(tt(b_re, x0, x1, ALU.subtract))
            step(tt(x0, b_im, wide(cr), ALU.mult))
            step(tt(b_im, x0, x2, ALU.add))
            step(V_.tensor_scalar(V("C_im"), V("C_im"), -1.0, None, ALU.mult))
            step(V_.tensor_scalar(small[:, 9:10], V("q_norm_2"), HD ** -0.5, None, ALU.mult))
            step(V_.memset(att[:, :], 0.0))

            dve.wait_ge(ctx_in, 16)
            square_sum(craw, DT)
            root()
            scaled(hc, craw, DT)
            dve.wait_ge(x_in, 16)
            square_sum(x[:, :, :], DT)
            root()
            scaled(h[:, :, :], x[:, :, :], DT)
            dve.wait_ge(pre_cols, 2)
            for v in range(2):
                step(tt(mods[:, 32 * v:32 * v + 32].rearrange("p (g m) -> p g m", g=2),
                        B6[:, 0:64].rearrange("p (g m v) -> p v g m", g=2, v=2)[:, v],
                        V("ada_b")[:, 0:32].rearrange("p (g m) -> p g m", g=2), ALU.add))
            modulated(hc, V("norm_g0"), mod("scale0c"), mod("shift0c"))
            modulated(h[:, :, :], V("norm_g0"), mod("scale0"), mod("shift0"))
            dve.sem_inc(h_ready, 1)

            ada_group(0)
            dve.wait_ge(unit_evac, UNIT0["ev"])
            step(head_norm(sq[:, 0:1024], 4, V("k_norm")), on=rot_in)
            ada_group(1)
            step(rope(kv_keys[:, :, 0:TOK], 2, 1))
            ev = UNIT0["ev"]
            dve.wait_ge(unit_evac, ev + 8)
            step(head_norm(flat(proj[:, 0:8, :]), 8, V("q_norm")), on=rot_in)
            dve.wait_ge(unit_evac, ev + 24)
            padded = tiles(att[:, :], CONV_T)
            step(tt(padded[:, :, CONV_W // 2:CONV_W // 2 + TOK], proj[:, 8:16, :], proj[:, 16:24, :], ALU.mult))
            aflat, pflat = att[:, :], flat(proj[:, :, :])
            with dve.Fori(0, CONV_T // 2) as i:
                for k in range(CONV_W):
                    for e in range(2):
                        o = pflat[:, bass.ds((8 + e) * TOK + i * (2 * TOK), TOK)]
                        src = aflat[:, bass.ds(e * PADW + k + i * (2 * PADW), TOK)]
                        wk = V("dw_w")[:, bass.ds(e * CONV_W + k + i * (2 * CONV_W), 1)]
                        if k == 0:
                            V_.tensor_scalar(o, src, wk, V("dw_b")[:, bass.ds(e + 2 * i, 1)], ALU.mult,
                                             ALU.add).then_inc(conv_step, 1)
                        else:
                            dve.wait_ge(conv_step, 2 * (k - 1) + e + 1 + i * (2 * CONV_W))
                            V_.scalar_tensor_tensor(out=o, in0=src, scalar=wk, in1=o, op0=ALU.mult,
                                                    op1=ALU.add).then_inc(conv_step, 1)
            dve.wait_ge(conv_step, CONV_T * CONV_W)
            step(rope(proj[:, 0:8, :], 8, 2), on=qk_ready)
            mods_from(0)
            mods_from(1)
            dve.wait_ge(unit_evac, ev + 40)

            def gate_attention(hh, o):
                step(tt(proj[:, hh, :], o, proj[:, 24 + hh, :], ALU.mult), on=o_read)

            softmax(0, 4, HD ** -0.5, gate_attention)
            dve.sem_inc(sum_in, 1)
            counts["sum_in"] = counts.get("sum_in", 0) + 1
            conv = proj[:, 8:16, :]
            centre(conv, CONV_T, 3)
            square_sum(conv, CONV_T)
            root()
            step(tt(conv, conv, over_tiles(rstd[:, :], CONV_T), ALU.mult), on=conv_normed)
            dve.wait_ge(conv_act, CONV_T)
            step(tt(conv, conv, proj[:, 32:40, :], ALU.mult), on=mix_ready)

            def add_residual(name):
                dve.wait_ge(unit_evac, UNIT0[name] + 16)
                step(tt(flat(x[:, :, :]), flat(x[:, :, :]), flat(h[:, :, :]), ALU.add))

            def normed_into_h(norm, scale, shift):
                square_sum(x[:, :, :], DT)
                root()
                scaled(h[:, :, :], x[:, :, :], DT)
                modulated(h[:, :, :], norm, scale, shift)
                dve.sem_inc(h_ready, 1)

            ada_group(2)
            mods_from(2)
            add_residual("ev_out")
            normed_into_h(V("norm_g1"), mod("scale1"), mod("shift1"))

            ada_group(3)
            od = UNIT0["od"]
            v = proj[:, 0:16, :]
            centre(v, DT, 6)
            square_sum(v, DT)
            ada_group(4)
            root()
            scaled(v, v, DT)
            affine(flat(v), DT, V("od_g"), V("od_b"))
            dve.sem_inc(gate_v_ready, 1)
            mods_from(3)
            ada_group(5)
            dve.wait_ge(unit_evac, od + 48)
            uz = flat(proj[:, 16:32, :])
            step(tt(uz, uz, flat(proj[:, 32:48, :]), ALU.mult))
            dve.wait_ge(bs_in, 16)
            for b in range(4):
                dve.wait_ge(sgu_done, b + 1)
                for e in range(2):
                    g = 2 * b + e
                    lo = (b % 2) * 1024 + e * 512
                    step(tt(tiles(flat(proj[:, 2 * g:2 * g + 2, :]), 4), tiles(M[:, lo:lo + 512], 4),
                            over_tiles(att[:, 1024 + g * P:1024 + (g + 1) * P], 4), ALU.add),
                         on=sgu_read if e else None)
                t4 = flat(proj[:, 4 * b:4 * b + 4, :])
                step(tt(t4, t4, uz[:, 1024 * b:1024 * (b + 1)], ALU.mult), on=sgu_ready if b == 3 else None)

            mods_from(4)
            mods_from(5)
            ada_group(6)
            add_residual("od_out")
            square_sum(x[:, :, :], DT)
            root()
            scaled(x[:, :, :], x[:, :, :], DT)
            affine(flat(x[:, :, :]), DT, V("final_g"))
            normed_into_h(V("norm1_w"), mod("scale2"), mod("shift2"))
            mods_from(6)

            gmask = C("gmask").rearrange("p (j g) -> p j g", j=4).unsqueeze(3).to_broadcast([P, 4, 8, 16])

            def expand(dst, name, q, on=None):
                src = square(V(name))[:, 4 * q:4 * q + 4, :].unsqueeze(2).to_broadcast([P, 4, 8, 16])
                step(tt(dst.rearrange("p (j g c) -> p j g c", j=4, g=8), src, gmask, ALU.mult), on=on)

            def expand_b(q):
                expand(att[:, 0:512], "B_re", q)
                expand(att[:, 512:1024], "B_im", q, on=ssm_bc)

            def times(dst, a, b):
                step(tt(dst, a, b, ALU.mult))

            def cross(dst, a, b, c, d, op, on=None):
                times(dst, a, b)
                times(tmp4, c, d)
                step(tt(dst, dst, tmp4, op), on=on)

            expand_b(0)
            dve.wait_ge(f_done, 1)
            z, zmin, ze = cum, f_min, f_exp_row
            step(V_.tensor_scalar(z, B7[0:8, 0:TOK], V("b_forget")[0:8, :], None, ALU.add))
            step(V_.tensor_scalar(zmin, z, 0.0, None, ALU.min))
            step(V_.scalar_tensor_tensor(out=ze, in0=z, scalar=-1.0, in1=z, op0=ALU.mult, op1=ALU.min), on=f_exp_in)
            dve.wait_ge(f_exp, 1)
            step(V_.tensor_scalar(ze, ze, 1.0, None, ALU.add), on=f_ln_in)
            dve.wait_ge(f_ln, 1)
            step(tt(zmin, zmin, ze, ALU.subtract))
            step(V_.tensor_tensor_scan(cum, ones[0:8, 0:1].to_broadcast([8, TOK]), zmin, 0.0, ALU.mult, ALU.add))
            step(V_.tensor_scalar(ncum, cum, -1.0, None, ALU.mult), on=cum_ready)

            def ssm(q):
                expand(sq[:, 1024:1536], "C_re", q)
                expand(sq[:, 1536:2048], "C_im", q)
                step(V_.memset(turn_cos[:, :, 0:1], 1.0))
                step(V_.memset(turn_sin[:, :, 0:1], 0.0))
                for k in range(8):
                    n = 1 << k
                    pc, ps = (powers[:, k, e, 4 * q:4 * q + 4].unsqueeze(2).to_broadcast([P, 4, n]) for e in range(2))
                    lo_c, lo_s = turn_cos[:, :, 0:n], turn_sin[:, :, 0:n]
                    hi_c, hi_s, t = turn_cos[:, :, n:2 * n], turn_sin[:, :, n:2 * n], tmp4[:, :, 0:n]
                    times(hi_c, lo_c, pc)
                    times(t, lo_s, ps)
                    step(tt(hi_c, hi_c, t, ALU.subtract))
                    times(hi_s, lo_c, ps)
                    times(t, lo_s, pc)
                    step(tt(hi_s, hi_s, t, ALU.add))
                dve.wait_ge(ssm_bu, q + 1)
                bu_re, bu_im = tiles(M[:, 0:1024], 4), tiles(M[:, 1024:2048], 4)
                cross(w_re, bu_re, turn_cos, bu_im, turn_sin, ALU.add)
                cross(w_im, bu_im, turn_cos, bu_re, turn_sin, ALU.subtract)
                if q < 3:
                    expand_b(q + 1)
                for j in range(4):
                    decay = mag[:, 4 * q + j:4 * q + j + 1].to_broadcast([P, TOK])
                    for z_, w_ in ((z_re, w_re), (z_im, w_im)):
                        step(V_.tensor_tensor_scan(z_[:, j * TOK:(j + 1) * TOK], decay, w_[:, j, :], 0.0, ALU.mult,
                                                   ALU.add))
                zr, zi = tiles(z_re, 4), tiles(z_im, 4)
                cross(w_re, zr, turn_cos, zi, turn_sin, ALU.subtract)
                cross(w_im, zr, turn_sin, zi, turn_cos, ALU.add, on=ssm_s)
                dve.wait_ge(ssm_y, q + 1)
                step(V_.scalar_tensor_tensor(out=proj[:, q, :], in0=proj[:, q, :], scalar=V("ssm_D")[:, q:q + 1],
                                             in1=B6[:, 0:TOK], op0=ALU.mult, op1=ALU.add), on=ssm_yd)

            for q in range(4):
                ssm(q)

            wi = UNIT0["w_in"]
            dve.wait_ge(unit_evac, wi + 12)
            step(head_norm(flat(proj[:, 4:12, :]), 8, V("k_norm_2")))
            dve.wait_ge(unit_evac, wi + 20)
            step(head_norm(flat(proj[:, 12:20, :]), 8, small[:, 9:10]), on=qk_ready)
            dve.wait_ge(unit_evac, UNIT0["glu"] + 4)
            y4 = flat(proj[:, 0:4, :])
            step(tt(y4, y4, flat(proj[:, 28:32, :]), ALU.mult), on=glu_ready)

            def keep_attention(hh, o):
                step(V_.tensor_copy(proj[:, 12 + hh, :], o), on=o_read)

            softmax(8, 2, 1.0, keep_attention)

            ada_group(7)
            ada_group(8)
            gates = UNIT0["gates"]
            s_branch, a_branch = flat(proj[:, 32:48, :]), sq[:, :]
            dve.wait_ge(unit_evac, gates + 16)
            step(tt(s_branch, s_branch, flat(proj[:, 0:16, :]), ALU.mult))
            ada_group(9)
            dve.wait_ge(unit_evac, gates + 32)
            step(tt(a_branch, a_branch, flat(proj[:, 16:32, :]), ALU.mult))
            step(tt(s_branch, s_branch, a_branch, ALU.add), on=merged)
            mods_from(7)
            mods_from(8)
            add_residual("w_out")
            normed_into_h(V("norm2_w"), mod("scale3"), mod("shift3"))
            dve.wait_ge(g3_done, 1)
            dve.wait_ge(g3b_in, 16)
            step(tt(att[:, 0:D], att[:, 0:D], M[:, :], ALU.add), on=g3_ready)

            tile = lambda n: flat(proj[:, n:n + 1, :])
            sv = tile(32).rearrange("p (r k) -> p r k", r=16)
            si = tile(33).bitcast(U32).rearrange("p (r k) -> p r k", r=16)
            sif = tile(34).rearrange("p (h s k) -> p h s k", h=8, s=2)
            tv = tile(35)[:, 0:128].rearrange("p (h k) -> p h k", h=8)
            tp = tile(35)[:, 128:256].bitcast(U32).rearrange("p (h k) -> p h k", h=8)
            half_i = tile(36).bitcast(U32)
            half_f = tile(37)
            chosen = tile(38)
            gsum = tile(39)
            masked = tile(43)
            cand = flat(proj[:, 0:8, :]).rearrange("p (h a b) -> p h a b", h=8, a=16)
            pick = flat(proj[:, 8:16, :]).rearrange("p (h a b) -> p h a b", h=8, a=16)
            iota = C("iota").unsqueeze(1).unsqueeze(1).to_broadcast([P, 8, 16, 16])

            def top16(values, best, where, width):
                step(V_.max(best[:, 0:8], values))
                step(V_.max_index(where[:, 0:8], best[:, 0:8], values))
                step(V_.match_replace(masked[:, 0:width], best[:, 0:8], values, LOWEST))
                step(V_.max(best[:, 8:16], masked[:, 0:width]))
                step(V_.max_index(where[:, 8:16], best[:, 8:16], masked[:, 0:width]))

            dve.wait_ge(sc_done, 2)
            for tk in range(2):
                dve.wait_ge(sc_copied, tk + 1)
                for r in range(16):
                    row = flat(proj[:, 16 + 8 * tk:24 + 8 * tk, :])[:, r * P:(r + 1) * P]
                    top16(row, sv[:, r, :], si[:, r, :], P)
                step(V_.tensor_copy(tile(34), tile(33).bitcast(U32)))
                svh = sv.rearrange("p (h s) k -> p h s k", s=2)
                step(tt(cand, svh[:, :, 0, :].unsqueeze(3).to_broadcast([P, 8, 16, 16]),
                        svh[:, :, 1, :].unsqueeze(2).to_broadcast([P, 8, 16, 16]), ALU.add))
                for hh in range(HEADS):
                    top16(flat(proj[:, hh:hh + 1, :]), tv[:, hh, :], tp[:, hh, :], 256)
                tpf = tile(35)[:, 128:256].bitcast(U32)
                step(V_.tensor_scalar(half_i[:, 0:128], tpf, 4, None, ALU.logical_shift_right))
                step(V_.tensor_scalar(half_i[:, 128:256], tpf, 15, None, ALU.bitwise_and))
                step(V_.tensor_copy(half_f, half_i))
                for s in range(2):
                    place = half_f[:, s * 128:(s + 1) * 128].rearrange("p (h k) -> p h k", h=8)
                    step(tt(pick, place.unsqueeze(3).to_broadcast([P, 8, 16, 16]), iota, ALU.is_equal))
                    step(tt(pick, pick, sif[:, :, s, :].unsqueeze(2).to_broadcast([P, 8, 16, 16]), ALU.mult))
                    step(V_.tensor_reduce(chosen[:, s * 128:(s + 1) * 128].rearrange("p (h k) -> p h k", h=8), pick, AX,
                                          ALU.add))
                step(V_.scalar_tensor_tensor(out=chosen[:, 0:128], in0=chosen[:, 0:128], scalar=128.0,
                                             in1=chosen[:, 128:256], op0=ALU.mult, op1=ALU.add))
                step(V_.tensor_copy(tile(40).bitcast(U32)[:, tk * P:(tk + 1) * P], chosen[:, 0:128]))
                gw = tile(41)[:, tk * P:(tk + 1) * P]
                gw3 = gw.rearrange("p (h k) -> p h k", h=8)
                step(tt(gw3, tv, tv[:, :, 0:1].to_broadcast([P, 8, 16]), ALU.subtract), on=gexp_in)
                dve.wait_ge(gexp_out, tk + 1)
                step(V_.tensor_reduce(gsum[:, 0:8], gw3, AX, ALU.add))
                step(V_.reciprocal(gsum[:, 8:16], gsum[:, 0:8]))
                step(tt(gw3, gw3, gsum[:, 8:16].unsqueeze(2).to_broadcast([P, 8, 16]), ALU.mult), on=picks_ready)

            dve.wait_ge(unit_done, NUNIT)
            dve.wait_ge(ht_copied, 8)
            step(V_.memset(flat(h[:, :, :]), 0.0))
            unused = flat(proj[:, 0:8, :])
            for tk in range(2):
                total = flat(h[:, :, :])[:, tk * D:(tk + 1) * D]
                tokens = sq[:, tk * D:(tk + 1) * D]

                def dot(i, s):
                    n = NSLOT * tk + s
                    dve.wait_ge(u_in[s], 16 * (NSLOT // SLOTS * tk + 1) + 16 * i)
                    if not (tk == 0 and s == 0):
                        dve.wait_ge(dot_done, n + SLOTS * i)
                    V_.tensor_tensor_reduce(out=unused, in0=tokens, in1=ring[:, s, :], scale=1.0, scalar=0.0,
                                            op0=ALU.mult, op1=ALU.add, accum_out=dots[:, s:s + 1]).then_inc(dot_done, 1)

                def add(i, s):
                    n = NSLOT * tk + s
                    dve.wait_ge(v_in[s], 16 * (NSLOT // SLOTS * tk + 1) + 16 * i)
                    dve.wait_ge(coef_ready, n + 1 + SLOTS * i)
                    if not (tk == 0 and s == 0):
                        dve.wait_ge(v_added, n + SLOTS * i)
                    V_.scalar_tensor_tensor(out=total, in0=aring[:, s, :], scalar=dots[:, 2 * SLOTS + s:2 * SLOTS + s + 1],
                                            in1=total, op0=ALU.mult, op1=ALU.add).then_inc(v_added, 1)

                with dve.Fori(0, NSLOT // SLOTS) as i:
                    for s in range(SLOTS):
                        dot(i, s)
                        if s > 0:
                            add(i, s - 1)
                    add(i, SLOTS - 1)
                dve.wait_ge(v_added, NSLOT * (tk + 1))
                step(tt(total, total, att[:, 0:D], ALU.mult))
                step(tt(total, total, acc[:, tk, :], ALU.add), on=out_ready)


def kernel(**inputs):
    import concourse.bacc as bacc
    from concourse.bass_utils import run_bass_kernel_spmd as run

    a = {k: np.asarray(v) for k, v in inputs.items()}

    def feature_major(v):
        return v.reshape(-1, P).T

    def tokens_last(m):
        return np.ascontiguousarray(m.T.reshape(-1, P, TOK).transpose(1, 0, 2)).reshape(P, -1)

    def chunks(w):
        k, n = w.shape
        per = D // k
        t = w.reshape(k // P, P, n // (P * per), per, P).transpose(2, 1, 3, 0, 4)
        return t.reshape(n // (P * per), P, CHUNK)

    ev = a["ev_w_in"][0]
    kv, q, za, ga, gb, zb = np.split(ev, [512, 1536, 2560, 3584, 4608], axis=1)
    u_, v_, z_ = np.split(a["od_w_in"][0], 3, axis=1)
    q2, k2, v2, f2, s2, gs2, ga2 = np.split(a["w_in_2"][0], [1024, 2048, 3072, 3080, 3592, 5640], axis=1)
    parts = [kv, q, ga, gb, za, zb, a["ev_w_out"][0], v_, u_, z_, a["od_w_out"][0], s2, k2, q2, v2, a["w_glu_2"][0],
             a["w_ssm_up_2"][0], a["w_attn_up_2"][0], gs2, ga2, a["w_out_2"][0], a["w_peer_q_2"][0]]
    weights = np.concatenate([chunks(w) for w in parts])
    assert len(weights) == NCHUNK

    a0, a1, a2 = a["ada_w"][0], a["ada_w"][1], a["w_ada_2"][0]
    groups = [(a0, 0), (a0, 1), (a0, 2), (a1, 0), (a1, 1), (a1, 2)] + [(a2, i) for i in range(6)]
    ada = np.concatenate([w[:, D * i:D * (i + 1)].reshape(DT, P, D) for w, i in groups])
    biases = np.concatenate([a["ada_b"][0], a["ada_b"][1], a["b_ada_2"][0]])

    vecs = np.zeros((P, NVEC), np.float32)

    def put(name, v):
        at, w = VEC[name]
        vecs[:, at:at + w] = v

    put("cond", np.concatenate([feature_major(a["c"]), feature_major(a["c_ctx"]), feature_major(a["c_2"])], axis=1))
    put("ada_b", feature_major(biases))
    for name, v in (("norm_g0", a["norm_g"][0]), ("norm_g1", a["norm_g"][1]), ("final_g", a["final_g"]),
                    ("norm1_w", a["norm1_w_2"]), ("norm2_w", a["norm2_w_2"]), ("q_norm", a["ev_q_norm"]),
                    ("k_norm", a["ev_k_norm"]), ("q_norm_2", a["q_norm_w_2"]), ("k_norm_2", a["k_norm_w_2"]),
                    ("dw_b", a["ev_dw_b"]), ("ln_g", a["ev_ln_g"]), ("ln_b", a["ev_ln_b"]), ("od_g", a["od_ln_g"]),
                    ("od_b", a["od_ln_b"]), ("A_re", a["ssm_A_re_2"]), ("A_im", a["ssm_A_im_2"]),
                    ("log_dt", np.repeat(a["ssm_log_dt_2"][0], 64)), ("ssm_D", a["ssm_D_2"]), ("b_glu", a["b_glu_2"])):
        put(name, feature_major(v))
    put("dw_w", a["ev_dw_w"][0].reshape(CONV_W, CONV_T, P).transpose(2, 1, 0).reshape(P, -1))
    vecs[0:8, VEC["b_forget"][0]] = a["b_forget_2"][0]
    for name in ("B_re", "B_im"):
        put(name, a[f"ssm_{name}_2"][0].reshape(16, P, 16).transpose(1, 0, 2).reshape(P, -1))
    for name in ("C_re", "C_im"):
        put(name, a[f"ssm_{name}_2"][0].transpose(0, 2, 1).reshape(16, P, 16).transpose(1, 0, 2).reshape(P, -1))
    put("w_f", f2.reshape(DT, P, 8).transpose(1, 0, 2).reshape(P, -1))

    arrays = {
        "xT": tokens_last(a["x"][0]), "ctxT": tokens_last(a["ctx"][0]), "consts": constants(), "vecs": vecs,
        "weights": weights, "ada": ada,
        "keysT": np.ascontiguousarray(a["peer_sub_keys_2"][0].reshape(16, P, P).transpose(2, 0, 1)).reshape(P, -1),
        "wsT": np.ascontiguousarray(a["od_ws"][0].transpose(2, 0, 1)).reshape(P, -1),
        "bs": np.ascontiguousarray(a["od_bs"][0]).reshape(-1),
        "g3_bias": np.ascontiguousarray(a["b_ada_2"][0][5 * D:]),
        "peer_u": np.ascontiguousarray(a["peer_u_2"][0]), "peer_v": np.ascontiguousarray(a["peer_v_2"][0]),
    }
    nc = bacc.Bacc("TRN2", target_bir_lowering=False, num_devices=1)
    args = [nc.dram_tensor(n, v.shape, F32, kind="ExternalInput").ap() for n, v in arrays.items()]
    out = nc.dram_tensor("out", (TOK, D), F32, kind="ExternalOutput").ap()
    build(nc, *args, out)
    r = run(nc, [arrays], core_ids=[0])
    return r.results[0]["out"].reshape(1, TOK, D)
```

```python
from contextlib import ExitStack

import concourse.bass as bass
from concourse import mybir
from concourse.alu_op_type import AluOpType as ALU
import numpy as np

F32 = mybir.dt.float32
U32 = mybir.dt.uint32
ACT = mybir.ActivationFunctionType
AX = mybir.AxisListType.X

P = 128
TOK = 256
D = 2048
DT = D // P
EPS = 1e-6
CHUNK = 2048
SLOTS = 4
HEADS = 8
HD = 128
KV = 2
CONV_T = 8
CONV_W = 31
PADW = TOK + CONV_W - 1
SEL = 16
NSLOT = HEADS * SEL
NEG = -1e30
LOWEST = -3.0e38
_hi = float(np.float32(np.floor(2 * np.pi * 2.0 ** 8) / 2.0 ** 8))
_mid = float(np.floor((2 * np.pi - _hi) * 2.0 ** 20) / 2.0 ** 20)
TURN = (_hi, _mid, 2 * np.pi - _hi - _mid)
HALF_TURN = 3.1415925
LN2 = float(np.log(2.0))
LN2_HI = float(np.floor(LN2 * 2.0 ** 14) / 2.0 ** 14)
ROUND = 1.5 * 2.0 ** 23

STREAM = [("kv", 4, 2), ("ev", 40, 1), ("ev_out", 16, 1), ("od", 48, 1), ("od_out", 16, 1), ("w_in", 28, 1),
          ("glu", 1, 4), ("ssm_up", 4, 4), ("attn_up", 8, 2), ("gates", 32, 1), ("w_out", 16, 1), ("peer_q", 16, 1)]
CHUNK0, UNIT0 = {}, {}
_c = _u = 0
for _n, _k, _g in STREAM:
    CHUNK0[_n], UNIT0[_n] = _c, _u
    _c += _k
    _u += _k * _g
NCHUNK = _c
NUNIT = _u
UNITS_THROUGH = []
for _n, _k, _g in STREAM:
    for _i in range(_k):
        UNITS_THROUGH.append(UNIT0[_n] + (_i + 1) * _g)

PRE_GROUPS = 2
ADA = ["gate0", "shift1", "scale1", "gate1", "shift2", "scale2", "gate2", "shift3", "scale3", "gate3"]
COND = {"gate0": 0, "shift1": 0, "scale1": 0, "gate1": 0}
NADA = 16 * (PRE_GROUPS + len(ADA))
MOD = {"shift0": 0, "scale0": 1, "shift0c": 2, "scale0c": 3}
MOD.update({n: 4 + i for i, n in enumerate(ADA)})

CONST = {}
_at = 0
for _n, _w in (("ident", 128), ("ones", 128), ("rot", 128), ("cos", TOK), ("sin", TOK), ("mask", 2 * TOK),
               ("gmask", 32), ("iota", 16)):
    CONST[_n] = (_at, _w)
    _at += _w
NCONST = _at
VEC = {}
_at = 0
for _n, _w in (("cond", 48), ("ada_b", 192), ("norm_g0", 16), ("norm_g1", 16), ("final_g", 16), ("norm1_w", 16),
               ("norm2_w", 16), ("q_norm", 1), ("k_norm", 1), ("q_norm_2", 1), ("k_norm_2", 1),
               ("dw_w", CONV_T * CONV_W), ("dw_b", 8), ("ln_g", 8), ("ln_b", 8), ("od_g", 16), ("od_b", 16),
               ("A_re", 16), ("A_im", 16), ("log_dt", 16), ("ssm_D", 4), ("b_glu", 4), ("b_forget", 1),
               ("B_re", 256), ("B_im", 256), ("C_re", 256), ("C_im", 256), ("w_f", 128)):
    VEC[_n] = (_at, _w)
    _at += _w
NVEC = _at


def constants():
    t = np.zeros((P, NCONST), np.float32)

    def put(name, a):
        a0, w = CONST[name]
        t[:, a0:a0 + w] = a

    put("ident", np.eye(P))
    put("ones", 1.0)
    rot = np.zeros((P, P))
    for i in range(HD // 2):
        rot[2 * i + 1, 2 * i] = -1.0
        rot[2 * i, 2 * i + 1] = 1.0
    put("rot", rot)
    f = np.float32
    pos = np.arange(TOK)
    inv = np.power(f(10000.0), np.arange(32, dtype=f) * f(-2.0 / 64)).astype(f)
    ang = np.concatenate([(pos // 64).astype(f)[:, None] * inv, (pos % 64).astype(f)[:, None] * inv], 1)
    ang = np.repeat(ang, 2, axis=1).T
    put("cos", np.cos(ang))
    put("sin", np.sin(ang))
    qpos = np.arange(2)[None, :, None] * P + np.arange(P)[:, None, None]
    put("mask", np.where(np.arange(TOK)[None, None, :] <= qpos, 0.0, NEG).reshape(P, -1))
    g = np.zeros((P, 4, 8))
    for p in range(P):
        for j in range(4):
            g[p, j, 2 * j + p // 64] = 1.0
    put("gmask", g.reshape(P, 32))
    put("iota", np.arange(16.0)[None, :])
    return t


def build(nc, xT, ctxT, consts, vecs, weights, ada, keysT, wsT, bs, g3_bias, peer_u, peer_v, out):
    with ExitStack() as ctx:
        def sb(name, shape, dt=F32):
            return ctx.enter_context(nc.sbuf_tensor(name, shape, dt))

        def sem(name):
            return ctx.enter_context(nc.semaphore(name))

        x = sb("x", [P, DT, TOK])
        h = sb("h", [P, DT, TOK])
        ring = sb("ring", [P, SLOTS, CHUNK])
        aring = sb("aring", [P, SLOTS, CHUNK])
        proj = sb("proj", [P, 48, TOK])
        acc = sb("acc", [P, 2, CHUNK])
        sq = sb("sq", [P, DT * TOK])
        att = sb("att", [P, CONV_T * PADW])
        cst = sb("cst", [P, NCONST])
        vec = sb("vec", [P, NVEC])
        mods = sb("mods", [P, 14 * 16])
        gs = sb("gs", [P, 16])
        cond = sb("cond", [P, 48])
        rstd = sb("rstd", [P, TOK])
        small = sb("small", [P, 192])
        powers = sb("powers", [P, 8, 2, 16])
        idx = sb("idx", [P, SLOTS], U32)
        dots = sb("dots", [P, 3 * SLOTS])

        M = ctx.enter_context(nc.psum_tensor("M", [P, 2048], F32))
        G = [ctx.enter_context(nc.psum_tensor(f"G{i}", [P, 512], F32)) for i in range(2)]
        B6 = ctx.enter_context(nc.psum_tensor("B6", [P, 512], F32))
        B7 = ctx.enter_context(nc.psum_tensor("B7", [P, 512], F32))
        O = [B6, B7]

        def C(name):
            a, w = CONST[name]
            return cst[:, a:a + w]

        def V(name):
            a, w = VEC[name]
            return vec[:, a:a + w]

        def mod(name):
            return mods[:, 16 * MOD[name]:16 * MOD[name] + 16]

        def flat(ap):
            return ap.rearrange("p a b -> p (a b)")

        def tiles(ap, n):
            return ap.rearrange("p (n t) -> p n t", n=n)

        def over_tiles(ap, n):
            return ap.unsqueeze(1).to_broadcast([P, n, ap.shape[-1]])

        ident, ones = C("ident"), C("ones")
        hc = proj[:, 32:48, :]
        craw = proj[:, 16:32, :]
        kv_keys = sq[:, 0:1024].rearrange("p (g k) -> p g k", g=2)
        kv_vals = sq[:, 1024:2048].rearrange("p (g k) -> p g k", g=2)
        head_sq_at = sq[:, 2048:4096]
        eps = small[:, 8:9]
        cum, ncum = att[0:8, 1024:1280], att[0:8, 1280:1536]
        f_min, f_exp_row = att[0:8, 1536:1792], att[0:8, 1792:2048]
        turn_cos, turn_sin = proj[:, 28:32, :], proj[:, 32:36, :]
        w_re, w_im, tmp4 = proj[:, 36:40, :], proj[:, 40:44, :], proj[:, 44:48, :]
        z_re, z_im = sq[:, 2048:3072], sq[:, 3072:4096]

        consts_in, vecs_in, x_in, ctx_in = sem("consts_in"), sem("vecs_in"), sem("x_in"), sem("ctx_in")
        spatial_in, bs_in, keys_in, g3b_in = sem("spatial_in"), sem("bs_in"), sem("keys_in"), sem("g3b_in")
        w_in = [sem(f"w_in{s}") for s in range(SLOTS)]
        ada_in = [sem(f"ada_in{s}") for s in range(SLOTS)]
        unit_done, unit_evac = sem("unit_done"), sem("unit_evac")
        ada_pe_used, ada_dve_used = sem("ada_pe_used"), sem("ada_dve_used")
        cond_ready, pre_rows, pre_cols = sem("cond_ready"), sem("pre_rows"), sem("pre_cols")
        mod_sums, mod_copied, mods_ready = sem("mod_sums"), sem("mod_copied"), sem("mods_ready")
        dve_step, act_step, pool_step = sem("dve_step"), sem("act_step"), sem("pool_step")
        sum_in, sum_done, std_ready = sem("sum_in"), sem("sum_done"), sem("std_ready")
        h_scaled, h_ready, hc_ready = sem("h_scaled"), sem("h_ready"), sem("hc_ready")
        head_sq, head_sums, head_std = sem("head_sq"), sem("head_sums"), sem("head_std")
        rot_in, rot_done, qk_ready = sem("rot_in"), sem("rot_done"), sem("qk_ready")
        v_turned, v_ready = sem("v_turned"), sem("v_ready")
        s_done, nmax_ready, exp_done, p_ready = sem("s_done"), sem("nmax_ready"), sem("exp_done"), sem("p_ready")
        pt_done, pt_copied, pv_done, o_read = sem("pt_done"), sem("pt_copied"), sem("pv_done"), sem("o_read")
        conv_normed, conv_act, mix_ready = sem("conv_normed"), sem("conv_act"), sem("mix_ready")
        gate_v_ready, vt_done, vt_copied = sem("gate_v_ready"), sem("vt_done"), sem("vt_copied")
        sgu_done, sgu_read, sgu_ready = sem("sgu_done"), sem("sgu_read"), sem("sgu_ready")
        f_done, f_exp_in, f_exp, f_ln_in, f_ln, cum_ready = (sem("f_done"), sem("f_exp_in"), sem("f_exp"),
                                                             sem("f_ln_in"), sem("f_ln"), sem("cum_ready"))
        trig_in, trig_out = sem("trig_in"), sem("trig_out")
        ssm_bc, ssm_bt, ssm_btc = sem("ssm_bc"), sem("ssm_bt"), sem("ssm_btc")
        ssm_bu, ssm_s, ssm_y, ssm_yd, ssm_g = (sem("ssm_bu"), sem("ssm_s"), sem("ssm_y"), sem("ssm_yd"), sem("ssm_g"))
        glu_ready, merged = sem("glu_ready"), sem("merged")
        g3_done, g3_ready = sem("g3_done"), sem("g3_ready")
        sc_done, sc_copied = sem("sc_done"), sem("sc_copied")
        ht_done, ht_copied = sem("ht_done"), sem("ht_copied")
        gexp_in, gexp_out, picks_ready = sem("gexp_in"), sem("gexp_out"), sem("picks_ready")
        u_in = [sem(f"u_in{s}") for s in range(SLOTS)]
        v_in = [sem(f"v_in{s}") for s in range(SLOTS)]
        gathers_begun = sem("gathers_begun")
        idx_set, dot_done, gelu_done, coef_ready, v_added = (sem("idx_set"), sem("dot_done"), sem("gelu_done"),
                                                             sem("coef_ready"), sem("v_added"))
        tile_step, conv_step, x_normed = sem("tile_step"), sem("conv_step"), sem("x_normed")
        out_ready, stored = sem("out_ready"), sem("stored")

        block = ctx.enter_context(nc.Block())

        @block.sync
        def _(sp):
            sp.dma_start(vec[:, :], vecs).then_inc(vecs_in, 16)
            sp.dma_start(flat(x[:, :, :]), xT).then_inc(x_in, 16)
            sp.dma_start(flat(craw), ctxT).then_inc(ctx_in, 16)
            sp.dma_start(cst[:, :], consts).then_inc(consts_in, 16)

            def load(c, slot, units_before):
                if units_before is not None:
                    sp.wait_ge(unit_done, units_before)
                sp.dma_start(ring[:, slot, :], weights[c]).then_inc(w_in[slot], 16)

            def straight(a, b):
                for c in range(a, b):
                    load(c, c % SLOTS, UNITS_THROUGH[c - SLOTS] if c >= SLOTS else None)

            def looped(a, b):
                with sp.Fori(0, (b - a) // SLOTS) as i:
                    for j in range(SLOTS):
                        load(a + j + SLOTS * i, (a + j) % SLOTS, UNITS_THROUGH[a + j - SLOTS] + SLOTS * i)

            glu, gates = CHUNK0["glu"], CHUNK0["gates"]
            straight(0, 8)
            looped(8, glu)
            straight(glu, gates + SLOTS)
            looped(gates + SLOTS, NCHUNK - SLOTS)
            straight(NCHUNK - SLOTS, NCHUNK)
            for tt in range(2):
                sp.wait_ge(out_ready, tt + 1)
                sp.dma_start(out[tt * P:(tt + 1) * P, :], flat(h[:, :, :])[:, tt * D:(tt + 1) * D]).then_inc(stored, 16)
            sp.wait_ge(stored, 32)

        @block.gpsimd
        def _(pool):
            def load(a, slot):
                pool.dma_start(aring[:, slot, :], ada[a]).then_inc(ada_in[slot], 16)

            for a in range(SLOTS):
                load(a, a)
            with pool.Fori(1, 16 * PRE_GROUPS // SLOTS) as i:
                for s in range(SLOTS):
                    pool.wait_ge(ada_pe_used, SLOTS * i + s - SLOTS + 1)
                    load(SLOTS * i + s, s)
            for s in range(SLOTS):
                pool.wait_ge(ada_pe_used, 16 * PRE_GROUPS - SLOTS + s + 1)
                load(16 * PRE_GROUPS + s, s)
            with pool.Fori(1, 16 * len(ADA) // SLOTS) as i:
                for s in range(SLOTS):
                    pool.wait_ge(ada_dve_used, SLOTS * i + s - SLOTS + 1)
                    load(16 * PRE_GROUPS + SLOTS * i + s, s)

            pool.wait_ge(pt_done, 16)
            pool.wait_ge(s_done, 16)
            pool.dma_start(att[:, 0:D], g3_bias.partition_broadcast(P)).then_inc(g3b_in, 16)

            pool.wait_ge(picks_ready, 1)
            pool.wait_ge(unit_done, NUNIT)
            pool.wait_ge(ada_dve_used, 16 * len(ADA))
            picks = flat(proj[:, 38:39, :]).bitcast(U32)

            def gather(n, s, before):
                if before is not None:
                    pool.wait_ge(dot_done, before)
                    pool.wait_ge(v_added, before)
                nc.gpsimd.tensor_copy(idx[:, s:s + 1], picks[:, bass.ds(n, 1)]).then_inc(idx_set, 1)
                pool.wait_ge(idx_set, n + 1)
                pool.sem_inc(gathers_begun, 1)
                where = bass.IndirectOffsetOnAxis(idx[:, s:s + 1], 0)
                pool.indirect_dma_start(ring[:, s, :], None, peer_u, where).then_inc(u_in[s], 16)
                pool.indirect_dma_start(aring[:, s, :], None, peer_v, where).then_inc(v_in[s], 16)

            for s in range(SLOTS):
                gather(s, s, None)
            with pool.Fori(1, NSLOT // SLOTS) as i:
                for s in range(SLOTS):
                    gather(SLOTS * i + s, s, SLOTS * i + s - SLOTS + 1)
            pool.wait_ge(picks_ready, 2)
            with pool.Fori(NSLOT // SLOTS, 2 * NSLOT // SLOTS) as i:
                for s in range(SLOTS):
                    gather(SLOTS * i + s, s, SLOTS * i + s - SLOTS + 1)

        @block.tensor
        def _(pe):
            unit_bank = lambda u: G[u % 2]

            def unit(slot, weights_at, k, rhs, u, bank, fresh=None):
                for t in range(k):
                    if fresh is not None:
                        pe.wait_ge(h_ready, 16 * fresh + t + 1)
                    mm = nc.tensor.matmul(bank[:, 0:TOK], lhsT=ring[:, slot, weights_at + t * P:weights_at + (t + 1) * P],
                                          rhs=rhs[:, t, :], start=(t == 0), stop=(t == k - 1))
                mm.then_inc(unit_done, 1)

            def dense(name, rhss, k=DT, first=0, count=None, fresh=None):
                per = len(rhss)
                n = dict((a, b) for a, b, _ in STREAM)[name]
                count = n if count is None else count
                c0, u0 = CHUNK0[name] + first, UNIT0[name] + first * per

                def chunk(j, i):
                    c = c0 + j
                    pe.wait_ge(w_in[c % SLOTS], 16 * (c // SLOTS + 1) + 16 * i)
                    for e in range(per):
                        u = u0 + j * per + e
                        if u >= 2:
                            pe.wait_ge(unit_evac, u - 1 + i * SLOTS * per)
                        if name == "kv" and j == 0 and e == 1:
                            pe.wait_ge(hc_ready, 1)
                        unit(c % SLOTS, e * k * P if per * k == DT else 0, k, rhss[e], u, unit_bank(u),
                             fresh if j == 0 and e == 0 else None)

                whole = count // SLOTS
                if whole >= 2 and u0 >= 2 and (SLOTS * per) % 2 == 0:
                    with pe.Fori(0, whole) as i:
                        for j in range(SLOTS):
                            chunk(j, i)
                    for j in range(whole * SLOTS, count):
                        chunk(j, 0)
                else:
                    for j in range(count):
                        chunk(j, 0)

            sums = [0]

            def feature_sum(src, n, at_a_time=None, bank=B7):
                for t in range(n):
                    if t % (at_a_time or n) == 0:
                        sums[0] += 1
                        pe.wait_ge(sum_in, sums[0])
                    mm = nc.tensor.matmul(bank[:, 0:TOK], lhsT=ones, rhs=src[:, t * TOK:(t + 1) * TOK],
                                          start=(t == 0), stop=(t == n - 1))
                mm.then_inc(sum_done, 1)

            heads_n = [0]

            def head_sum(n):
                heads_n[0] += 1
                pe.wait_ge(head_sq, heads_n[0])
                for j in range(n // 2):
                    mm = nc.tensor.matmul(M[:, j * 512:(j + 1) * 512], lhsT=ones, rhs=head_sq_at[:, j * 512:(j + 1) * 512],
                                          start=True, stop=True)
                mm.then_inc(head_sums, 1)

            rots = [0]

            def rotate(srcs):
                rots[0] += 1
                pe.wait_ge(rot_in, rots[0])
                for j, s in enumerate(srcs):
                    w = s.shape[-1]
                    mm = nc.tensor.matmul(M[:, j * w:(j + 1) * w], lhsT=C("rot"), rhs=s, start=True, stop=True)
                mm.then_inc(rot_done, 1)

            def mod_sum(g, units):
                pe.wait_ge(ada_dve_used, 16 * (g + 1))
                pe.wait_ge(unit_evac, units)
                for m in range(DT):
                    mm = nc.tensor.matmul(G[0][:, m:m + 1], lhsT=acc[:, g % 2, m * P:(m + 1) * P],
                                          rhs=ones[:, 0:1], start=True, stop=True)
                mm.then_inc(mod_sums, 1)
                pe.wait_ge(mod_copied, g + 1)

            def attention(base, nk, q_of, k_of, v_of, pt, extra, between={}):
                w = nk * P

                def scores(hh):
                    if hh > 0:
                        pe.wait_ge(exp_done, 2 * (base + hh))
                    for qt in range(2):
                        o = M[:, qt * w:(qt + 1) * w]
                        mm = nc.tensor.matmul(o, lhsT=q_of(hh)[:, qt * P:(qt + 1) * P], rhs=k_of(hh),
                                              start=True, stop=not extra)
                        if extra:
                            nc.tensor.matmul(o, lhsT=cum[:, qt * P:(qt + 1) * P], rhs=pick_rows(hh),
                                             start=False, stop=False)
                            mm = nc.tensor.matmul(o, lhsT=pick_rows(hh)[:, 0:P], rhs=ncum, start=False, stop=True)
                    mm.then_inc(s_done, 1)

                scores(0)
                for hh in range(HEADS):
                    if hh + 1 < HEADS:
                        scores(hh + 1)
                    pe.wait_ge(p_ready, base + hh + 1)
                    if base + hh > 0:
                        pe.wait_ge(pt_copied, base + hh)
                    for kt in range(nk):
                        for qt in range(2):
                            mm = nc.tensor.transpose(M[:, 1024 + kt * 256 + qt * P:1024 + kt * 256 + (qt + 1) * P],
                                                     att[:, qt * w + kt * P:qt * w + (kt + 1) * P], ident)
                    mm.then_inc(pt_done, 1)
                    pe.wait_ge(pt_copied, base + hh + 1)
                    if base + hh >= 2:
                        pe.wait_ge(o_read, base + hh - 1)
                    for kt in range(nk):
                        mm = nc.tensor.matmul(O[hh % 2][:, 0:TOK], lhsT=v_of(hh, kt),
                                              rhs=pt[:, kt * 256:(kt + 1) * 256], start=(kt == 0), stop=(kt == nk - 1))
                    mm.then_inc(pv_done, 1)
                    if hh in between:
                        between[hh]()

            pe.wait_ge(cond_ready, 1)
            cond_v = cond[:, :].rearrange("p (v t) -> p v t", v=3)
            for g in range(PRE_GROUPS):
                if g > 0:
                    pe.wait_ge(pre_rows, g)
                for t in range(DT):
                    pe.wait_ge(ada_in[t % SLOTS], 16 * (4 * g + t // SLOTS + 1))
                    for nb in range(4):
                        mm = nc.tensor.matmul(M[0:2, nb * 512:(nb + 1) * 512], lhsT=cond_v[:, 0:2, t],
                                              rhs=aring[:, t % SLOTS, nb * 512:(nb + 1) * 512],
                                              start=(t == 0), stop=(t == DT - 1))
                    mm.then_inc(ada_pe_used, 1)
                if g == 0:
                    pe.wait_ge(consts_in, 16)
                    feature_sum(sq, DT)
                    feature_sum(sq, DT)
                pe.wait_ge(pre_rows, g + 1)
                for m in range(DT):
                    mm = nc.tensor.matmul(B6[:, g * 32 + 2 * m:g * 32 + 2 * m + 2], lhsT=acc[0:2, g, m * P:(m + 1) * P],
                                          rhs=ident[0:2, 0:2], start=True, stop=True)
                mm.then_inc(pre_cols, 1)

            dense("kv", [h, hc], fresh=0)
            dense("ev", [h], first=0, count=8)
            head_sum(4)
            dense("ev", [h], first=8, count=8)
            rotate([kv_keys[:, g, 0:TOK] for g in range(2)])
            dense("ev", [h], first=16, count=8)
            head_sum(8)
            dense("ev", [h], first=24, count=8)
            rotate([flat(proj[:, 0:8, :])[:, j * 512:(j + 1) * 512] for j in range(4)])
            mod_sum(0, UNIT0["ev"] + 32)
            dense("ev", [h], first=32, count=8)
            mod_sum(1, UNIT0["ev_out"])
            pe.wait_ge(qk_ready, 1)
            for g in range(KV):
                for kt in range(4):
                    mm = nc.tensor.transpose(M[:, 1024 + kt * 256 + g * P:1024 + kt * 256 + (g + 1) * P],
                                             kv_vals[:, g, kt * P:(kt + 1) * P], ident)
            mm.then_inc(v_turned, 1)
            pe.wait_ge(v_ready, 1)
            vtok = sq[:, 3072:4096]
            attention(0, 4, lambda hh: proj[:, hh, :], lambda hh: kv_keys[:, hh // 4, :],
                      lambda hh, kt: vtok[:, kt * 256 + (hh // 4) * P:kt * 256 + (hh // 4 + 1) * P],
                      sq[:, 2048:3072], False,
                      {1: lambda: feature_sum(flat(proj[:, 8:16, :]), CONV_T, bank=G[1]),
                       4: lambda: feature_sum(flat(proj[:, 16:24, :]), CONV_T, bank=G[1])})
            pe.wait_ge(mix_ready, 1)
            dense("ev_out", [proj])
            mod_sum(2, UNIT0["od"])

            feature_sum(sq, DT, 4)
            dense("od", [h], first=0, count=4, fresh=1)
            dense("od", [h], first=4, count=12)
            pe.wait_ge(unit_evac, UNIT0["od"] + 16)
            for t in range(DT):
                mm = nc.tensor.matmul(B7[:, 0:TOK], lhsT=ones, rhs=proj[:, t, :], start=(t == 0), stop=(t == DT - 1))
            mm.then_inc(sum_done, 1)
            mod_sum(3, UNIT0["od"] + 16)
            dense("od", [h], first=16, count=16)
            feature_sum(sq, DT)
            mod_sum(4, UNIT0["od"] + 32)
            dense("od", [h], first=32, count=16)
            pe.wait_ge(gate_v_ready, 1)
            for b in range(4):
                half = (b % 2) * 1024
                if b >= 2:
                    pe.wait_ge(vt_copied, b - 1)
                for j in range(8):
                    n, c = (b % 2) * 8 + j, b // 2
                    mm = nc.tensor.transpose(M[:, half + j * P:half + (j + 1) * P], proj[:, n, c * P:(c + 1) * P], ident)
                mm.then_inc(vt_done, 1)
            pe.wait_ge(spatial_in, 16)
            for b in range(4):
                half = (b % 2) * 1024
                pe.wait_ge(vt_copied, 4 if b < 2 else 4)
                if b >= 2:
                    pe.wait_ge(sgu_read, b - 1)
                for j in range(4):
                    n = 4 * b + j
                    for c in range(2):
                        mm = nc.tensor.matmul(M[:, half + j * TOK + c * P:half + j * TOK + (c + 1) * P],
                                              lhsT=sq[:, c * D + n * P:c * D + (n + 1) * P],
                                              rhs=att[:, (n // 2) * P:(n // 2 + 1) * P], start=True, stop=True)
                mm.then_inc(sgu_done, 1)
            mod_sum(5, UNIT0["od_out"])
            pe.wait_ge(sgu_ready, 1)
            dense("od_out", [proj])
            mod_sum(6, UNIT0["w_in"])

            feature_sum(sq, DT, 4)
            feature_sum(sq, DT, 4)
            dense("w_in", [h], first=0, count=4, fresh=2)
            for t in range(DT):
                mm = nc.tensor.matmul(B7[0:8, 0:TOK], lhsT=V("w_f")[:, t * 8:(t + 1) * 8], rhs=h[:, t, :],
                                      start=(t == 0), stop=(t == DT - 1))
            mm.then_inc(f_done, 1)

            def turn_b(q):
                pe.wait_ge(ssm_bc, q + 1)
                for part in range(2):
                    for j in range(4):
                        o = M[:, 1024 * part + j * P:1024 * part + (j + 1) * P]
                        mm = nc.tensor.transpose(o, att[:, part * 512 + j * P:part * 512 + (j + 1) * P], ident)
                mm.then_inc(ssm_bt, 1)

            def inputs_of_states(q):
                pe.wait_ge(ssm_btc, q + 1)
                for part in range(2):
                    for j in range(4):
                        mm = nc.tensor.matmul(M[:, 1024 * part + j * TOK:1024 * part + (j + 1) * TOK],
                                              lhsT=sq[:, part * 512 + j * P:part * 512 + (j + 1) * P],
                                              rhs=proj[:, q, :], start=True, stop=True)
                mm.then_inc(ssm_bu, 1)

            def outputs_of_states(q):
                pe.wait_ge(ssm_s, q + 1)
                for part in range(2):
                    for j in range(4):
                        mm = nc.tensor.matmul(B6[:, 0:TOK], lhsT=sq[:, 1024 + part * 512 + j * P:1024 + part * 512 + (j + 1) * P],
                                              rhs=ssm_w[part][:, j * TOK:(j + 1) * TOK],
                                              start=(part == 0 and j == 0), stop=(part == 1 and j == 3))
                mm.then_inc(ssm_y, 1)

            ssm_w = [flat(w_re), flat(w_im)]
            turn_b(0)
            dense("w_in", [h], first=4, count=4)
            inputs_of_states(0)
            dense("w_in", [h], first=8, count=4)
            for q in range(1, 4):
                outputs_of_states(q - 1)
                turn_b(q)
                inputs_of_states(q)
                dense("w_in", [h], first=8 + 4 * q, count=4)
            outputs_of_states(3)
            dense("w_in", [h], first=24, count=4)
            head_sum(8)
            head_sum(8)
            pe.wait_ge(ssm_g, 4)
            dense("glu", [proj, proj, proj, proj], k=4)
            pe.wait_ge(qk_ready, 2)
            for hh in range(HEADS):
                for kt in range(2):
                    mm = nc.tensor.transpose(M[:, kt * 1024 + hh * P:kt * 1024 + (hh + 1) * P],
                                             proj[:, 20 + hh, kt * P:(kt + 1) * P], ident)
            mm.then_inc(v_turned, 1)
            pe.wait_ge(v_ready, 2)
            pe.wait_ge(cum_ready, 1)
            vtok2 = flat(proj[:, 36:44, :])

            def pick_rows(hh):
                return ident[0:8, hh:hh + 1].to_broadcast([8, TOK])

            attention(8, 2, lambda hh: proj[:, 12 + hh, :], lambda hh: proj[:, 4 + hh, :],
                      lambda hh, kt: vtok2[:, kt * 1024 + hh * P:kt * 1024 + (hh + 1) * P], sq[:, 2048:2560], True)
            pe.wait_ge(glu_ready, 1)
            dense("ssm_up", [proj, proj, proj, proj], k=4)
            pe.wait_ge(o_read, 16)
            dense("attn_up", [proj[:, 12:20, :], proj[:, 12:20, :]], k=8)
            dense("gates", [h], count=16)
            mod_sum(7, UNIT0["gates"] + 16)
            dense("gates", [h], first=16, count=16)
            mod_sum(8, UNIT0["w_out"])
            pe.wait_ge(merged, 1)
            dense("w_out", [proj[:, 32:48, :]])
            pe.wait_ge(ada_dve_used, 16 * len(ADA))
            for nb in range(4):
                mm = nc.tensor.matmul(M[:, nb * 512:(nb + 1) * 512], lhsT=ones, rhs=acc[:, 1, nb * 512:(nb + 1) * 512],
                                      start=True, stop=True)
            mm.then_inc(g3_done, 1)
            feature_sum(sq, DT, 4)

            def turn_to_tokens(src, first):
                for b in range(4):
                    half = (b % 2) * 1024
                    if first + b >= 2:
                        pe.wait_ge(ht_copied, first + b - 1)
                    for j in range(8):
                        n, c = (b % 2) * 8 + j, b // 2
                        mm = nc.tensor.transpose(M[:, half + j * P:half + (j + 1) * P], src[:, n, c * P:(c + 1) * P], ident)
                    mm.then_inc(ht_done, 1)

            keys = flat(proj[:, 40:48, :])

            def key_scores(r):
                if r == 0:
                    pe.wait_ge(keys_in, 16)
                pe.wait_ge(unit_evac, UNIT0["peer_q"] + r + 1)
                if r >= 2:
                    pe.wait_ge(sc_copied, r - 1)
                for half in range(2):
                    mm = nc.tensor.matmul(O[r % 2][:, half * P:(half + 1) * P], lhsT=proj[:, r, half * P:(half + 1) * P],
                                          rhs=keys[:, r * P:(r + 1) * P], start=True, stop=True)
                mm.then_inc(sc_done, 1)

            dense("peer_q", [h], count=1, fresh=3)
            for r in range(1, 16):
                dense("peer_q", [h], first=r, count=1)
                key_scores(r - 1)
            key_scores(15)
            pe.wait_ge(g3_ready, 1)
            turn_to_tokens(h, 0)
            turn_to_tokens(x, 4)

        @block.scalar
        def _(act):
            def leave(u, dst, func, i=0, per=0, scale=1.0, bias=0.0):
                act.wait_ge(unit_done, u + 1 + i)
                nc.scalar.activation(dst, G[u % 2][:, 0:TOK], func, bias=bias, scale=scale).then_inc(unit_evac, 1)

            def leave_many(u0, tile0, n, func):
                if n >= 8:
                    with act.Fori(0, n // 4) as i:
                        for j in range(4):
                            leave(u0 + j, flat(proj[:, :, :])[:, bass.ds((tile0 + j) * TOK + i * (4 * TOK), TOK)], func, i=4 * i)
                else:
                    for j in range(n):
                        leave(u0 + j, proj[:, tile0 + j, :], func)

            def leave_gated(u0, gate):
                for n in range(DT):
                    leave(u0 + n, h[:, n, :], ACT.Identity, scale=gate[:, n:n + 1])

            def mod_out(g):
                act.wait_ge(mod_sums, g + 1)
                nc.scalar.activation(mods[:, 16 * (4 + g):16 * (5 + g)], G[0][:, 0:16], ACT.Copy).then_inc(mod_copied, 1)

            sums = [0]

            def std(n, count=1, bank=B7):
                sums[0] += count
                act.wait_ge(sum_done, sums[0])
                nc.scalar.activation(rstd[:, :], bank[:, 0:TOK], ACT.Sqrt, bias=eps, scale=1.0 / n).then_inc(std_ready, 1)

            def modulate(nth, shift):
                for t in range(DT):
                    act.wait_ge(h_scaled, 4 * nth + t // 4 + 1)
                    nc.scalar.activation(h[:, t, :], h[:, t, :], ACT.Identity, bias=shift[:, t:t + 1],
                                         scale=gs[:, t:t + 1]).then_inc(h_ready, 1)

            hn = [0]

            def head_stds(n):
                hn[0] += 1
                act.wait_ge(head_sums, hn[0])
                nc.scalar.activation(head_sq_at[:, 0:n * TOK], M[:, 0:n * TOK], ACT.Sqrt, bias=eps, scale=1.0 / HD).then_inc(head_std, 1)

            def softmax_steps(base, nk, pt, scale, between={}):
                w = nk * P

                def exps(hh):
                    act.wait_ge(nmax_ready, base + hh + 1)
                    if base == 0 and hh > 0:
                        act.wait_ge(pt_done, base + hh)
                    for qt in range(2):
                        src = M[:, qt * w:(qt + 1) * w] if nk == 4 else att[:, qt * w:(qt + 1) * w]
                        nc.scalar.activation(att[:, qt * w:(qt + 1) * w], src, ACT.Exp, bias=small[:, 2 + qt:3 + qt],
                                                 scale=scale, accum_out=small[:, 4 + qt:5 + qt]).then_inc(exp_done, 1)

                exps(0)
                for hh in range(HEADS):
                    act.wait_ge(pt_done, base + hh + 1)
                    if hh > 0:
                        act.wait_ge(pv_done, base + hh)
                    nc.scalar.activation(pt, M[:, 1024:1024 + nk * 256], ACT.Copy).then_inc(pt_copied, 1)
                    if hh + 1 < HEADS:
                        exps(hh + 1)
                    if hh in between:
                        between[hh]()

            act.wait_ge(vecs_in, 16)
            act.wait_ge(dve_step, 1)
            nc.scalar.activation(cond[:, :], V("cond"), ACT.Silu).then_inc(cond_ready, 1)
            act.wait_ge(trig_in, 1)
            nc.scalar.activation(small[:, 64:96], small[:, 64:96], ACT.Sin).then_inc(trig_out, 1)
            for g in range(PRE_GROUPS):
                act.wait_ge(ada_pe_used, 16 * (g + 1))
                nc.scalar.activation(acc[0:2, g, :], M[0:2, :], ACT.Copy).then_inc(pre_rows, 1)
                if g == 0:
                    std(D)
                    std(D)
            modulate(0, mod("shift0"))
            for t in range(4):
                dst = (kv_keys if t < 2 else kv_vals)[:, t % 2, :]
                leave(2 * t, dst[:, 0:TOK], ACT.Copy)
                leave(2 * t + 1, dst[:, TOK:2 * TOK], ACT.Copy)
            u = UNIT0["ev"]
            leave_many(u, 0, 8, ACT.Copy)
            head_stds(4)
            leave_many(u + 8, 8, 8, ACT.Copy)
            leave_many(u + 16, 16, 8, ACT.Sigmoid)
            head_stds(8)
            leave_many(u + 24, 24, 8, ACT.Silu)
            mod_out(0)
            leave_many(u + 32, 32, 8, ACT.Silu)
            mod_out(1)
            act.wait_ge(v_turned, 1)
            nc.scalar.activation(sq[:, 3072:4096], M[:, 1024:2048], ACT.Copy).then_inc(v_ready, 1)

            def conv_silu():
                act.wait_ge(conv_normed, 1)
                for t in range(CONV_T):
                    nc.scalar.activation(proj[:, 8 + t, :], proj[:, 8 + t, :], ACT.Silu, bias=V("ln_b")[:, t:t + 1],
                                         scale=V("ln_g")[:, t:t + 1]).then_inc(conv_act, 1)

            softmax_steps(0, 4, sq[:, 2048:3072], HD ** -0.5,
                          {4: lambda: std(CONV_T * P, count=2, bank=G[1]), 7: conv_silu})
            act.dma_start(att[:, 0:1024], wsT).then_inc(spatial_in, 16)
            act.dma_start(att[:, 1024:2048], bs.partition_broadcast(P)).then_inc(bs_in, 16)
            act.wait_ge(mods_ready, 1)
            leave_gated(UNIT0["ev_out"], mod("gate0"))
            mod_out(2)
            std(D)
            modulate(1, mod("shift1"))
            u = UNIT0["od"]
            leave_many(u, 0, 16, ACT.Gelu_apprx_tanh)
            mod_out(3)
            leave_many(u + 16, 16, 16, ACT.Gelu_apprx_tanh)
            std(D, count=2)
            mod_out(4)
            leave_many(u + 32, 32, 16, ACT.Silu)
            for b in range(4):
                act.wait_ge(vt_done, b + 1)
                half = (b % 2) * 1024
                nc.scalar.activation(sq[:, (b // 2) * D + (b % 2) * 1024:(b // 2) * D + (b % 2) * 1024 + 1024],
                                     M[:, half:half + 1024], ACT.Copy).then_inc(vt_copied, 1)
            mod_out(5)
            act.wait_ge(mods_ready, 4)
            leave_gated(UNIT0["od_out"], mod("gate1"))
            mod_out(6)
            std(D)
            std(D)
            modulate(2, mod("shift2"))
            u = UNIT0["w_in"]
            leave_many(u, 0, 4, ACT.Copy)
            act.wait_ge(f_exp_in, 1)
            nc.scalar.activation(f_exp_row, f_exp_row, ACT.Exp).then_inc(f_exp, 1)
            act.wait_ge(f_ln_in, 1)
            nc.scalar.activation(f_exp_row, f_exp_row, ACT.Ln).then_inc(f_ln, 1)

            def copy_b(q):
                act.wait_ge(ssm_bt, q + 1)
                nc.scalar.activation(sq[:, 0:1024].rearrange("p (a b) -> p a b", a=2),
                                     M[:, :].rearrange("p (a b) -> p a b", a=2)[:, :, 0:512], ACT.Copy).then_inc(ssm_btc, 1)

            def gelu_y(q):
                act.wait_ge(ssm_yd, q + 1)
                nc.scalar.activation(proj[:, q, :], proj[:, q, :], ACT.Gelu).then_inc(ssm_g, 1)

            copy_b(0)
            leave_many(u + 4, 4, 4, ACT.Copy)
            leave_many(u + 8, 8, 4, ACT.Copy)
            for q in range(1, 4):
                copy_b(q)
                leave_many(u + 8 + 4 * q, 8 + 4 * q, 4, ACT.Copy)
                gelu_y(q - 1)
            leave_many(u + 24, 24, 4, ACT.Copy)
            gelu_y(3)
            head_stds(8)
            head_stds(8)
            for t in range(4):
                leave(UNIT0["glu"] + t, proj[:, 28 + t, :], ACT.Sigmoid, bias=V("b_glu")[:, t:t + 1])
            act.wait_ge(v_turned, 2)
            nc.scalar.activation(flat(proj[:, 36:44, :]), M[:, :], ACT.Copy).then_inc(v_ready, 1)
            softmax_steps(8, 2, sq[:, 2048:2560], 1.0)
            act.wait_ge(pv_done, 16)
            leave_many(UNIT0["ssm_up"], 32, 16, ACT.Copy)
            for n in range(DT):
                leave(UNIT0["attn_up"] + n, sq[:, n * TOK:(n + 1) * TOK], ACT.Copy)
            act.wait_ge(unit_done, UNIT0["gates"])
            leave_many(UNIT0["gates"], 0, 16, ACT.Sigmoid)
            mod_out(7)
            leave_many(UNIT0["gates"] + 16, 16, 16, ACT.Sigmoid)
            mod_out(8)
            act.wait_ge(mods_ready, 7)
            leave_gated(UNIT0["w_out"], mod("gate2"))
            act.dma_start(flat(proj[:, 40:48, :]), keysT).then_inc(keys_in, 16)
            std(D)
            modulate(3, mod("shift3"))
            scores = proj[:, 16:32, :]

            def keep_scores(r):
                act.wait_ge(sc_done, r + 1)
                nc.scalar.activation(scores[:, r, :], O[r % 2][:, 0:TOK], ACT.Copy).then_inc(sc_copied, 1)

            leave(UNIT0["peer_q"], proj[:, 0, :], ACT.Copy)
            for r in range(1, 16):
                leave(UNIT0["peer_q"] + r, proj[:, r, :], ACT.Copy)
                keep_scores(r - 1)
            keep_scores(15)

            def to_tokens(dst, first):
                for b in range(4):
                    act.wait_ge(ht_done, first + b + 1)
                    half = (b % 2) * 1024
                    nc.scalar.activation(dst[:, (b // 2) * D + half:(b // 2) * D + half + 1024], M[:, half:half + 1024],
                                         ACT.Copy).then_inc(ht_copied, 1)

            to_tokens(sq, 0)
            to_tokens(flat(acc[:, :, :]), 4)
            for tt in range(2):
                act.wait_ge(gexp_in, tt + 1)
                g = flat(proj[:, 39:40, :])[:, tt * P:(tt + 1) * P]
                nc.scalar.activation(g, g, ACT.Exp).then_inc(gexp_out, 1)
            gw = flat(proj[:, 39:40, :])
            act.wait_ge(picks_ready, 2)
            with act.Fori(0, 2 * NSLOT // SLOTS) as i:
                for s in range(SLOTS):
                    act.wait_ge(dot_done, SLOTS * i + s + 1)
                    nc.scalar.activation(dots[:, SLOTS + s:SLOTS + s + 1], dots[:, s:s + 1], ACT.Gelu).then_inc(gelu_done, 1)
                    act.wait_ge(gelu_done, SLOTS * i + s + 1)
                    nc.scalar.activation(dots[:, 2 * SLOTS + s:2 * SLOTS + s + 1], gw[:, bass.ds(SLOTS * i + s, 1)],
                                         ACT.Copy, scale=dots[:, SLOTS + s:SLOTS + s + 1]).then_inc(coef_ready, 1)

        @block.vector
        def _(dve):
            V_ = nc.vector
            counts = {}

            def step(ins, on=None):
                s, key = (dve_step, "step") if on is None else (on, on.name)
                counts[key] = counts.get(key, 0) + 1
                ins.then_inc(s, 1)
                dve.wait_ge(s, counts[key])

            tt = V_.tensor_tensor
            loop_count = [0]

            def affine(buf, n, mul, add=None):
                base = loop_count[0]
                loop_count[0] += n
                with dve.Fori(0, n // 4) as i:
                    for j in range(4):
                        t = buf[:, bass.ds(j * TOK + i * (4 * TOK), TOK)]
                        m = mul[:, bass.ds(4 * i + j, 1)]
                        a = None if add is None else add[:, bass.ds(4 * i + j, 1)]
                        V_.tensor_scalar(t, t, m, a, ALU.mult, *([] if add is None else [ALU.add])).then_inc(tile_step, 1)
                dve.wait_ge(tile_step, base + n)

            sums = {"sum": 0, "std": 0}

            def square_sum(src3, n, dst=None):
                s = flat(src3)
                step(tt(sq[:, 0:n * TOK] if dst is None else dst, s, s, ALU.mult), on=sum_in)

            def root():
                sums["std"] += 1
                dve.wait_ge(std_ready, sums["std"])
                step(V_.reciprocal(rstd[:, :], rstd[:, :]))

            def scaled(dst3, src3, n):
                step(tt(dst3, src3, over_tiles(rstd[:, :], n), ALU.mult))

            def centre(t3, n, nth, bank=B7):
                dve.wait_ge(sum_done, nth)
                step(V_.scalar_tensor_tensor(out=t3, in0=over_tiles(bank[:, 0:TOK], n), scalar=-1.0 / (n * P), in1=t3,
                                             op0=ALU.mult, op1=ALU.add))

            def ada_group(g):
                if g < 2:
                    dve.wait_ge(pre_cols, 2)
                else:
                    dve.wait_ge(mod_sums, g - 1)
                v = 0 if g < 4 else 32
                a = acc[:, g % 2, :]

                def chunk(k, i):
                    s = k % SLOTS
                    dve.wait_ge(ada_in[s], 16 * (4 * (PRE_GROUPS + g) + 1 + i))
                    c = cond[:, bass.ds(v + s + SLOTS * i, 1)]
                    if k == 0 and isinstance(i, int):
                        V_.tensor_scalar(a, aring[:, s, :], c, None, ALU.mult).then_inc(ada_dve_used, 1)
                    else:
                        dve.wait_ge(ada_dve_used, 16 * g + s + SLOTS * i)
                        V_.scalar_tensor_tensor(out=a, in0=aring[:, s, :], scalar=c, in1=a, op0=ALU.mult,
                                                op1=ALU.add).then_inc(ada_dve_used, 1)

                for k in range(SLOTS):
                    chunk(k, 0)
                with dve.Fori(1, 16 // SLOTS) as i:
                    for k in range(SLOTS):
                        chunk(k, i)

            def mods_from(g):
                dve.wait_ge(mod_copied, g + 1)
                m = mods[:, 16 * (4 + g):16 * (5 + g)]
                step(tt(m, m, V("ada_b")[:, 16 * (2 + g):16 * (3 + g)], ALU.add), on=mods_ready)

            def norm_weight(dst, norm, scale):
                step(V_.scalar_tensor_tensor(out=dst, in0=scale, scalar=1.0, in1=norm, op0=ALU.add, op1=ALU.mult))

            def head_norm(src, n, weight):
                step(tt(head_sq_at[:, 0:n * TOK], src, src, ALU.mult), on=head_sq)
                counts["head"] = counts.get("head", 0) + 1
                dve.wait_ge(head_std, counts["head"])
                step(V_.reciprocal(head_sq_at[:, 0:n * TOK], head_sq_at[:, 0:n * TOK]))
                return V_.scalar_tensor_tensor(out=src, in0=src, scalar=weight, in1=head_sq_at[:, 0:n * TOK],
                                               op0=ALU.mult, op1=ALU.mult)

            def rope(src3, n, nth):
                dve.wait_ge(rot_done, nth)
                t = tiles(head_sq_at[:, 0:n * TOK], n)
                step(tt(t, tiles(M[:, 0:n * TOK], n), over_tiles(C("sin"), n), ALU.mult))
                step(tt(src3, src3, over_tiles(C("cos"), n), ALU.mult))
                return tt(src3, src3, t, ALU.add)

            def softmax(base, nk, scale, finish, between={}):
                w = nk * P
                probs = att[:, 0:2 * w].rearrange("p (a b) -> p a b", a=2)

                def maxima(hh):
                    dve.wait_ge(s_done, base + hh + 1)
                    s = M[:, 0:2 * w].rearrange("p (a b) -> p a b", a=2)
                    if base:
                        if hh:
                            dve.wait_ge(pt_done, base + hh)
                        step(tt(probs, s, C("mask").rearrange("p (a b) -> p a b", a=2), ALU.add))
                        s = probs
                    step(V_.tensor_reduce(small[:, 0:2], s, AX, ALU.max))
                    step(V_.tensor_scalar(small[:, 2:4], small[:, 0:2], -scale, None, ALU.mult), on=nmax_ready)

                maxima(0)
                for hh in range(HEADS):
                    dve.wait_ge(exp_done, 2 * (base + hh + 1))
                    step(V_.reciprocal(small[:, 6:8], small[:, 4:6]))
                    step(V_.tensor_scalar(probs[:, 0, :], probs[:, 0, :], small[:, 6:7], None, ALU.mult))
                    step(V_.tensor_scalar(probs[:, 1, :], probs[:, 1, :], small[:, 7:8], None, ALU.mult), on=p_ready)
                    if hh + 1 < HEADS:
                        maxima(hh + 1)
                    dve.wait_ge(pv_done, base + hh + 1)
                    finish(hh, O[hh % 2][:, 0:TOK])
                    if hh in between:
                        between[hh]()

            step(V_.memset(eps, EPS))
            dve.wait_ge(vecs_in, 16)
            S = lambda a: small[:, a:a + 16]
            dt, mag, theta, sin_, cos_, k_, t0, t1 = S(16), S(32), S(48), S(64), S(80), S(96), S(112), S(128)
            cr, ci = S(144), S(160)

            def exact_exp(dst, src):
                n, r, p = k_, t0, t1
                step(V_.tensor_scalar(r, src, -87.0, 88.0, ALU.max, ALU.min))
                step(V_.tensor_scalar(n, r, 1.0 / LN2, ROUND, ALU.mult, ALU.add))
                step(V_.tensor_scalar(n, n, ROUND, None, ALU.subtract))
                step(V_.scalar_tensor_tensor(out=r, in0=n, scalar=-LN2_HI, in1=r, op0=ALU.mult, op1=ALU.add))
                step(V_.scalar_tensor_tensor(out=r, in0=n, scalar=-(LN2 - LN2_HI), in1=r, op0=ALU.mult, op1=ALU.add))
                step(V_.tensor_scalar(p, r, 1.0 / 5040, 1.0 / 720, ALU.mult, ALU.add))
                for c in (1.0 / 120, 1.0 / 24, 1.0 / 6, 0.5, 1.0, 1.0):
                    step(tt(p, p, r, ALU.mult))
                    step(V_.tensor_scalar(p, p, c, None, ALU.add))
                step(V_.tensor_scalar(n, n, 127.0, 2.0 ** 23, ALU.add, ALU.mult))
                step(V_.tensor_copy(r.bitcast(U32), n))
                step(tt(p, p, r, ALU.mult))
                step(V_.scalar_tensor_tensor(out=dst, in0=src, scalar=-87.0, in1=p, op0=ALU.is_ge, op1=ALU.mult))

            exact_exp(dt, V("log_dt"))
            step(tt(theta, V("A_re"), dt, ALU.mult))
            exact_exp(mag, theta)
            step(tt(theta, V("A_im"), dt, ALU.mult))
            step(V_.tensor_scalar(k_, theta, 1.0 / (2 * np.pi), ROUND, ALU.mult, ALU.add))
            step(V_.tensor_scalar(k_, k_, ROUND, None, ALU.subtract))
            step(V_.scalar_tensor_tensor(out=t0, in0=k_, scalar=-TURN[0], in1=theta, op0=ALU.mult, op1=ALU.add))
            step(V_.scalar_tensor_tensor(out=t1, in0=k_, scalar=-TURN[1], in1=t0, op0=ALU.mult, op1=ALU.add))
            step(V_.scalar_tensor_tensor(out=t0, in0=k_, scalar=-TURN[2], in1=t1, op0=ALU.mult, op1=ALU.add))
            step(V_.tensor_scalar(sin_, t0, HALF_TURN, -HALF_TURN, ALU.min, ALU.max))
            step(V_.scalar_tensor_tensor(out=t1, in0=sin_, scalar=-1.0, in1=sin_, op0=ALU.mult, op1=ALU.max))
            step(V_.tensor_scalar(cos_, t1, -1.0, float(np.pi / 2), ALU.mult, ALU.add), on=trig_in)
            dve.wait_ge(trig_out, 1)
            step(V_.tensor_copy(powers[:, 0, 0, :], cos_))
            step(V_.tensor_copy(powers[:, 0, 1, :], sin_))
            for k in range(7):
                c, s_ = powers[:, k, 0, :], powers[:, k, 1, :]
                step(tt(t0, c, c, ALU.mult))
                step(tt(t1, s_, s_, ALU.mult))
                step(tt(powers[:, k + 1, 0, :], t0, t1, ALU.subtract))
                step(V_.scalar_tensor_tensor(out=powers[:, k + 1, 1, :], in0=c, scalar=2.0, in1=s_, op0=ALU.mult,
                                             op1=ALU.mult))
            a_re, a_im, den = cos_, sin_, k_
            step(tt(a_re, mag, cos_, ALU.mult))
            step(tt(a_im, mag, sin_, ALU.mult))
            step(V_.tensor_scalar(a_re, a_re, 1.0, None, ALU.subtract))
            step(tt(t0, V("A_re"), V("A_re"), ALU.mult))
            step(tt(t1, V("A_im"), V("A_im"), ALU.mult))
            step(tt(den, t0, t1, ALU.add))
            step(V_.reciprocal(den, den))
            for out_, p_, q_, op in ((cr, (a_re, "A_re"), (a_im, "A_im"), ALU.add),
                                     (ci, (a_im, "A_re"), (a_re, "A_im"), ALU.subtract)):
                step(tt(t0, p_[0], V(p_[1]), ALU.mult))
                step(tt(t1, q_[0], V(q_[1]), ALU.mult))
                step(tt(t0, t0, t1, op))
                step(tt(out_, t0, den, ALU.mult))
            wide = lambda ap: ap.unsqueeze(2).to_broadcast([P, 16, 16])
            square = lambda ap: ap.rearrange("p (a b) -> p a b", a=16)
            b_re, b_im = square(V("B_re")), square(V("B_im"))
            x0, x1, x2 = (square(att[:, 256 * i:256 * (i + 1)]) for i in range(3))
            step(tt(x0, b_re, wide(cr), ALU.mult))
            step(tt(x1, b_im, wide(ci), ALU.mult))
            step(tt(x2, b_re, wide(ci), ALU.mult))
            step(tt(b_re, x0, x1, ALU.subtract))
            step(tt(x0, b_im, wide(cr), ALU.mult))
            step(tt(b_im, x0, x2, ALU.add))
            step(V_.tensor_scalar(V("C_im"), V("C_im"), -1.0, None, ALU.mult))
            step(V_.tensor_scalar(small[:, 9:10], V("q_norm_2"), HD ** -0.5, None, ALU.mult))
            step(V_.memset(att[:, :], 0.0))

            dve.wait_ge(ctx_in, 16)
            square_sum(craw, DT)
            root()
            scaled(hc, craw, DT)
            dve.wait_ge(x_in, 16)
            square_sum(x[:, :, :], DT)
            root()
            scaled(h[:, :, :], x[:, :, :], DT)
            dve.wait_ge(pre_cols, 2)
            for v in range(2):
                step(tt(mods[:, 32 * v:32 * v + 32].rearrange("p (g m) -> p g m", g=2),
                        B6[:, 0:64].rearrange("p (g m v) -> p v g m", g=2, v=2)[:, v],
                        V("ada_b")[:, 0:32].rearrange("p (g m) -> p g m", g=2), ALU.add))
            norm_weight(gs[:, :], V("norm_g0"), mod("scale0"))
            dve.sem_inc(h_scaled, 4)
            norm_weight(S(176), V("norm_g0"), mod("scale0c"))
            affine(flat(hc), DT, S(176), mod("shift0c"))
            dve.sem_inc(hc_ready, 1)

            ada_group(0)
            dve.wait_ge(unit_evac, UNIT0["ev"])
            step(head_norm(sq[:, 0:1024], 4, V("k_norm")), on=rot_in)
            ada_group(1)
            step(rope(kv_keys[:, :, 0:TOK], 2, 1))
            ev = UNIT0["ev"]
            dve.wait_ge(unit_evac, ev + 8)
            step(head_norm(flat(proj[:, 0:8, :]), 8, V("q_norm")), on=rot_in)
            dve.wait_ge(unit_evac, ev + 24)
            padded = tiles(att[:, :], CONV_T)
            step(tt(padded[:, :, CONV_W // 2:CONV_W // 2 + TOK], proj[:, 8:16, :], proj[:, 16:24, :], ALU.mult))
            aflat, pflat = att[:, :], flat(proj[:, :, :])
            with dve.Fori(0, CONV_T // 2) as i:
                for k in range(CONV_W):
                    for e in range(2):
                        o = pflat[:, bass.ds((8 + e) * TOK + i * (2 * TOK), TOK)]
                        src = aflat[:, bass.ds(e * PADW + k + i * (2 * PADW), TOK)]
                        wk = V("dw_w")[:, bass.ds(e * CONV_W + k + i * (2 * CONV_W), 1)]
                        if k == 0:
                            V_.tensor_scalar(o, src, wk, V("dw_b")[:, bass.ds(e + 2 * i, 1)], ALU.mult,
                                             ALU.add).then_inc(conv_step, 1)
                        else:
                            dve.wait_ge(conv_step, 2 * (k - 1) + e + 1 + i * (2 * CONV_W))
                            V_.scalar_tensor_tensor(out=o, in0=src, scalar=wk, in1=o, op0=ALU.mult,
                                                    op1=ALU.add).then_inc(conv_step, 1)
            dve.wait_ge(conv_step, CONV_T * CONV_W)
            step(rope(proj[:, 0:8, :], 8, 2), on=qk_ready)
            mods_from(0)
            mods_from(1)
            dve.wait_ge(unit_evac, ev + 40)

            def gate_attention(hh, o):
                step(tt(proj[:, hh, :], o, proj[:, 24 + hh, :], ALU.mult), on=o_read)

            conv = proj[:, 8:16, :]
            dve.sem_inc(sum_in, 1)
            counts[sum_in.name] += 1

            def conv_centre():
                centre(conv, CONV_T, 3, bank=G[1])
                square_sum(conv, CONV_T, dst=flat(proj[:, 16:24, :]))

            def conv_scale():
                root()
                step(tt(conv, conv, over_tiles(rstd[:, :], CONV_T), ALU.mult), on=conv_normed)

            softmax(0, 4, HD ** -0.5, gate_attention, {2: conv_centre, 5: conv_scale})
            dve.wait_ge(conv_act, CONV_T)
            step(tt(conv, conv, proj[:, 32:40, :], ALU.mult), on=mix_ready)

            def square_four(j):
                step(tt(sq[:, 1024 * j:1024 * (j + 1)], flat(x[:, 4 * j:4 * j + 4, :]), flat(x[:, 4 * j:4 * j + 4, :]),
                        ALU.mult), on=sum_in)

            def add_residual(name):
                for j in range(4):
                    dve.wait_ge(unit_evac, UNIT0[name] + 4 * (j + 1))
                    x4 = flat(x[:, 4 * j:4 * j + 4, :])
                    step(tt(x4, x4, flat(h[:, 4 * j:4 * j + 4, :]), ALU.add))
                    square_four(j)

            def normed_into_h(norm, scale):
                norm_weight(gs[:, :], norm, scale)
                root()
                for j in range(4):
                    four = slice(4 * j, 4 * j + 4)
                    step(tt(h[:, four, :], x[:, four, :], over_tiles(rstd[:, :], 4), ALU.mult), on=h_scaled)

            counts[h_scaled.name] = 4
            ada_group(2)
            add_residual("ev_out")
            mods_from(2)
            normed_into_h(V("norm_g1"), mod("scale1"))

            ada_group(3)
            od = UNIT0["od"]
            v = proj[:, 0:16, :]
            centre(v, DT, 6)
            square_sum(v, DT)
            ada_group(4)
            root()
            scaled(v, v, DT)
            affine(flat(v), DT, V("od_g"), V("od_b"))
            dve.sem_inc(gate_v_ready, 1)
            mods_from(3)
            ada_group(5)
            dve.wait_ge(unit_evac, od + 48)
            uz = flat(proj[:, 16:32, :])
            step(tt(uz, uz, flat(proj[:, 32:48, :]), ALU.mult))
            dve.wait_ge(bs_in, 16)
            for b in range(4):
                dve.wait_ge(sgu_done, b + 1)
                for e in range(2):
                    g = 2 * b + e
                    lo = (b % 2) * 1024 + e * 512
                    step(tt(tiles(flat(proj[:, 2 * g:2 * g + 2, :]), 4), tiles(M[:, lo:lo + 512], 4),
                            over_tiles(att[:, 1024 + g * P:1024 + (g + 1) * P], 4), ALU.add),
                         on=sgu_read if e else None)
                t4 = flat(proj[:, 4 * b:4 * b + 4, :])
                step(tt(t4, t4, uz[:, 1024 * b:1024 * (b + 1)], ALU.mult), on=sgu_ready if b == 3 else None)

            mods_from(4)
            mods_from(5)
            ada_group(6)
            add_residual("od_out")
            root()
            for t in range(DT):
                V_.scalar_tensor_tensor(out=x[:, t, :], in0=x[:, t, :], scalar=V("final_g")[:, t:t + 1], in1=rstd[:, :],
                                        op0=ALU.mult, op1=ALU.mult).then_inc(x_normed, 1)
                if t % 4 == 3:
                    dve.wait_ge(x_normed, t + 1)
                    square_four(t // 4)
            normed_into_h(V("norm1_w"), mod("scale2"))
            mods_from(6)

            gmask = C("gmask").rearrange("p (j g) -> p j g", j=4).unsqueeze(3).to_broadcast([P, 4, 8, 16])

            def expand(dst, name, q, on=None):
                src = square(V(name))[:, 4 * q:4 * q + 4, :].unsqueeze(2).to_broadcast([P, 4, 8, 16])
                step(tt(dst.rearrange("p (j g c) -> p j g c", j=4, g=8), src, gmask, ALU.mult), on=on)

            def expand_b(q):
                expand(att[:, 0:512], "B_re", q)
                expand(att[:, 512:1024], "B_im", q, on=ssm_bc)

            def times(dst, a, b):
                step(tt(dst, a, b, ALU.mult))

            def cross(dst, a, b, c, d, op, on=None):
                times(dst, a, b)
                times(tmp4, c, d)
                step(tt(dst, dst, tmp4, op), on=on)

            expand_b(0)
            dve.wait_ge(f_done, 1)
            z, zmin, ze = cum, f_min, f_exp_row
            step(V_.tensor_scalar(z, B7[0:8, 0:TOK], V("b_forget")[0:8, :], None, ALU.add))
            step(V_.tensor_scalar(zmin, z, 0.0, None, ALU.min))
            step(V_.scalar_tensor_tensor(out=ze, in0=z, scalar=-1.0, in1=z, op0=ALU.mult, op1=ALU.min), on=f_exp_in)
            dve.wait_ge(f_exp, 1)
            step(V_.tensor_scalar(ze, ze, 1.0, None, ALU.add), on=f_ln_in)
            dve.wait_ge(f_ln, 1)
            step(tt(zmin, zmin, ze, ALU.subtract))
            step(V_.tensor_tensor_scan(cum, ones[0:8, 0:1].to_broadcast([8, TOK]), zmin, 0.0, ALU.mult, ALU.add))
            step(V_.tensor_scalar(ncum, cum, -1.0, None, ALU.mult), on=cum_ready)

            def ssm(q):
                expand(sq[:, 1024:1536], "C_re", q)
                expand(sq[:, 1536:2048], "C_im", q)
                step(V_.memset(turn_cos[:, :, 0:1], 1.0))
                step(V_.memset(turn_sin[:, :, 0:1], 0.0))
                for k in range(8):
                    n = 1 << k
                    pc, ps = (powers[:, k, e, 4 * q:4 * q + 4].unsqueeze(2).to_broadcast([P, 4, n]) for e in range(2))
                    lo_c, lo_s = turn_cos[:, :, 0:n], turn_sin[:, :, 0:n]
                    hi_c, hi_s, t = turn_cos[:, :, n:2 * n], turn_sin[:, :, n:2 * n], tmp4[:, :, 0:n]
                    times(hi_c, lo_c, pc)
                    times(t, lo_s, ps)
                    step(tt(hi_c, hi_c, t, ALU.subtract))
                    times(hi_s, lo_c, ps)
                    times(t, lo_s, pc)
                    step(tt(hi_s, hi_s, t, ALU.add))
                dve.wait_ge(ssm_bu, q + 1)
                bu_re, bu_im = tiles(M[:, 0:1024], 4), tiles(M[:, 1024:2048], 4)
                cross(w_re, bu_re, turn_cos, bu_im, turn_sin, ALU.add)
                cross(w_im, bu_im, turn_cos, bu_re, turn_sin, ALU.subtract)
                if q < 3:
                    expand_b(q + 1)
                for j in range(4):
                    decay = mag[:, 4 * q + j:4 * q + j + 1].to_broadcast([P, TOK])
                    for z_, w_ in ((z_re, w_re), (z_im, w_im)):
                        step(V_.tensor_tensor_scan(z_[:, j * TOK:(j + 1) * TOK], decay, w_[:, j, :], 0.0, ALU.mult,
                                                   ALU.add))
                zr, zi = tiles(z_re, 4), tiles(z_im, 4)
                cross(w_re, zr, turn_cos, zi, turn_sin, ALU.subtract)
                cross(w_im, zr, turn_sin, zi, turn_cos, ALU.add, on=ssm_s)
                dve.wait_ge(ssm_y, q + 1)
                step(V_.scalar_tensor_tensor(out=proj[:, q, :], in0=proj[:, q, :], scalar=V("ssm_D")[:, q:q + 1],
                                             in1=B6[:, 0:TOK], op0=ALU.mult, op1=ALU.add), on=ssm_yd)

            for q in range(4):
                ssm(q)

            wi = UNIT0["w_in"]
            dve.wait_ge(unit_evac, wi + 12)
            step(head_norm(flat(proj[:, 4:12, :]), 8, V("k_norm_2")))
            dve.wait_ge(unit_evac, wi + 20)
            step(head_norm(flat(proj[:, 12:20, :]), 8, small[:, 9:10]), on=qk_ready)
            dve.wait_ge(unit_evac, UNIT0["glu"] + 4)
            y4 = flat(proj[:, 0:4, :])
            step(tt(y4, y4, flat(proj[:, 28:32, :]), ALU.mult), on=glu_ready)

            def keep_attention(hh, o):
                step(V_.tensor_copy(proj[:, 12 + hh, :], o), on=o_read)

            softmax(8, 2, 1.0, keep_attention)

            ada_group(7)
            ada_group(8)
            gates = UNIT0["gates"]
            s_branch, a_branch = flat(proj[:, 32:48, :]), sq[:, :]
            dve.wait_ge(unit_evac, gates + 16)
            step(tt(s_branch, s_branch, flat(proj[:, 0:16, :]), ALU.mult))
            ada_group(9)
            dve.wait_ge(unit_evac, gates + 32)
            step(tt(a_branch, a_branch, flat(proj[:, 16:32, :]), ALU.mult))
            step(tt(s_branch, s_branch, a_branch, ALU.add), on=merged)
            mods_from(7)
            mods_from(8)
            add_residual("w_out")
            normed_into_h(V("norm2_w"), mod("scale3"))
            dve.wait_ge(g3_done, 1)
            dve.wait_ge(g3b_in, 16)
            step(tt(att[:, 0:D], att[:, 0:D], M[:, :], ALU.add), on=g3_ready)

            tile = lambda n: flat(proj[:, n:n + 1, :])
            sv = [tile(32 + k).rearrange("p (r k) -> p r k", r=16) for k in range(2)]
            si = [tile(34 + k).bitcast(U32) for k in range(2)]
            tv = tile(36)[:, 0:128].rearrange("p (h k) -> p h k", h=8)
            tp = tile(36)[:, 128:256].bitcast(U32)
            masked = tile(37)
            sif = tile(40).rearrange("p (h s k) -> p h s k", h=8, s=2)
            half_i = tile(41).bitcast(U32)
            half_f = tile(42)
            chosen = tile(43)
            gsum = tile(44)
            cand = flat(proj[:, 0:8, :]).rearrange("p (h a b) -> p h a b", h=8, a=16)
            pick = flat(proj[:, 8:16, :]).rearrange("p (h a b) -> p h a b", h=8, a=16)
            iota = C("iota").unsqueeze(1).unsqueeze(1).to_broadcast([P, 8, 16, 16])

            def top16(values, best, where, width):
                step(V_.max(best[:, 0:8], values))
                step(V_.max_index(where[:, 0:8], best[:, 0:8], values))
                step(V_.match_replace(masked[:, 0:width], best[:, 0:8], values, LOWEST))
                step(V_.max(best[:, 8:16], masked[:, 0:width]))
                step(V_.max_index(where[:, 8:16], best[:, 8:16], masked[:, 0:width]))

            for r in range(16):
                dve.wait_ge(sc_copied, r + 1)
                for tk in range(2):
                    top16(proj[:, 16 + r, tk * P:(tk + 1) * P], sv[tk][:, r, :], si[tk][:, r * SEL:(r + 1) * SEL], P)
            dve.wait_ge(sc_done, 16)
            for tk in range(2):
                step(V_.tensor_copy(tile(40), si[tk]))
                svh = sv[tk].rearrange("p (h s) k -> p h s k", s=2)
                step(tt(cand, svh[:, :, 0, :].unsqueeze(3).to_broadcast([P, 8, 16, 16]),
                        svh[:, :, 1, :].unsqueeze(2).to_broadcast([P, 8, 16, 16]), ALU.add))
                for hh in range(HEADS):
                    top16(flat(proj[:, hh:hh + 1, :]), tv[:, hh, :], tp[:, hh * SEL:(hh + 1) * SEL], 256)
                step(V_.tensor_scalar(half_i[:, 0:128], tp, 4, None, ALU.logical_shift_right))
                step(V_.tensor_scalar(half_i[:, 128:256], tp, 15, None, ALU.bitwise_and))
                step(V_.tensor_copy(half_f, half_i))
                for s in range(2):
                    place = half_f[:, s * 128:(s + 1) * 128].rearrange("p (h k) -> p h k", h=8)
                    step(tt(pick, place.unsqueeze(3).to_broadcast([P, 8, 16, 16]), iota, ALU.is_equal))
                    step(tt(pick, pick, sif[:, :, s, :].unsqueeze(2).to_broadcast([P, 8, 16, 16]), ALU.mult))
                    step(V_.tensor_reduce(chosen[:, s * 128:(s + 1) * 128].rearrange("p (h k) -> p h k", h=8), pick, AX,
                                          ALU.add))
                step(V_.scalar_tensor_tensor(out=chosen[:, 0:128], in0=chosen[:, 0:128], scalar=128.0,
                                             in1=chosen[:, 128:256], op0=ALU.mult, op1=ALU.add))
                step(V_.tensor_copy(tile(38).bitcast(U32)[:, tk * P:(tk + 1) * P], chosen[:, 0:128]))
                gw = tile(39)[:, tk * P:(tk + 1) * P]
                gw3 = gw.rearrange("p (h k) -> p h k", h=8)
                step(tt(gw3, tv, tv[:, :, 0:1].to_broadcast([P, 8, 16]), ALU.subtract), on=gexp_in)
                dve.wait_ge(gexp_out, tk + 1)
                step(V_.tensor_reduce(gsum[:, 0:8], gw3, AX, ALU.add))
                step(V_.reciprocal(gsum[:, 8:16], gsum[:, 0:8]))
                step(tt(gw3, gw3, gsum[:, 8:16].unsqueeze(2).to_broadcast([P, 8, 16]), ALU.mult), on=picks_ready)

            dve.wait_ge(unit_done, NUNIT)
            dve.wait_ge(ht_copied, 8)
            step(V_.memset(flat(h[:, :, :]), 0.0))
            unused = flat(proj[:, 0:8, :])
            for tk in range(2):
                total = flat(h[:, :, :])[:, tk * D:(tk + 1) * D]
                tokens = sq[:, tk * D:(tk + 1) * D]

                def dot(i, s):
                    n = NSLOT * tk + s
                    dve.wait_ge(u_in[s], 16 * (NSLOT // SLOTS * tk + 1) + 16 * i)
                    if not (tk == 0 and s == 0):
                        dve.wait_ge(dot_done, n + SLOTS * i)
                    V_.tensor_tensor_reduce(out=unused, in0=tokens, in1=ring[:, s, :], scale=1.0, scalar=0.0,
                                            op0=ALU.mult, op1=ALU.add, accum_out=dots[:, s:s + 1]).then_inc(dot_done, 1)

                def add(i, s):
                    n = NSLOT * tk + s
                    dve.wait_ge(v_in[s], 16 * (NSLOT // SLOTS * tk + 1) + 16 * i)
                    dve.wait_ge(coef_ready, n + 1 + SLOTS * i)
                    if not (tk == 0 and s == 0):
                        dve.wait_ge(v_added, n + SLOTS * i)
                    V_.scalar_tensor_tensor(out=total, in0=aring[:, s, :], scalar=dots[:, 2 * SLOTS + s:2 * SLOTS + s + 1],
                                            in1=total, op0=ALU.mult, op1=ALU.add).then_inc(v_added, 1)

                with dve.Fori(0, NSLOT // SLOTS) as i:
                    for s in range(SLOTS):
                        dot(i, s)
                        if s > 0:
                            add(i, s - 1)
                    add(i, SLOTS - 1)
                dve.wait_ge(v_added, NSLOT * (tk + 1))
                step(tt(total, total, att[:, 0:D], ALU.mult))
                step(tt(total, total, acc[:, tk, :], ALU.add), on=out_ready)


def kernel(**inputs):
    import concourse.bacc as bacc
    from concourse.bass_utils import run_bass_kernel_spmd as run

    a = {k: np.asarray(v) for k, v in inputs.items()}

    def feature_major(v):
        return v.reshape(-1, P).T

    def tokens_last(m):
        return np.ascontiguousarray(m.T.reshape(-1, P, TOK).transpose(1, 0, 2)).reshape(P, -1)

    def chunks(w):
        k, n = w.shape
        per = D // k
        t = w.reshape(k // P, P, n // (P * per), per, P).transpose(2, 1, 3, 0, 4)
        return t.reshape(n // (P * per), P, CHUNK)

    ev = a["ev_w_in"][0]
    kv, q, za, ga, gb, zb = np.split(ev, [512, 1536, 2560, 3584, 4608], axis=1)
    u_, v_, z_ = np.split(a["od_w_in"][0], 3, axis=1)
    q2, k2, v2, f2, s2, gs2, ga2 = np.split(a["w_in_2"][0], [1024, 2048, 3072, 3080, 3592, 5640], axis=1)
    parts = [kv, q, ga, gb, za, zb, a["ev_w_out"][0], v_, u_, z_, a["od_w_out"][0], s2, k2, q2, v2, a["w_glu_2"][0],
             a["w_ssm_up_2"][0], a["w_attn_up_2"][0], gs2, ga2, a["w_out_2"][0], a["w_peer_q_2"][0]]
    weights = np.concatenate([chunks(w) for w in parts])
    assert len(weights) == NCHUNK

    a0, a1, a2 = a["ada_w"][0], a["ada_w"][1], a["w_ada_2"][0]
    groups = [(a0, 0), (a0, 1), (a0, 2), (a1, 0), (a1, 1), (a1, 2)] + [(a2, i) for i in range(6)]
    ada = np.concatenate([w[:, D * i:D * (i + 1)].reshape(DT, P, D) for w, i in groups])
    biases = np.concatenate([a["ada_b"][0], a["ada_b"][1], a["b_ada_2"][0]])

    vecs = np.zeros((P, NVEC), np.float32)

    def put(name, v):
        at, w = VEC[name]
        vecs[:, at:at + w] = v

    put("cond", np.concatenate([feature_major(a["c"]), feature_major(a["c_ctx"]), feature_major(a["c_2"])], axis=1))
    put("ada_b", feature_major(biases))
    for name, v in (("norm_g0", a["norm_g"][0]), ("norm_g1", a["norm_g"][1]), ("final_g", a["final_g"]),
                    ("norm1_w", a["norm1_w_2"]), ("norm2_w", a["norm2_w_2"]), ("q_norm", a["ev_q_norm"]),
                    ("k_norm", a["ev_k_norm"]), ("q_norm_2", a["q_norm_w_2"]), ("k_norm_2", a["k_norm_w_2"]),
                    ("dw_b", a["ev_dw_b"]), ("ln_g", a["ev_ln_g"]), ("ln_b", a["ev_ln_b"]), ("od_g", a["od_ln_g"]),
                    ("od_b", a["od_ln_b"]), ("A_re", a["ssm_A_re_2"]), ("A_im", a["ssm_A_im_2"]),
                    ("log_dt", np.repeat(a["ssm_log_dt_2"][0], 64)), ("ssm_D", a["ssm_D_2"]), ("b_glu", a["b_glu_2"])):
        put(name, feature_major(v))
    put("dw_w", a["ev_dw_w"][0].reshape(CONV_W, CONV_T, P).transpose(2, 1, 0).reshape(P, -1))
    vecs[0:8, VEC["b_forget"][0]] = a["b_forget_2"][0]
    for name in ("B_re", "B_im"):
        put(name, a[f"ssm_{name}_2"][0].reshape(16, P, 16).transpose(1, 0, 2).reshape(P, -1))
    for name in ("C_re", "C_im"):
        put(name, a[f"ssm_{name}_2"][0].transpose(0, 2, 1).reshape(16, P, 16).transpose(1, 0, 2).reshape(P, -1))
    put("w_f", f2.reshape(DT, P, 8).transpose(1, 0, 2).reshape(P, -1))

    arrays = {
        "xT": tokens_last(a["x"][0]), "ctxT": tokens_last(a["ctx"][0]), "consts": constants(), "vecs": vecs,
        "weights": weights, "ada": ada,
        "keysT": np.ascontiguousarray(a["peer_sub_keys_2"][0].reshape(16, P, P).transpose(2, 0, 1)).reshape(P, -1),
        "wsT": np.ascontiguousarray(a["od_ws"][0].transpose(2, 0, 1)).reshape(P, -1),
        "bs": np.ascontiguousarray(a["od_bs"][0]).reshape(-1),
        "g3_bias": np.ascontiguousarray(a["b_ada_2"][0][5 * D:]),
        "peer_u": np.ascontiguousarray(a["peer_u_2"][0]), "peer_v": np.ascontiguousarray(a["peer_v_2"][0]),
    }
    nc = bacc.Bacc("TRN2", target_bir_lowering=False, num_devices=1)
    args = [nc.dram_tensor(n, v.shape, F32, kind="ExternalInput").ap() for n, v in arrays.items()]
    out = nc.dram_tensor("out", (TOK, D), F32, kind="ExternalOutput").ap()
    build(nc, *args, out)
    r = run(nc, [arrays], core_ids=[0])
    return r.results[0]["out"].reshape(1, TOK, D)
```

```python
from contextlib import ExitStack

import concourse.bass as bass
from concourse import mybir
from concourse.alu_op_type import AluOpType as ALU
import numpy as np

F32 = mybir.dt.float32
U32 = mybir.dt.uint32
ACT = mybir.ActivationFunctionType
AX = mybir.AxisListType.X

P = 128
TOK = 256
D = 2048
DT = D // P
EPS = 1e-6
CHUNK = 2048
SLOTS = 4
HEADS = 8
HD = 128
KV = 2
CONV_T = 8
CONV_W = 31
PADW = TOK + CONV_W - 1
SEL = 16
NSLOT = HEADS * SEL
NEG = -1e30
LOWEST = -3.0e38
_hi = float(np.float32(np.floor(2 * np.pi * 2.0 ** 8) / 2.0 ** 8))
_mid = float(np.floor((2 * np.pi - _hi) * 2.0 ** 20) / 2.0 ** 20)
TURN = (_hi, _mid, 2 * np.pi - _hi - _mid)
HALF_TURN = 3.1415925
LN2 = float(np.log(2.0))
LN2_HI = float(np.floor(LN2 * 2.0 ** 14) / 2.0 ** 14)
ROUND = 1.5 * 2.0 ** 23

STREAM = [("kv", 4, 2), ("ev", 40, 1), ("ev_out", 16, 1), ("od", 48, 1), ("od_out", 16, 1), ("w_in", 28, 1),
          ("glu", 1, 4), ("ssm_up", 4, 4), ("attn_up", 8, 2), ("gates", 32, 1), ("w_out", 16, 1), ("peer_q", 16, 1)]
CHUNK0, UNIT0 = {}, {}
_c = _u = 0
for _n, _k, _g in STREAM:
    CHUNK0[_n], UNIT0[_n] = _c, _u
    _c += _k
    _u += _k * _g
NCHUNK = _c
NUNIT = _u
UNITS_THROUGH = []
for _n, _k, _g in STREAM:
    for _i in range(_k):
        UNITS_THROUGH.append(UNIT0[_n] + (_i + 1) * _g)

PRE_GROUPS = 2
ADA = ["gate0", "shift1", "scale1", "gate1", "shift2", "scale2", "gate2", "shift3", "scale3", "gate3"]
NADA = 16 * (PRE_GROUPS + len(ADA))
MOD = {"shift0": 0, "scale0": 1, "shift0c": 2, "scale0c": 3}
MOD.update({n: 4 + i for i, n in enumerate(ADA)})

CONST = {}
_at = 0
for _n, _w in (("ident", 128), ("ones", 128), ("rot", 128), ("cos", TOK), ("sin", TOK), ("mask", 2 * TOK),
               ("gmask", 32), ("iota", 16), ("head_col", 2 * HEADS - 1)):
    CONST[_n] = (_at, _w)
    _at += _w
NCONST = _at
VEC = {}
_at = 0
for _n, _w in (("ada_b", 192), ("norm_g0", 16), ("norm_g1", 16), ("final_g", 16), ("norm1_w", 16),
               ("norm2_w", 16), ("q_norm", 1), ("k_norm", 1), ("q_norm_2", 1), ("k_norm_2", 1),
               ("dw_w", CONV_T * CONV_W), ("dw_b", 8), ("ln_g", 8), ("ln_b", 8), ("od_g", 16), ("od_b", 16),
               ("A_re", 16), ("A_im", 16), ("log_dt", 16), ("ssm_D", 4), ("b_glu", 4), ("b_forget", 1),
               ("B_re", 256), ("B_im", 256), ("C_re", 256), ("C_im", 256), ("w_f", 128)):
    VEC[_n] = (_at, _w)
    _at += _w
NVEC = _at


def constants():
    t = np.zeros((P, NCONST), np.float32)

    def put(name, a):
        a0, w = CONST[name]
        t[:, a0:a0 + w] = a

    put("ident", np.eye(P))
    put("ones", 1.0)
    rot = np.zeros((P, P))
    for i in range(HD // 2):
        rot[2 * i + 1, 2 * i] = -1.0
        rot[2 * i, 2 * i + 1] = 1.0
    put("rot", rot)
    f = np.float32
    pos = np.arange(TOK)
    inv = np.power(f(10000.0), np.arange(32, dtype=f) * f(-2.0 / 64)).astype(f)
    ang = np.concatenate([(pos // 64).astype(f)[:, None] * inv, (pos % 64).astype(f)[:, None] * inv], 1)
    ang = np.repeat(ang, 2, axis=1).T
    put("cos", np.cos(ang))
    put("sin", np.sin(ang))
    qpos = np.arange(2)[None, :, None] * P + np.arange(P)[:, None, None]
    put("mask", np.where(np.arange(TOK)[None, None, :] <= qpos, 0.0, NEG).reshape(P, -1))
    g = np.zeros((P, 4, 8))
    for p in range(P):
        for j in range(4):
            g[p, j, 2 * j + p // 64] = 1.0
    put("gmask", g.reshape(P, 32))
    put("iota", np.arange(16.0)[None, :])
    put("head_col", np.arange(2 * HEADS - 1)[None, :] == HEADS - 1)
    return t


def build(nc, xT, ctxT, consts, conds, vecs, weights, ada, keysT, wsT, bs, g3_bias, peer_u, peer_v, out):
    with ExitStack() as ctx:
        def sb(name, shape, dt=F32):
            return ctx.enter_context(nc.sbuf_tensor(name, shape, dt))

        def sem(name):
            return ctx.enter_context(nc.semaphore(name))

        x = sb("x", [P, DT, TOK])
        h = sb("h", [P, DT, TOK])
        ring = sb("ring", [P, SLOTS, CHUNK])
        aring = sb("aring", [P, SLOTS, CHUNK])
        proj = sb("proj", [P, 48, TOK])
        acc = sb("acc", [P, 2, CHUNK])
        sq = sb("sq", [P, DT * TOK])
        att = sb("att", [P, CONV_T * PADW])
        cst = sb("cst", [P, NCONST])
        vec = sb("vec", [P, NVEC])
        mods = sb("mods", [P, 14 * 16])
        gs = sb("gs", [P, 16])
        cond = sb("cond", [P, 48])
        rstd = sb("rstd", [P, TOK])
        small = sb("small", [P, 192])
        powers = sb("powers", [P, 8, 2, 16])
        seeds = sb("seeds", [P, 2, 16, 16])
        head_rows = sb("head_rows", [HEADS, 2, TOK])
        idx = sb("idx", [P, SLOTS], U32)
        dots = sb("dots", [P, 3 * SLOTS])

        M = ctx.enter_context(nc.psum_tensor("M", [P, 2048], F32))
        G = [ctx.enter_context(nc.psum_tensor(f"G{i}", [P, 512], F32)) for i in range(2)]
        B6 = ctx.enter_context(nc.psum_tensor("B6", [P, 512], F32))
        B7 = ctx.enter_context(nc.psum_tensor("B7", [P, 512], F32))
        O = [B6, B7]

        def C(name):
            a, w = CONST[name]
            return cst[:, a:a + w]

        def V(name):
            a, w = VEC[name]
            return vec[:, a:a + w]

        def mod(name):
            return mods[:, 16 * MOD[name]:16 * MOD[name] + 16]

        def flat(ap):
            return ap.rearrange("p a b -> p (a b)")

        def tiles(ap, n):
            return ap.rearrange("p (n t) -> p n t", n=n)

        def over_tiles(ap, n):
            return ap.unsqueeze(1).to_broadcast([P, n, ap.shape[-1]])

        ident, ones = C("ident"), C("ones")
        hc = proj[:, 32:48, :]
        craw = proj[:, 16:32, :]
        kv_keys = sq[:, 0:1024].rearrange("p (g k) -> p g k", g=2)
        kv_vals = sq[:, 1024:2048].rearrange("p (g k) -> p g k", g=2)
        head_sq_at = sq[:, 2048:4096]
        eps = small[:, 8:9]
        cum, ncum = att[0:8, 1024:1280], att[0:8, 1280:1536]
        f_min, f_exp_row = att[0:8, 1536:1792], att[0:8, 1792:2048]
        turn_cos, turn_sin = proj[:, 28:32, :], proj[:, 32:36, :]
        w_re, w_im, tmp4 = proj[:, 36:40, :], proj[:, 40:44, :], proj[:, 44:48, :]
        z_re, z_im = sq[:, 2048:3072], sq[:, 3072:4096]

        conds_in = sem("conds_in")
        consts_in, vecs_in, x_in, ctx_in = sem("consts_in"), sem("vecs_in"), sem("x_in"), sem("ctx_in")
        spatial_in, bs_in, keys_in, g3b_in = sem("spatial_in"), sem("bs_in"), sem("keys_in"), sem("g3b_in")
        w_in = [sem(f"w_in{s}") for s in range(SLOTS)]
        ada_in = [sem(f"ada_in{s}") for s in range(SLOTS)]
        unit_done, unit_evac = sem("unit_done"), sem("unit_evac")
        ada_pe_used, ada_dve_used = sem("ada_pe_used"), sem("ada_dve_used")
        cond_ready, pre_rows, pre_cols = sem("cond_ready"), sem("pre_rows"), sem("pre_cols")
        mod_sums, mod_copied, mods_ready = sem("mod_sums"), sem("mod_copied"), sem("mods_ready")
        dve_step = sem("dve_step")
        sum_in, sum_done, std_ready = sem("sum_in"), sem("sum_done"), sem("std_ready")
        h_scaled, h_ready, hc_ready = sem("h_scaled"), sem("h_ready"), sem("hc_ready")
        head_sq, head_sums, head_std = sem("head_sq"), sem("head_sums"), sem("head_std")
        head_inv, head_spread, head_used = sem("head_inv"), sem("head_spread"), sem("head_used")
        rot_in, rot_done, qk_ready = sem("rot_in"), sem("rot_done"), sem("qk_ready")
        v_turned, v_ready = sem("v_turned"), sem("v_ready")
        s_done, nmax_ready, exp_done, p_ready = sem("s_done"), sem("nmax_ready"), sem("exp_done"), sem("p_ready")
        pt_done, pt_copied, pv_done, o_read = sem("pt_done"), sem("pt_copied"), sem("pv_done"), sem("o_read")
        conv_normed, conv_act, mix_ready = sem("conv_normed"), sem("conv_act"), sem("mix_ready")
        gate_v_ready, vt_done, vt_copied = sem("gate_v_ready"), sem("vt_done"), sem("vt_copied")
        sgu_done, sgu_read, sgu_ready = sem("sgu_done"), sem("sgu_read"), sem("sgu_ready")
        f_done, f_exp_in, f_exp, f_ln_in, f_ln, cum_ready = (sem("f_done"), sem("f_exp_in"), sem("f_exp"),
                                                             sem("f_ln_in"), sem("f_ln"), sem("cum_ready"))
        trig_in, trig_out = sem("trig_in"), sem("trig_out")
        ssm_bc, ssm_bt, ssm_btc = sem("ssm_bc"), sem("ssm_bt"), sem("ssm_btc")
        ssm_bu, ssm_s, ssm_y, ssm_yd, ssm_g = (sem("ssm_bu"), sem("ssm_s"), sem("ssm_y"), sem("ssm_yd"), sem("ssm_g"))
        glu_ready, merged = sem("glu_ready"), sem("merged")
        g3_done, g3_ready = sem("g3_done"), sem("g3_ready")
        sc_done, sc_copied = sem("sc_done"), sem("sc_copied")
        ht_done, ht_copied = sem("ht_done"), sem("ht_copied")
        gexp_in, gexp_out, picks_ready = sem("gexp_in"), sem("gexp_out"), sem("picks_ready")
        u_in = [sem(f"u_in{s}") for s in range(SLOTS)]
        v_in = [sem(f"v_in{s}") for s in range(SLOTS)]
        gathers_begun = sem("gathers_begun")
        idx_set, dot_done, gelu_done, coef_ready, v_added = (sem("idx_set"), sem("dot_done"), sem("gelu_done"),
                                                             sem("coef_ready"), sem("v_added"))
        tile_step, conv_step, x_normed = sem("tile_step"), sem("conv_step"), sem("x_normed")
        out_ready, stored = sem("out_ready"), sem("stored")

        block = ctx.enter_context(nc.Block())

        @block.sync
        def _(sp):
            sp.dma_start(cond[:, :], conds).then_inc(conds_in, 16)
            sp.dma_start(vec[:, :], vecs).then_inc(vecs_in, 16)
            sp.wait_ge(ada_pe_used, 1)
            sp.dma_start(flat(x[:, :, :]), xT).then_inc(x_in, 16)
            sp.dma_start(flat(craw), ctxT).then_inc(ctx_in, 16)
            sp.dma_start(cst[:, :], consts).then_inc(consts_in, 16)

            def load(c, slot, units_before):
                if units_before is not None:
                    sp.wait_ge(unit_done, units_before)
                sp.dma_start(ring[:, slot, :], weights[c]).then_inc(w_in[slot], 16)

            def straight(a, b):
                for c in range(a, b):
                    load(c, c % SLOTS, UNITS_THROUGH[c - SLOTS] if c >= SLOTS else None)

            def looped(a, b):
                with sp.Fori(0, (b - a) // SLOTS) as i:
                    for j in range(SLOTS):
                        load(a + j + SLOTS * i, (a + j) % SLOTS, UNITS_THROUGH[a + j - SLOTS] + SLOTS * i)

            glu, gates = CHUNK0["glu"], CHUNK0["gates"]
            sp.wait_ge(ada_pe_used, DT - 2)
            straight(0, 8)
            looped(8, glu)
            straight(glu, gates + SLOTS)
            looped(gates + SLOTS, NCHUNK - SLOTS)
            straight(NCHUNK - SLOTS, NCHUNK)
            for tt in range(2):
                sp.wait_ge(out_ready, tt + 1)
                sp.dma_start(out[tt * P:(tt + 1) * P, :], flat(h[:, :, :])[:, tt * D:(tt + 1) * D]).then_inc(stored, 16)
            sp.wait_ge(stored, 32)

        @block.gpsimd
        def _(pool):
            def load(a, slot):
                pool.dma_start(aring[:, slot, :], ada[a]).then_inc(ada_in[slot], 16)

            for a in range(SLOTS):
                load(a, a)
            with pool.Fori(1, 16 * PRE_GROUPS // SLOTS) as i:
                for s in range(SLOTS):
                    pool.wait_ge(ada_pe_used, SLOTS * i + s - SLOTS + 1)
                    load(SLOTS * i + s, s)
            for s in range(SLOTS):
                pool.wait_ge(ada_pe_used, 16 * PRE_GROUPS - SLOTS + s + 1)
                load(16 * PRE_GROUPS + s, s)
            with pool.Fori(1, 16 * len(ADA) // SLOTS) as i:
                for s in range(SLOTS):
                    pool.wait_ge(ada_dve_used, SLOTS * i + s - SLOTS + 1)
                    load(16 * PRE_GROUPS + SLOTS * i + s, s)

            pool.wait_ge(pt_done, 16)
            pool.wait_ge(s_done, 16)
            pool.dma_start(att[:, 0:D], g3_bias.partition_broadcast(P)).then_inc(g3b_in, 16)

            pool.wait_ge(picks_ready, 1)
            pool.wait_ge(unit_done, NUNIT)
            pool.wait_ge(ada_dve_used, 16 * len(ADA))
            picks = flat(proj[:, 38:39, :]).bitcast(U32)

            def gather(n, s, before):
                if before is not None:
                    pool.wait_ge(dot_done, before)
                    pool.wait_ge(v_added, before)
                nc.gpsimd.tensor_copy(idx[:, s:s + 1], picks[:, bass.ds(n, 1)]).then_inc(idx_set, 1)
                pool.wait_ge(idx_set, n + 1)
                pool.sem_inc(gathers_begun, 1)
                where = bass.IndirectOffsetOnAxis(idx[:, s:s + 1], 0)
                pool.indirect_dma_start(ring[:, s, :], None, peer_u, where).then_inc(u_in[s], 16)
                pool.indirect_dma_start(aring[:, s, :], None, peer_v, where).then_inc(v_in[s], 16)

            for s in range(SLOTS):
                gather(s, s, None)
            with pool.Fori(1, NSLOT // SLOTS) as i:
                for s in range(SLOTS):
                    gather(SLOTS * i + s, s, SLOTS * i + s - SLOTS + 1)
            pool.wait_ge(picks_ready, 2)
            with pool.Fori(NSLOT // SLOTS, 2 * NSLOT // SLOTS) as i:
                for s in range(SLOTS):
                    gather(SLOTS * i + s, s, SLOTS * i + s - SLOTS + 1)

        @block.tensor
        def _(pe):
            unit_bank = lambda u: G[u % 2]

            def unit(slot, weights_at, k, rhs, u, bank, fresh=None):
                for t in range(k):
                    if fresh is not None:
                        pe.wait_ge(h_ready, 16 * fresh + t + 1)
                    mm = nc.tensor.matmul(bank[:, 0:TOK], lhsT=ring[:, slot, weights_at + t * P:weights_at + (t + 1) * P],
                                          rhs=rhs[:, t, :], start=(t == 0), stop=(t == k - 1))
                mm.then_inc(unit_done, 1)

            def dense(name, rhss, k=DT, first=0, count=None, fresh=None):
                per = len(rhss)
                n = dict((a, b) for a, b, _ in STREAM)[name]
                count = n if count is None else count
                c0, u0 = CHUNK0[name] + first, UNIT0[name] + first * per

                def chunk(j, i):
                    c = c0 + j
                    pe.wait_ge(w_in[c % SLOTS], 16 * (c // SLOTS + 1) + 16 * i)
                    for e in range(per):
                        u = u0 + j * per + e
                        if u >= 2:
                            pe.wait_ge(unit_evac, u - 1 + i * SLOTS * per)
                        if name == "kv" and j == 0 and e == 1:
                            pe.wait_ge(hc_ready, 1)
                        unit(c % SLOTS, e * k * P if per * k == DT else 0, k, rhss[e], u, unit_bank(u),
                             fresh if j == 0 and e == 0 else None)

                whole = count // SLOTS
                if whole >= 2 and u0 >= 2 and (SLOTS * per) % 2 == 0:
                    with pe.Fori(0, whole) as i:
                        for j in range(SLOTS):
                            chunk(j, i)
                    for j in range(whole * SLOTS, count):
                        chunk(j, 0)
                else:
                    for j in range(count):
                        chunk(j, 0)

            sums = [0]

            def feature_sum(src, n, at_a_time=None, bank=B7):
                for t in range(n):
                    if t % (at_a_time or n) == 0:
                        sums[0] += 1
                        pe.wait_ge(sum_in, sums[0])
                    mm = nc.tensor.matmul(bank[:, 0:TOK], lhsT=ones, rhs=src[:, t * TOK:(t + 1) * TOK],
                                          start=(t == 0), stop=(t == n - 1))
                mm.then_inc(sum_done, 1)

            def feature_sum_of_fours():
                for j in range(DT // 4):
                    sums[0] += 1
                    pe.wait_ge(sum_in, sums[0])
                    mm = nc.tensor.matmul(B7[:, 0:TOK], lhsT=ones, rhs=sq[:, 4 * j * TOK:(4 * j + 1) * TOK],
                                          start=(j == 0), stop=(j == DT // 4 - 1))
                mm.then_inc(sum_done, 1)

            heads_n = [0, 0]

            def head_sum(n, squares=head_sq_at, row=0):
                heads_n[0] += 1
                pe.wait_ge(head_sq, heads_n[0])
                for j in range(n):
                    mm = nc.tensor.matmul((B6 if row else M)[0:HEADS, 0:TOK],
                                          lhsT=C("head_col")[:, HEADS - 1 - j:2 * HEADS - 1 - j],
                                          rhs=squares[:, j * TOK:(j + 1) * TOK], start=(j == 0), stop=(j == n - 1))
                mm.then_inc(head_sums, 1)

            def head_rows_spread(n, row=0):
                heads_n[1] += 1
                pe.wait_ge(head_inv, heads_n[1])
                for j in range(n):
                    mm = nc.tensor.matmul(M[:, j * TOK:(j + 1) * TOK],
                                          lhsT=ident[0:HEADS, j:j + 1].to_broadcast([HEADS, P]),
                                          rhs=head_rows[:, row, :], start=True, stop=True)
                mm.then_inc(head_spread, 1)

            rots = [0]

            def rotate(srcs):
                rots[0] += 1
                pe.wait_ge(rot_in, rots[0])
                for j, s in enumerate(srcs):
                    w = s.shape[-1]
                    mm = nc.tensor.matmul(M[:, j * w:(j + 1) * w], lhsT=C("rot"), rhs=s, start=True, stop=True)
                mm.then_inc(rot_done, 1)

            def mod_sum(g, units):
                pe.wait_ge(ada_dve_used, 16 * (g + 1))
                pe.wait_ge(unit_evac, units)
                for m in range(DT):
                    mm = nc.tensor.matmul(G[0][:, m:m + 1], lhsT=acc[:, g % 2, m * P:(m + 1) * P],
                                          rhs=ones[:, 0:1], start=True, stop=True)
                mm.then_inc(mod_sums, 1)
                pe.wait_ge(mod_copied, g + 1)

            def attention(base, nk, q_of, k_of, v_of, pt, extra, between={}):
                w = nk * P

                def scores(hh):
                    if hh > 0:
                        pe.wait_ge(exp_done, 2 * (base + hh))
                    for qt in range(2):
                        o = M[:, qt * w:(qt + 1) * w]
                        mm = nc.tensor.matmul(o, lhsT=q_of(hh)[:, qt * P:(qt + 1) * P], rhs=k_of(hh),
                                              start=True, stop=not extra)
                        if extra:
                            nc.tensor.matmul(o, lhsT=cum[:, qt * P:(qt + 1) * P], rhs=pick_rows(hh),
                                             start=False, stop=False)
                            mm = nc.tensor.matmul(o, lhsT=pick_rows(hh)[:, 0:P], rhs=ncum, start=False, stop=True)
                    mm.then_inc(s_done, 1)

                scores(0)
                for hh in range(HEADS):
                    if hh + 1 < HEADS:
                        scores(hh + 1)
                    pe.wait_ge(p_ready, base + hh + 1)
                    if base + hh > 0:
                        pe.wait_ge(pt_copied, base + hh)
                    for kt in range(nk):
                        for qt in range(2):
                            mm = nc.tensor.transpose(M[:, 1024 + kt * 256 + qt * P:1024 + kt * 256 + (qt + 1) * P],
                                                     att[:, qt * w + kt * P:qt * w + (kt + 1) * P], ident)
                    mm.then_inc(pt_done, 1)
                    pe.wait_ge(pt_copied, base + hh + 1)
                    if base + hh >= 2:
                        pe.wait_ge(o_read, base + hh - 1)
                    for kt in range(nk):
                        mm = nc.tensor.matmul(O[hh % 2][:, 0:TOK], lhsT=v_of(hh, kt),
                                              rhs=pt[:, kt * 256:(kt + 1) * 256], start=(kt == 0), stop=(kt == nk - 1))
                    mm.then_inc(pv_done, 1)
                    if hh in between:
                        between[hh]()

            pe.wait_ge(cond_ready, 1)
            cond_v = cond[:, :].rearrange("p (v t) -> p v t", v=3)

            def rows_to_columns(g):
                pe.wait_ge(pre_rows, g + 1)
                for m in range(DT):
                    mm = nc.tensor.matmul(B6[:, g * 32 + 2 * m:g * 32 + 2 * m + 2], lhsT=acc[0:2, g, m * P:(m + 1) * P],
                                          rhs=ident[0:2, 0:2], start=True, stop=True)
                mm.then_inc(pre_cols, 1)

            for g in range(PRE_GROUPS):
                if g > 0:
                    pe.wait_ge(pre_rows, g)
                for t in range(DT):
                    pe.wait_ge(ada_in[t % SLOTS], 16 * (4 * g + t // SLOTS + 1))
                    for nb in range(4):
                        mm = nc.tensor.matmul(M[0:2, nb * 512:(nb + 1) * 512], lhsT=cond_v[:, 0:2, t],
                                              rhs=aring[:, t % SLOTS, nb * 512:(nb + 1) * 512],
                                              start=(t == 0), stop=(t == DT - 1))
                    mm.then_inc(ada_pe_used, 1)
                    if g == 1 and t == 5:
                        rows_to_columns(0)
                        feature_sum(sq, DT)
                if g == 0:
                    pe.wait_ge(consts_in, 16)
                    feature_sum(sq, DT)
            rows_to_columns(1)

            dense("kv", [h, hc], fresh=0)
            dense("ev", [h], first=0, count=8)
            head_sum(4)
            dense("ev", [h], first=8, count=2)
            head_rows_spread(4)
            dense("ev", [h], first=10, count=6)
            rotate([kv_keys[:, g, 0:TOK] for g in range(2)])
            dense("ev", [h], first=16, count=8)
            dense("ev", [h], first=24, count=1)
            head_sum(8)
            dense("ev", [h], first=25, count=4)
            head_rows_spread(8)
            dense("ev", [h], first=29, count=3)
            rotate([flat(proj[:, 0:8, :])[:, j * 512:(j + 1) * 512] for j in range(4)])
            mod_sum(0, UNIT0["ev"] + 32)
            dense("ev", [h], first=32, count=2)
            pe.wait_ge(qk_ready, 1)
            for g in range(KV):
                for kt in range(4):
                    mm = nc.tensor.transpose(M[:, 1024 + kt * 256 + g * P:1024 + kt * 256 + (g + 1) * P],
                                             kv_vals[:, g, kt * P:(kt + 1) * P], ident)
            mm.then_inc(v_turned, 1)
            pe.wait_ge(v_ready, 1)
            vtok = sq[:, 3072:4096]

            def zb(first, count=1):
                dense("ev", [h], first=32 + first, count=count)

            def conv_mean():
                pe.wait_ge(unit_evac, UNIT0["ev"] + 34)
                feature_sum(flat(proj[:, 8:16, :]), CONV_T, bank=G[1])

            def zb_after_mean():
                pe.wait_ge(sum_in, sums[0] + 1)
                zb(3)

            def conv_variance():
                pe.wait_ge(unit_evac, UNIT0["ev"] + 36)
                feature_sum(flat(proj[:, 16:24, :]), CONV_T, bank=G[1])

            def zb_after_variance():
                pe.wait_ge(std_ready, 3)
                zb(5)

            attention(0, 4, lambda hh: proj[:, hh, :], lambda hh: kv_keys[:, hh // 4, :],
                      lambda hh, kt: vtok[:, kt * 256 + (hh // 4) * P:kt * 256 + (hh // 4 + 1) * P],
                      sq[:, 2048:3072], False,
                      {0: lambda: zb(2), 1: conv_mean, 3: zb_after_mean, 4: conv_variance,
                       5: lambda: zb(4), 6: zb_after_variance, 7: lambda: zb(6, 2)})
            pe.wait_ge(mix_ready, 1)
            dense("ev_out", [proj])
            mod_sum(1, UNIT0["od"])
            mod_sum(2, UNIT0["od"])

            feature_sum_of_fours()
            dense("od", [h], first=0, count=4, fresh=1)
            dense("od", [h], first=4, count=12)
            mod_sum(3, UNIT0["od"] + 16)
            dense("od", [h], first=16, count=2)
            feature_sum(sq, 1)
            dense("od", [h], first=18, count=14)
            feature_sum(sq, 1)
            mod_sum(4, UNIT0["od"] + 32)
            dense("od", [h], first=32, count=16)
            pe.wait_ge(gate_v_ready, 1)
            for b in range(4):
                half = (b % 2) * 1024
                if b >= 2:
                    pe.wait_ge(vt_copied, b - 1)
                for j in range(8):
                    n, c = (b % 2) * 8 + j, b // 2
                    mm = nc.tensor.transpose(M[:, half + j * P:half + (j + 1) * P], proj[:, n, c * P:(c + 1) * P], ident)
                mm.then_inc(vt_done, 1)
            pe.wait_ge(spatial_in, 16)
            for b in range(4):
                half = (b % 2) * 1024
                pe.wait_ge(vt_copied, 4 if b < 2 else 4)
                if b >= 2:
                    pe.wait_ge(sgu_read, b - 1)
                for j in range(4):
                    n = 4 * b + j
                    for c in range(2):
                        mm = nc.tensor.matmul(M[:, half + j * TOK + c * P:half + j * TOK + (c + 1) * P],
                                              lhsT=sq[:, c * D + n * P:c * D + (n + 1) * P],
                                              rhs=att[:, (n // 2) * P:(n // 2 + 1) * P], start=True, stop=True)
                mm.then_inc(sgu_done, 1)
            mod_sum(5, UNIT0["od_out"])
            pe.wait_ge(sgu_ready, 1)
            dense("od_out", [proj])
            mod_sum(6, UNIT0["w_in"])

            feature_sum_of_fours()
            feature_sum(sq, DT, 4)
            dense("w_in", [h], first=0, count=4, fresh=2)
            for t in range(DT):
                mm = nc.tensor.matmul(B7[0:8, 0:TOK], lhsT=V("w_f")[:, t * 8:(t + 1) * 8], rhs=h[:, t, :],
                                      start=(t == 0), stop=(t == DT - 1))
            mm.then_inc(f_done, 1)

            def turn_b(q):
                pe.wait_ge(ssm_bc, q + 1)
                for part in range(2):
                    for j in range(4):
                        o = M[:, 1024 * part + j * P:1024 * part + (j + 1) * P]
                        mm = nc.tensor.transpose(o, att[:, part * 512 + j * P:part * 512 + (j + 1) * P], ident)
                mm.then_inc(ssm_bt, 1)

            def inputs_of_states(q):
                pe.wait_ge(ssm_btc, q + 1)
                for part in range(2):
                    for j in range(4):
                        mm = nc.tensor.matmul(M[:, 1024 * part + j * TOK:1024 * part + (j + 1) * TOK],
                                              lhsT=sq[:, part * 512 + j * P:part * 512 + (j + 1) * P],
                                              rhs=proj[:, q, :], start=True, stop=True)
                mm.then_inc(ssm_bu, 1)

            def outputs_of_states(q):
                pe.wait_ge(ssm_s, q + 1)
                for part in range(2):
                    for j in range(4):
                        mm = nc.tensor.matmul(B6[:, 0:TOK], lhsT=sq[:, 1024 + part * 512 + j * P:1024 + part * 512 + (j + 1) * P],
                                              rhs=ssm_w[part][:, j * TOK:(j + 1) * TOK],
                                              start=(part == 0 and j == 0), stop=(part == 1 and j == 3))
                mm.then_inc(ssm_y, 1)

            ssm_w = [flat(w_re), flat(w_im)]
            turn_b(0)
            dense("w_in", [h], first=4, count=4)
            inputs_of_states(0)
            dense("w_in", [h], first=8, count=4)
            for q in range(1, 4):
                outputs_of_states(q - 1)
                turn_b(q)
                inputs_of_states(q)
                dense("w_in", [h], first=8 + 4 * q, count=4)
            outputs_of_states(3)
            dense("w_in", [h], first=24, count=4)
            head_sum(8, sq, row=0)
            head_sum(8, row=1)
            head_rows_spread(8, row=0)
            pe.wait_ge(ssm_g, 4)
            dense("glu", [proj, proj, proj, proj], k=4)
            pe.wait_ge(head_used, 1)
            head_rows_spread(8, row=1)
            pe.wait_ge(qk_ready, 2)
            for hh in range(HEADS):
                for kt in range(2):
                    mm = nc.tensor.transpose(M[:, kt * 1024 + hh * P:kt * 1024 + (hh + 1) * P],
                                             proj[:, 20 + hh, kt * P:(kt + 1) * P], ident)
            mm.then_inc(v_turned, 1)
            pe.wait_ge(v_ready, 2)
            pe.wait_ge(cum_ready, 1)
            vtok2 = flat(proj[:, 36:44, :])

            def pick_rows(hh):
                return ident[0:8, hh:hh + 1].to_broadcast([8, TOK])

            def ssm_up(first):
                if first == 0:
                    pe.wait_ge(glu_ready, 1)
                dense("ssm_up", [proj, proj, proj, proj], k=4, first=first, count=1)

            attention(8, 2, lambda hh: proj[:, 12 + hh, :], lambda hh: proj[:, 4 + hh, :],
                      lambda hh, kt: vtok2[:, kt * 1024 + hh * P:kt * 1024 + (hh + 1) * P], sq[:, 2048:2560], True,
                      {0: lambda: ssm_up(0), 2: lambda: ssm_up(1), 4: lambda: ssm_up(2), 6: lambda: ssm_up(3)})
            pe.wait_ge(o_read, 16)
            dense("attn_up", [proj[:, 12:20, :], proj[:, 12:20, :]], k=8)
            dense("gates", [h], count=16)
            mod_sum(7, UNIT0["gates"] + 16)
            dense("gates", [h], first=16, count=16)
            mod_sum(8, UNIT0["w_out"])
            pe.wait_ge(merged, 1)
            dense("w_out", [proj[:, 0:16, :]])
            pe.wait_ge(ada_dve_used, 16 * len(ADA))
            for nb in range(4):
                mm = nc.tensor.matmul(M[:, nb * 512:(nb + 1) * 512], lhsT=ones, rhs=acc[:, 1, nb * 512:(nb + 1) * 512],
                                      start=True, stop=True)
            mm.then_inc(g3_done, 1)
            feature_sum_of_fours()

            def turn_to_tokens(src, first):
                for b in range(4):
                    half = (b % 2) * 1024
                    if first + b >= 2:
                        pe.wait_ge(ht_copied, first + b - 1)
                    for j in range(8):
                        n, c = (b % 2) * 8 + j, b // 2
                        mm = nc.tensor.transpose(M[:, half + j * P:half + (j + 1) * P], src[:, n, c * P:(c + 1) * P], ident)
                    mm.then_inc(ht_done, 1)

            keys = flat(proj[:, 40:48, :])

            def key_scores(r):
                if r == 0:
                    pe.wait_ge(keys_in, 16)
                pe.wait_ge(unit_evac, UNIT0["peer_q"] + r + 1)
                if r >= 2:
                    pe.wait_ge(sc_copied, r - 1)
                for half in range(2):
                    mm = nc.tensor.matmul(O[r % 2][:, half * P:(half + 1) * P], lhsT=proj[:, r, half * P:(half + 1) * P],
                                          rhs=keys[:, r * P:(r + 1) * P], start=True, stop=True)
                mm.then_inc(sc_done, 1)

            dense("peer_q", [h], count=1, fresh=3)
            for r in range(1, 16):
                dense("peer_q", [h], first=r, count=1)
                key_scores(r - 1)
            key_scores(15)
            pe.wait_ge(g3_ready, 1)
            turn_to_tokens(h, 0)
            turn_to_tokens(x, 4)

        @block.scalar
        def _(act):
            def leave(u, dst, func, i=0, per=0, scale=1.0, bias=0.0):
                act.wait_ge(unit_done, u + 1 + i)
                nc.scalar.activation(dst, G[u % 2][:, 0:TOK], func, bias=bias, scale=scale).then_inc(unit_evac, 1)

            def leave_many(u0, tile0, n, func):
                if n >= 8:
                    with act.Fori(0, n // 4) as i:
                        for j in range(4):
                            leave(u0 + j, flat(proj[:, :, :])[:, bass.ds((tile0 + j) * TOK + i * (4 * TOK), TOK)], func, i=4 * i)
                else:
                    for j in range(n):
                        leave(u0 + j, proj[:, tile0 + j, :], func)

            def leave_gated(u0, gate):
                for n in range(DT):
                    leave(u0 + n, h[:, n, :], ACT.Identity, scale=gate[:, n:n + 1])

            def mod_out(g):
                act.wait_ge(mod_sums, g + 1)
                nc.scalar.activation(mods[:, 16 * (4 + g):16 * (5 + g)], G[0][:, 0:16], ACT.Copy).then_inc(mod_copied, 1)

            sums = [0]

            def std(n, count=1, bank=B7):
                sums[0] += count
                act.wait_ge(sum_done, sums[0])
                nc.scalar.activation(rstd[:, :], bank[:, 0:TOK], ACT.Sqrt, bias=eps, scale=1.0 / n).then_inc(std_ready, 1)

            def modulate(nth, shift):
                for t in range(DT):
                    act.wait_ge(h_scaled, 4 * nth + t // 4 + 1)
                    nc.scalar.activation(h[:, t, :], h[:, t, :], ACT.Identity, bias=shift[:, t:t + 1],
                                         scale=gs[:, t:t + 1]).then_inc(h_ready, 1)

            hn = [0]

            def head_stds(row=0):
                hn[0] += 1
                act.wait_ge(head_sums, hn[0])
                nc.scalar.activation(head_rows[:, row, :], (B6 if row else M)[0:HEADS, 0:TOK], ACT.Sqrt,
                                     bias=eps[0:HEADS, :], scale=1.0 / HD).then_inc(head_std, 1)

            def softmax_steps(base, nk, pt, scale, between={}):
                w = nk * P

                def exps(hh):
                    act.wait_ge(nmax_ready, base + hh + 1)
                    if base == 0 and hh > 0:
                        act.wait_ge(pt_done, base + hh)
                    for qt in range(2):
                        src = M[:, qt * w:(qt + 1) * w] if nk == 4 else att[:, qt * w:(qt + 1) * w]
                        nc.scalar.activation(att[:, qt * w:(qt + 1) * w], src, ACT.Exp, bias=small[:, 2 + qt:3 + qt],
                                                 scale=scale, accum_out=small[:, 4 + qt:5 + qt]).then_inc(exp_done, 1)

                exps(0)
                for hh in range(HEADS):
                    act.wait_ge(pt_done, base + hh + 1)
                    if hh > 0:
                        act.wait_ge(pv_done, base + hh)
                    nc.scalar.activation(pt, M[:, 1024:1024 + nk * 256], ACT.Copy).then_inc(pt_copied, 1)
                    if hh + 1 < HEADS:
                        exps(hh + 1)
                    if hh in between:
                        between[hh]()

            act.wait_ge(conds_in, 16)
            nc.scalar.activation(cond[:, :], cond[:, :], ACT.Silu).then_inc(cond_ready, 1)
            act.wait_ge(dve_step, 1)
            act.wait_ge(vecs_in, 16)
            act.wait_ge(trig_in, 1)
            nc.scalar.activation(small[:, 64:96], small[:, 64:96], ACT.Sin).then_inc(trig_out, 1)
            for g in range(PRE_GROUPS):
                act.wait_ge(ada_pe_used, 16 * (g + 1))
                nc.scalar.activation(acc[0:2, g, :], M[0:2, :], ACT.Copy).then_inc(pre_rows, 1)
                if g == 0:
                    std(D)
                    std(D)
            modulate(0, mod("shift0"))
            for t in range(4):
                dst = (kv_keys if t < 2 else kv_vals)[:, t % 2, :]
                leave(2 * t, dst[:, 0:TOK], ACT.Copy)
                leave(2 * t + 1, dst[:, TOK:2 * TOK], ACT.Copy)
            u = UNIT0["ev"]
            leave_many(u, 8, 8, ACT.Copy)
            head_stds()
            leave_many(u + 8, 16, 8, ACT.Sigmoid)
            leave_many(u + 16, 0, 8, ACT.Copy)
            leave_many(u + 24, 24, 1, ACT.Silu)
            head_stds()
            leave_many(u + 25, 25, 7, ACT.Silu)
            mod_out(0)
            leave_many(u + 32, 32, 2, ACT.Silu)
            act.wait_ge(v_turned, 1)
            nc.scalar.activation(sq[:, 3072:4096], M[:, 1024:2048], ACT.Copy).then_inc(v_ready, 1)

            def conv_silu():
                act.wait_ge(conv_normed, 1)
                for t in range(CONV_T):
                    nc.scalar.activation(proj[:, 8 + t, :], proj[:, 8 + t, :], ACT.Silu, bias=V("ln_b")[:, t:t + 1],
                                         scale=V("ln_g")[:, t:t + 1]).then_inc(conv_act, 1)

            def zb(first, count=1):
                leave_many(UNIT0["ev"] + 32 + first, 32 + first, count, ACT.Silu)

            def zb_and_conv():
                zb(5)
                conv_silu()

            softmax_steps(0, 4, sq[:, 2048:3072], HD ** -0.5,
                          {0: lambda: zb(2), 3: lambda: zb(3),
                           4: lambda: std(CONV_T * P, count=2, bank=G[1]), 5: lambda: zb(4), 6: zb_and_conv,
                           7: lambda: zb(6, 2)})
            act.dma_start(att[:, 0:1024], wsT).then_inc(spatial_in, 16)
            act.dma_start(att[:, 1024:2048], bs.partition_broadcast(P)).then_inc(bs_in, 16)
            act.wait_ge(mods_ready, 1)
            leave_gated(UNIT0["ev_out"], mod("gate0"))
            mod_out(1)
            mod_out(2)
            std(D)
            modulate(1, mod("shift1"))
            u = UNIT0["od"]
            leave_many(u, 0, 16, ACT.Gelu_apprx_tanh)
            mod_out(3)
            leave_many(u + 16, 16, 16, ACT.Gelu_apprx_tanh)
            std(D, count=2)
            mod_out(4)
            leave_many(u + 32, 32, 16, ACT.Silu)
            for b in range(4):
                act.wait_ge(vt_done, b + 1)
                half = (b % 2) * 1024
                nc.scalar.activation(sq[:, (b // 2) * D + (b % 2) * 1024:(b // 2) * D + (b % 2) * 1024 + 1024],
                                     M[:, half:half + 1024], ACT.Copy).then_inc(vt_copied, 1)
            mod_out(5)
            act.wait_ge(mods_ready, 4)
            leave_gated(UNIT0["od_out"], mod("gate1"))
            mod_out(6)
            std(D)
            std(D)
            modulate(2, mod("shift2"))
            u = UNIT0["w_in"]
            leave_many(u, 0, 4, ACT.Copy)
            act.wait_ge(f_exp_in, 1)
            nc.scalar.activation(f_exp_row, f_exp_row, ACT.Exp).then_inc(f_exp, 1)
            act.wait_ge(f_ln_in, 1)
            nc.scalar.activation(f_exp_row, f_exp_row, ACT.Ln).then_inc(f_ln, 1)

            def copy_b(q):
                act.wait_ge(ssm_bt, q + 1)
                nc.scalar.activation(sq[:, 0:1024].rearrange("p (a b) -> p a b", a=2),
                                     M[:, :].rearrange("p (a b) -> p a b", a=2)[:, :, 0:512], ACT.Copy).then_inc(ssm_btc, 1)

            def gelu_y(q):
                act.wait_ge(ssm_yd, q + 1)
                nc.scalar.activation(proj[:, q, :], proj[:, q, :], ACT.Gelu).then_inc(ssm_g, 1)

            copy_b(0)
            leave_many(u + 4, 4, 4, ACT.Copy)
            leave_many(u + 8, 8, 4, ACT.Copy)
            for q in range(1, 4):
                copy_b(q)
                leave_many(u + 8 + 4 * q, 8 + 4 * q, 4, ACT.Copy)
                gelu_y(q - 1)
            leave_many(u + 24, 24, 4, ACT.Copy)
            gelu_y(3)
            head_stds(0)
            head_stds(1)
            for t in range(4):
                leave(UNIT0["glu"] + t, proj[:, 28 + t, :], ACT.Sigmoid, bias=V("b_glu")[:, t:t + 1])
            act.wait_ge(v_turned, 2)
            nc.scalar.activation(flat(proj[:, 36:44, :]), M[:, :], ACT.Copy).then_inc(v_ready, 1)

            def ssm_up(first):
                for n in range(4 * first, 4 * first + 4):
                    leave(UNIT0["ssm_up"] + n, sq[:, n * TOK:(n + 1) * TOK] if n < 8 else proj[:, 20 + n, :], ACT.Copy)

            softmax_steps(8, 2, sq[:, 2048:2560], 1.0,
                          {0: lambda: ssm_up(0), 2: lambda: ssm_up(1), 4: lambda: ssm_up(2), 6: lambda: ssm_up(3)})
            act.wait_ge(pv_done, 16)
            for n in range(8):
                leave(UNIT0["attn_up"] + n, sq[:, (8 + n) * TOK:(9 + n) * TOK], ACT.Copy)
            leave_many(UNIT0["attn_up"] + 8, 36, 8, ACT.Copy)
            act.wait_ge(unit_done, UNIT0["gates"])
            leave_many(UNIT0["gates"], 0, 16, ACT.Sigmoid)
            mod_out(7)
            leave_many(UNIT0["gates"] + 16, 16, 12, ACT.Sigmoid)
            leave_many(UNIT0["gates"] + 28, 44, 4, ACT.Sigmoid)
            mod_out(8)
            act.wait_ge(mods_ready, 7)
            leave_gated(UNIT0["w_out"], mod("gate2"))
            act.dma_start(flat(proj[:, 40:48, :]), keysT).then_inc(keys_in, 16)
            std(D)
            modulate(3, mod("shift3"))
            scores = proj[:, 16:32, :]

            def keep_scores(r):
                act.wait_ge(sc_done, r + 1)
                nc.scalar.activation(scores[:, r, :], O[r % 2][:, 0:TOK], ACT.Copy).then_inc(sc_copied, 1)

            leave(UNIT0["peer_q"], proj[:, 0, :], ACT.Copy)
            for r in range(1, 16):
                leave(UNIT0["peer_q"] + r, proj[:, r, :], ACT.Copy)
                keep_scores(r - 1)
            keep_scores(15)

            def to_tokens(dst, first):
                for b in range(4):
                    act.wait_ge(ht_done, first + b + 1)
                    half = (b % 2) * 1024
                    nc.scalar.activation(dst[:, (b // 2) * D + half:(b // 2) * D + half + 1024], M[:, half:half + 1024],
                                         ACT.Copy).then_inc(ht_copied, 1)

            to_tokens(sq, 0)
            to_tokens(flat(acc[:, :, :]), 4)
            gw = flat(proj[:, 39:40, :])

            def gate_exp(tk):
                act.wait_ge(gexp_in, tk + 1)
                g = gw[:, tk * P:(tk + 1) * P]
                nc.scalar.activation(g, g, ACT.Exp).then_inc(gexp_out, 1)
                act.wait_ge(picks_ready, tk + 1)

            def coefficients(first, end):
                with act.Fori(first // SLOTS, end // SLOTS) as i:
                    for s in range(SLOTS):
                        act.wait_ge(dot_done, SLOTS * i + s + 1)
                        nc.scalar.activation(dots[:, SLOTS + s:SLOTS + s + 1], dots[:, s:s + 1], ACT.Gelu).then_inc(gelu_done, 1)
                        act.wait_ge(gelu_done, SLOTS * i + s + 1)
                        nc.scalar.activation(dots[:, 2 * SLOTS + s:2 * SLOTS + s + 1], gw[:, bass.ds(SLOTS * i + s, 1)],
                                             ACT.Copy, scale=dots[:, SLOTS + s:SLOTS + s + 1]).then_inc(coef_ready, 1)

            gate_exp(0)
            coefficients(0, HEADS * SLOTS)
            gate_exp(1)
            coefficients(HEADS * SLOTS, 2 * NSLOT)

        @block.vector
        def _(dve):
            V_ = nc.vector
            counts = {}

            def step(ins, on=None):
                s, key = (dve_step, "step") if on is None else (on, on.name)
                counts[key] = counts.get(key, 0) + 1
                ins.then_inc(s, 1)
                dve.wait_ge(s, counts[key])

            tt = V_.tensor_tensor
            loop_count = [0]

            def affine(buf, n, mul, add=None):
                base = loop_count[0]
                loop_count[0] += n
                with dve.Fori(0, n // 4) as i:
                    for j in range(4):
                        t = buf[:, bass.ds(j * TOK + i * (4 * TOK), TOK)]
                        m = mul[:, bass.ds(4 * i + j, 1)]
                        a = None if add is None else add[:, bass.ds(4 * i + j, 1)]
                        V_.tensor_scalar(t, t, m, a, ALU.mult, *([] if add is None else [ALU.add])).then_inc(tile_step, 1)
                dve.wait_ge(tile_step, base + n)

            sums = {"sum": 0, "std": 0}

            def square_sum(src3, n, dst=None):
                s = flat(src3)
                step(tt(sq[:, 0:n * TOK] if dst is None else dst, s, s, ALU.mult), on=sum_in)

            def add_tiles(dst, src, n):
                while n > 1:
                    n //= 2
                    step(tt(dst[:, 0:n * TOK], src[:, 0:n * TOK], src[:, n * TOK:2 * n * TOK], ALU.add),
                         on=sum_in if n == 1 else None)
                    src = dst

            def root():
                sums["std"] += 1
                dve.wait_ge(std_ready, sums["std"])
                step(V_.reciprocal(rstd[:, :], rstd[:, :]))

            def scaled(dst3, src3, n):
                step(tt(dst3, src3, over_tiles(rstd[:, :], n), ALU.mult))

            def centre(t3, n, nth, bank=B7):
                dve.wait_ge(sum_done, nth)
                step(V_.scalar_tensor_tensor(out=t3, in0=over_tiles(bank[:, 0:TOK], n), scalar=-1.0 / (n * P), in1=t3,
                                             op0=ALU.mult, op1=ALU.add))

            def ada_group(g):
                if g < 2:
                    dve.wait_ge(pre_cols, 2)
                else:
                    dve.wait_ge(mod_sums, g - 1)
                v = 0 if g < 4 else 32
                a = acc[:, g % 2, :]

                def chunk(k, i):
                    s = k % SLOTS
                    dve.wait_ge(ada_in[s], 16 * (4 * (PRE_GROUPS + g) + 1 + i))
                    c = cond[:, bass.ds(v + s + SLOTS * i, 1)]
                    if k == 0 and isinstance(i, int):
                        V_.tensor_scalar(a, aring[:, s, :], c, None, ALU.mult).then_inc(ada_dve_used, 1)
                    else:
                        dve.wait_ge(ada_dve_used, 16 * g + s + SLOTS * i)
                        V_.scalar_tensor_tensor(out=a, in0=aring[:, s, :], scalar=c, in1=a, op0=ALU.mult,
                                                op1=ALU.add).then_inc(ada_dve_used, 1)

                for k in range(SLOTS):
                    chunk(k, 0)
                with dve.Fori(1, 16 // SLOTS) as i:
                    for k in range(SLOTS):
                        chunk(k, i)

            def ada_part(g, first, count):
                v = 0 if g < 4 else 32
                a = acc[:, g % 2, :]
                for k in range(first, first + count):
                    dve.wait_ge(ada_in[k % SLOTS], 16 * (4 * (PRE_GROUPS + g) + 1 + k // SLOTS))
                    c = cond[:, v + k:v + k + 1]
                    if k == 0:
                        V_.tensor_scalar(a, aring[:, k % SLOTS, :], c, None, ALU.mult).then_inc(ada_dve_used, 1)
                    else:
                        dve.wait_ge(ada_dve_used, 16 * g + k)
                        V_.scalar_tensor_tensor(out=a, in0=aring[:, k % SLOTS, :], scalar=c, in1=a, op0=ALU.mult,
                                                op1=ALU.add).then_inc(ada_dve_used, 1)

            def mods_from(g):
                dve.wait_ge(mod_copied, g + 1)
                m = mods[:, 16 * (4 + g):16 * (5 + g)]
                step(tt(m, m, V("ada_b")[:, 16 * (2 + g):16 * (3 + g)], ALU.add), on=mods_ready)

            def norm_weight(dst, norm, scale):
                step(V_.scalar_tensor_tensor(out=dst, in0=scale, scalar=1.0, in1=norm, op0=ALU.add, op1=ALU.mult))

            def head_squares(src, n, dst=head_sq_at):
                step(tt(dst[:, 0:n * TOK], src, src, ALU.mult), on=head_sq)

            def head_inverse(row=0):
                counts["head"] = counts.get("head", 0) + 1
                dve.wait_ge(head_std, counts["head"])
                step(V_.reciprocal(head_rows[:, row, :], head_rows[:, row, :]), on=head_inv)

            def head_scale(src, n, weight):
                counts["spread"] = counts.get("spread", 0) + 1
                dve.wait_ge(head_spread, counts["spread"])
                return V_.scalar_tensor_tensor(out=src, in0=src, scalar=weight, in1=M[:, 0:n * TOK],
                                               op0=ALU.mult, op1=ALU.mult)

            def rope(src3, n, nth):
                dve.wait_ge(rot_done, nth)
                t = tiles(head_sq_at[:, 0:n * TOK], n)
                step(tt(t, tiles(M[:, 0:n * TOK], n), over_tiles(C("sin"), n), ALU.mult))
                step(tt(src3, src3, over_tiles(C("cos"), n), ALU.mult))
                return tt(src3, src3, t, ALU.add)

            def softmax(base, nk, scale, finish, between={}):
                w = nk * P
                probs = att[:, 0:2 * w].rearrange("p (a b) -> p a b", a=2)

                def maxima(hh):
                    dve.wait_ge(s_done, base + hh + 1)
                    s = M[:, 0:2 * w].rearrange("p (a b) -> p a b", a=2)
                    if base:
                        if hh:
                            dve.wait_ge(pt_done, base + hh)
                        step(tt(probs, s, C("mask").rearrange("p (a b) -> p a b", a=2), ALU.add))
                        s = probs
                    step(V_.tensor_reduce(small[:, 0:2], s, AX, ALU.max))
                    step(V_.tensor_scalar(small[:, 2:4], small[:, 0:2], -scale, None, ALU.mult), on=nmax_ready)

                maxima(0)
                for hh in range(HEADS):
                    dve.wait_ge(exp_done, 2 * (base + hh + 1))
                    step(V_.reciprocal(small[:, 6:8], small[:, 4:6]))
                    step(V_.tensor_scalar(probs[:, 0, :], probs[:, 0, :], small[:, 6:7], None, ALU.mult))
                    step(V_.tensor_scalar(probs[:, 1, :], probs[:, 1, :], small[:, 7:8], None, ALU.mult), on=p_ready)
                    if hh + 1 < HEADS:
                        maxima(hh + 1)
                    dve.wait_ge(pv_done, base + hh + 1)
                    finish(hh, O[hh % 2][:, 0:TOK])
                    if hh in between:
                        between[hh]()

            step(V_.memset(eps, EPS))
            dve.wait_ge(vecs_in, 16)
            S = lambda a: small[:, a:a + 16]
            dt, mag, theta, sin_, cos_, k_, t0, t1 = S(16), S(32), S(48), S(64), S(80), S(96), S(112), S(128)
            cr, ci = S(144), S(160)

            def times(dst, a, b):
                step(tt(dst, a, b, ALU.mult))

            def double_phases(c, s, scratch, k, power):
                n = 1 << k
                pc, ps = (power[:, e].unsqueeze(2).to_broadcast([P, c.shape[1], n]) for e in range(2))
                lo_c, lo_s, hi_c, hi_s, t = c[:, :, 0:n], s[:, :, 0:n], c[:, :, n:2 * n], s[:, :, n:2 * n], scratch[:, :, 0:n]
                times(hi_c, lo_c, pc)
                times(t, lo_s, ps)
                step(tt(hi_c, hi_c, t, ALU.subtract))
                times(hi_s, lo_c, ps)
                times(t, lo_s, pc)
                step(tt(hi_s, hi_s, t, ALU.add))

            def exact_exp(dst, src):
                n, r, p = k_, t0, t1
                step(V_.tensor_scalar(r, src, -87.0, 88.0, ALU.max, ALU.min))
                step(V_.tensor_scalar(n, r, 1.0 / LN2, ROUND, ALU.mult, ALU.add))
                step(V_.tensor_scalar(n, n, ROUND, None, ALU.subtract))
                step(V_.scalar_tensor_tensor(out=r, in0=n, scalar=-LN2_HI, in1=r, op0=ALU.mult, op1=ALU.add))
                step(V_.scalar_tensor_tensor(out=r, in0=n, scalar=-(LN2 - LN2_HI), in1=r, op0=ALU.mult, op1=ALU.add))
                step(V_.tensor_scalar(p, r, 1.0 / 5040, 1.0 / 720, ALU.mult, ALU.add))
                for c in (1.0 / 120, 1.0 / 24, 1.0 / 6, 0.5, 1.0, 1.0):
                    step(tt(p, p, r, ALU.mult))
                    step(V_.tensor_scalar(p, p, c, None, ALU.add))
                step(V_.tensor_scalar(n, n, 127.0, 2.0 ** 23, ALU.add, ALU.mult))
                step(V_.tensor_copy(r.bitcast(U32), n))
                step(tt(p, p, r, ALU.mult))
                step(V_.scalar_tensor_tensor(out=dst, in0=src, scalar=-87.0, in1=p, op0=ALU.is_ge, op1=ALU.mult))

            exact_exp(dt, V("log_dt"))
            step(tt(theta, V("A_re"), dt, ALU.mult))
            exact_exp(mag, theta)
            step(tt(theta, V("A_im"), dt, ALU.mult))
            step(V_.tensor_scalar(k_, theta, 1.0 / (2 * np.pi), ROUND, ALU.mult, ALU.add))
            step(V_.tensor_scalar(k_, k_, ROUND, None, ALU.subtract))
            step(V_.scalar_tensor_tensor(out=t0, in0=k_, scalar=-TURN[0], in1=theta, op0=ALU.mult, op1=ALU.add))
            step(V_.scalar_tensor_tensor(out=t1, in0=k_, scalar=-TURN[1], in1=t0, op0=ALU.mult, op1=ALU.add))
            step(V_.scalar_tensor_tensor(out=t0, in0=k_, scalar=-TURN[2], in1=t1, op0=ALU.mult, op1=ALU.add))
            step(V_.tensor_scalar(sin_, t0, HALF_TURN, -HALF_TURN, ALU.min, ALU.max))
            step(V_.scalar_tensor_tensor(out=t1, in0=sin_, scalar=-1.0, in1=sin_, op0=ALU.mult, op1=ALU.max))
            step(V_.tensor_scalar(cos_, t1, -1.0, float(np.pi / 2), ALU.mult, ALU.add), on=trig_in)
            dve.wait_ge(trig_out, 1)
            step(V_.tensor_copy(powers[:, 0, 0, :], cos_))
            step(V_.tensor_copy(powers[:, 0, 1, :], sin_))
            for k in range(7):
                c, s_ = powers[:, k, 0, :], powers[:, k, 1, :]
                step(tt(t0, c, c, ALU.mult))
                step(tt(t1, s_, s_, ALU.mult))
                step(tt(powers[:, k + 1, 0, :], t0, t1, ALU.subtract))
                step(V_.scalar_tensor_tensor(out=powers[:, k + 1, 1, :], in0=c, scalar=2.0, in1=s_, op0=ALU.mult,
                                             op1=ALU.mult))
            step(V_.memset(seeds[:, 0, :, 0:1], 1.0))
            step(V_.memset(seeds[:, 1, :, 0:1], 0.0))
            for k in range(4):
                double_phases(seeds[:, 0], seeds[:, 1], att[:, 1024:1280].rearrange("p (a b) -> p a b", a=16), k,
                              powers[:, k, :, :])
            a_re, a_im, den = cos_, sin_, k_
            step(tt(a_re, mag, cos_, ALU.mult))
            step(tt(a_im, mag, sin_, ALU.mult))
            step(V_.tensor_scalar(a_re, a_re, 1.0, None, ALU.subtract))
            step(tt(t0, V("A_re"), V("A_re"), ALU.mult))
            step(tt(t1, V("A_im"), V("A_im"), ALU.mult))
            step(tt(den, t0, t1, ALU.add))
            step(V_.reciprocal(den, den))
            for out_, p_, q_, op in ((cr, (a_re, "A_re"), (a_im, "A_im"), ALU.add),
                                     (ci, (a_im, "A_re"), (a_re, "A_im"), ALU.subtract)):
                step(tt(t0, p_[0], V(p_[1]), ALU.mult))
                step(tt(t1, q_[0], V(q_[1]), ALU.mult))
                step(tt(t0, t0, t1, op))
                step(tt(out_, t0, den, ALU.mult))
            wide = lambda ap: ap.unsqueeze(2).to_broadcast([P, 16, 16])
            square = lambda ap: ap.rearrange("p (a b) -> p a b", a=16)
            b_re, b_im = square(V("B_re")), square(V("B_im"))
            x0, x1, x2 = (square(att[:, 256 * i:256 * (i + 1)]) for i in range(3))
            step(tt(x0, b_re, wide(cr), ALU.mult))
            step(tt(x1, b_im, wide(ci), ALU.mult))
            step(tt(x2, b_re, wide(ci), ALU.mult))
            step(tt(b_re, x0, x1, ALU.subtract))
            step(tt(x0, b_im, wide(cr), ALU.mult))
            step(tt(b_im, x0, x2, ALU.add))
            step(V_.tensor_scalar(V("C_im"), V("C_im"), -1.0, None, ALU.mult))
            step(V_.tensor_scalar(small[:, 9:10], V("q_norm_2"), HD ** -0.5, None, ALU.mult))
            step(V_.memset(att[:, :], 0.0))

            dve.wait_ge(ctx_in, 16)
            square_sum(craw, DT)
            root()
            scaled(hc, craw, DT)
            dve.wait_ge(x_in, 16)
            square_sum(x[:, :, :], DT)
            root()
            scaled(h[:, :, :], x[:, :, :], DT)
            dve.wait_ge(pre_cols, 2)
            for v in range(2):
                step(tt(mods[:, 32 * v:32 * v + 32].rearrange("p (g m) -> p g m", g=2),
                        B6[:, 0:64].rearrange("p (g m v) -> p v g m", g=2, v=2)[:, v],
                        V("ada_b")[:, 0:32].rearrange("p (g m) -> p g m", g=2), ALU.add))
            norm_weight(gs[:, :], V("norm_g0"), mod("scale0"))
            dve.sem_inc(h_scaled, 4)
            norm_weight(S(176), V("norm_g0"), mod("scale0c"))
            affine(flat(hc), DT, S(176), mod("shift0c"))
            dve.sem_inc(hc_ready, 1)

            ada_group(0)
            dve.wait_ge(unit_evac, UNIT0["ev"])
            head_squares(sq[:, 0:1024], 4)
            head_inverse()
            step(head_scale(sq[:, 0:1024], 4, V("k_norm")), on=rot_in)
            step(rope(kv_keys[:, :, 0:TOK], 2, 1))
            ev = UNIT0["ev"]
            dve.wait_ge(unit_evac, ev + 16)
            padded = tiles(att[:, :], CONV_T)
            step(tt(padded[:, :, CONV_W // 2:CONV_W // 2 + TOK], proj[:, 8:16, :], proj[:, 16:24, :], ALU.mult))
            aflat, pflat = att[:, :], flat(proj[:, :, :])

            def conv_pairs(first, count):
                with dve.Fori(first, first + count) as i:
                    for k in range(CONV_W):
                        for e in range(2):
                            o = pflat[:, bass.ds((8 + e) * TOK + i * (2 * TOK), TOK)]
                            src = aflat[:, bass.ds(e * PADW + k + i * (2 * PADW), TOK)]
                            wk = V("dw_w")[:, bass.ds(e * CONV_W + k + i * (2 * CONV_W), 1)]
                            if k == 0:
                                V_.tensor_scalar(o, src, wk, V("dw_b")[:, bass.ds(e + 2 * i, 1)], ALU.mult,
                                                 ALU.add).then_inc(conv_step, 1)
                            else:
                                dve.wait_ge(conv_step, 2 * (k - 1) + e + 1 + i * (2 * CONV_W))
                                V_.scalar_tensor_tensor(out=o, in0=src, scalar=wk, in1=o, op0=ALU.mult,
                                                        op1=ALU.add).then_inc(conv_step, 1)

            conv_pairs(0, 2)
            dve.wait_ge(unit_evac, ev + 24)
            head_squares(flat(proj[:, 0:8, :]), 8)
            conv_pairs(2, 1)
            head_inverse()
            conv_pairs(3, 1)
            dve.wait_ge(conv_step, CONV_T * CONV_W)
            step(head_scale(flat(proj[:, 0:8, :]), 8, V("q_norm")), on=rot_in)
            step(rope(proj[:, 0:8, :], 8, 2), on=qk_ready)
            mods_from(0)
            dve.wait_ge(unit_evac, ev + 32)

            def gate_attention(hh, o):
                step(tt(proj[:, hh, :], o, proj[:, 24 + hh, :], ALU.mult), on=o_read)

            conv = proj[:, 8:16, :]
            dve.sem_inc(sum_in, 1)
            counts[sum_in.name] += 1

            def conv_centre():
                centre(conv, CONV_T, 3, bank=G[1])
                square_sum(conv, CONV_T, dst=flat(proj[:, 16:24, :]))

            def conv_scale():
                root()
                step(tt(conv, conv, over_tiles(rstd[:, :], CONV_T), ALU.mult), on=conv_normed)

            softmax(0, 4, HD ** -0.5, gate_attention, 
                    {0: lambda: ada_part(1, 0, 3), 1: lambda: ada_part(1, 3, 2), 2: conv_centre,
                     3: lambda: ada_part(1, 5, 3), 4: lambda: ada_part(1, 8, 2), 5: conv_scale,
                     6: lambda: ada_part(1, 10, 3), 7: lambda: ada_part(1, 13, 3)})
            dve.wait_ge(conv_act, CONV_T)
            dve.wait_ge(unit_evac, ev + 38)
            step(tt(conv[:, 0:6, :], conv[:, 0:6, :], proj[:, 32:38, :], ALU.mult))
            dve.wait_ge(unit_evac, ev + 40)
            step(tt(conv[:, 6:8, :], conv[:, 6:8, :], proj[:, 38:40, :], ALU.mult), on=mix_ready)

            def square_four(j, add_up=True):
                four, squares = flat(x[:, 4 * j:4 * j + 4, :]), sq[:, 1024 * j:1024 * (j + 1)]
                step(tt(squares, four, four, ALU.mult), on=None if add_up else sum_in)
                if add_up:
                    add_tiles(squares, squares, 4)

            def add_residual(name):
                for j in range(4):
                    dve.wait_ge(unit_evac, UNIT0[name] + 4 * (j + 1))
                    x4 = flat(x[:, 4 * j:4 * j + 4, :])
                    step(tt(x4, x4, flat(h[:, 4 * j:4 * j + 4, :]), ALU.add))
                    square_four(j)

            def normed_into_h(norm, scale):
                norm_weight(gs[:, :], norm, scale)
                root()
                for j in range(4):
                    four = slice(4 * j, 4 * j + 4)
                    step(tt(h[:, four, :], x[:, four, :], over_tiles(rstd[:, :], 4), ALU.mult), on=h_scaled)

            counts[h_scaled.name] = 4
            ada_group(2)
            add_residual("ev_out")
            mods_from(1)
            mods_from(2)
            normed_into_h(V("norm_g1"), mod("scale1"))

            ada_group(3)
            od = UNIT0["od"]
            v = proj[:, 0:16, :]
            dve.wait_ge(unit_evac, od + 16)
            add_tiles(sq, flat(v), DT)
            centre(v, DT, 6)
            step(tt(sq[:, :], flat(v), flat(v), ALU.mult))
            add_tiles(sq, sq, DT)
            ada_group(4)
            root()
            scaled(v, v, DT)
            affine(flat(v), DT, V("od_g"), V("od_b"))
            dve.sem_inc(gate_v_ready, 1)
            mods_from(3)
            ada_group(5)
            dve.wait_ge(unit_evac, od + 48)
            uz = flat(proj[:, 16:32, :])
            step(tt(uz, uz, flat(proj[:, 32:48, :]), ALU.mult))
            dve.wait_ge(bs_in, 16)
            for b in range(4):
                dve.wait_ge(sgu_done, b + 1)
                for e in range(2):
                    g = 2 * b + e
                    lo = (b % 2) * 1024 + e * 512
                    step(tt(tiles(flat(proj[:, 2 * g:2 * g + 2, :]), 4), tiles(M[:, lo:lo + 512], 4),
                            over_tiles(att[:, 1024 + g * P:1024 + (g + 1) * P], 4), ALU.add),
                         on=sgu_read if e else None)
                t4 = flat(proj[:, 4 * b:4 * b + 4, :])
                step(tt(t4, t4, uz[:, 1024 * b:1024 * (b + 1)], ALU.mult), on=sgu_ready if b == 3 else None)

            mods_from(4)
            mods_from(5)
            ada_group(6)
            add_residual("od_out")
            root()
            for t in range(DT):
                V_.scalar_tensor_tensor(out=x[:, t, :], in0=x[:, t, :], scalar=V("final_g")[:, t:t + 1], in1=rstd[:, :],
                                        op0=ALU.mult, op1=ALU.mult).then_inc(x_normed, 1)
                if t % 4 == 3:
                    dve.wait_ge(x_normed, t + 1)
                    square_four(t // 4, add_up=False)
            normed_into_h(V("norm1_w"), mod("scale2"))
            mods_from(6)

            gmask = C("gmask").rearrange("p (j g) -> p j g", j=4).unsqueeze(3).to_broadcast([P, 4, 8, 16])

            def expand(dst, name, q, on=None):
                src = square(V(name))[:, 4 * q:4 * q + 4, :].unsqueeze(2).to_broadcast([P, 4, 8, 16])
                step(tt(dst.rearrange("p (j g c) -> p j g c", j=4, g=8), src, gmask, ALU.mult), on=on)

            def expand_b(q):
                expand(att[:, 0:512], "B_re", q)
                expand(att[:, 512:1024], "B_im", q, on=ssm_bc)

            def cross(dst, a, b, c, d, op, on=None):
                times(dst, a, b)
                times(tmp4, c, d)
                step(tt(dst, dst, tmp4, op), on=on)

            expand_b(0)
            dve.wait_ge(f_done, 1)
            z, zmin, ze = cum, f_min, f_exp_row
            step(V_.tensor_scalar(z, B7[0:8, 0:TOK], V("b_forget")[0:8, :], None, ALU.add))
            step(V_.tensor_scalar(zmin, z, 0.0, None, ALU.min))
            step(V_.scalar_tensor_tensor(out=ze, in0=z, scalar=-1.0, in1=z, op0=ALU.mult, op1=ALU.min), on=f_exp_in)
            dve.wait_ge(f_exp, 1)
            step(V_.tensor_scalar(ze, ze, 1.0, None, ALU.add), on=f_ln_in)
            dve.wait_ge(f_ln, 1)
            step(tt(zmin, zmin, ze, ALU.subtract))
            step(V_.tensor_tensor_scan(cum, ones[0:8, 0:1].to_broadcast([8, TOK]), zmin, 0.0, ALU.mult, ALU.add))
            step(V_.tensor_scalar(ncum, cum, -1.0, None, ALU.mult), on=cum_ready)

            def ssm(q):
                expand(sq[:, 1024:1536], "C_re", q)
                expand(sq[:, 1536:2048], "C_im", q)
                step(V_.tensor_copy(turn_cos[:, :, 0:16], seeds[:, 0, 4 * q:4 * q + 4, :]))
                step(V_.tensor_copy(turn_sin[:, :, 0:16], seeds[:, 1, 4 * q:4 * q + 4, :]))
                for k in range(4, 8):
                    double_phases(turn_cos, turn_sin, tmp4, k, powers[:, k, :, 4 * q:4 * q + 4])
                dve.wait_ge(ssm_bu, q + 1)
                bu_re, bu_im = tiles(M[:, 0:1024], 4), tiles(M[:, 1024:2048], 4)
                cross(w_re, bu_re, turn_cos, bu_im, turn_sin, ALU.add)
                cross(w_im, bu_im, turn_cos, bu_re, turn_sin, ALU.subtract)
                if q < 3:
                    expand_b(q + 1)
                for j in range(4):
                    decay = mag[:, 4 * q + j:4 * q + j + 1].to_broadcast([P, TOK])
                    for z_, w_ in ((z_re, w_re), (z_im, w_im)):
                        step(V_.tensor_tensor_scan(z_[:, j * TOK:(j + 1) * TOK], decay, w_[:, j, :], 0.0, ALU.mult,
                                                   ALU.add))
                zr, zi = tiles(z_re, 4), tiles(z_im, 4)
                cross(w_re, zr, turn_cos, zi, turn_sin, ALU.subtract)
                cross(w_im, zr, turn_sin, zi, turn_cos, ALU.add, on=ssm_s)
                dve.wait_ge(ssm_y, q + 1)
                step(V_.scalar_tensor_tensor(out=proj[:, q, :], in0=proj[:, q, :], scalar=V("ssm_D")[:, q:q + 1],
                                             in1=B6[:, 0:TOK], op0=ALU.mult, op1=ALU.add), on=ssm_yd)

            for q in range(4):
                ssm(q)

            wi = UNIT0["w_in"]
            keys_, queries = flat(proj[:, 4:12, :]), flat(proj[:, 12:20, :])
            dve.wait_ge(unit_evac, wi + 12)
            head_squares(keys_, 8, dst=sq)
            dve.wait_ge(unit_evac, wi + 20)
            head_squares(queries, 8)
            head_inverse(0)
            head_inverse(1)
            step(head_scale(keys_, 8, V("k_norm_2")), on=head_used)
            step(head_scale(queries, 8, small[:, 9:10]), on=qk_ready)
            dve.wait_ge(unit_evac, UNIT0["glu"] + 4)
            y4 = flat(proj[:, 0:4, :])
            step(tt(y4, y4, flat(proj[:, 28:32, :]), ALU.mult), on=glu_ready)

            def keep_attention(hh, o):
                step(V_.tensor_copy(proj[:, 12 + hh, :], o), on=o_read)

            softmax(8, 2, 1.0, keep_attention)

            ada_group(7)
            ada_group(8)
            gates = UNIT0["gates"]
            part = lambda a, n: flat(proj[:, a:a + n, :])
            dve.wait_ge(unit_evac, gates + 16)
            step(tt(part(0, 8), part(0, 8), sq[:, 0:2048], ALU.mult))
            step(tt(part(8, 8), part(8, 8), part(28, 8), ALU.mult))
            ada_group(9)
            dve.wait_ge(unit_evac, gates + 28)
            step(tt(part(16, 8), part(16, 8), sq[:, 2048:4096], ALU.mult))
            step(tt(part(24, 4), part(24, 4), part(36, 4), ALU.mult))
            step(tt(part(0, 12), part(0, 12), part(16, 12), ALU.add))
            dve.wait_ge(unit_evac, gates + 32)
            step(tt(part(44, 4), part(44, 4), part(40, 4), ALU.mult))
            step(tt(part(12, 4), part(12, 4), part(44, 4), ALU.add), on=merged)
            mods_from(7)
            mods_from(8)
            add_residual("w_out")
            normed_into_h(V("norm2_w"), mod("scale3"))
            dve.wait_ge(g3_done, 1)
            dve.wait_ge(g3b_in, 16)
            step(tt(att[:, 0:D], att[:, 0:D], M[:, :], ALU.add), on=g3_ready)

            tile = lambda n: flat(proj[:, n:n + 1, :])
            sv = [tile(32 + k).rearrange("p (r k) -> p r k", r=16) for k in range(2)]
            si = [tile(34 + k).bitcast(U32) for k in range(2)]
            tvp = [tile(36), rstd[:, :]]
            tv = [a[:, 0:128].rearrange("p (h k) -> p h k", h=8) for a in tvp]
            tp = [a[:, 128:256].bitcast(U32) for a in tvp]
            masked = tile(37)
            sif = small[:, 16:48].rearrange("p (s k) -> p s k", s=2)
            half_i, half_f = small[:, 48:80].bitcast(U32), small[:, 80:112]
            chosen = powers[:, :, :, :].rearrange("p a b c -> p (a b c)")
            gsum = small[:, 112:128]
            iota = C("iota").unsqueeze(1).to_broadcast([P, 16, 16])

            def top16(values, best, where, width):
                step(V_.max(best[:, 0:8], values))
                step(V_.max_index(where[:, 0:8], best[:, 0:8], values))
                step(V_.match_replace(masked[:, 0:width], best[:, 0:8], values, LOWEST))
                step(V_.max(best[:, 8:16], masked[:, 0:width]))
                step(V_.max_index(where[:, 8:16], best[:, 8:16], masked[:, 0:width]))

            def pick_experts(tk, hh):
                here = slice(hh * SEL, (hh + 1) * SEL)
                pair = flat(proj[:, 16 + 2 * hh + tk:17 + 2 * hh + tk, :])
                pair3 = pair.rearrange("p (a b) -> p a b", a=16)
                step(tt(pair3, sv[tk][:, 2 * hh, :].unsqueeze(2).to_broadcast([P, 16, 16]),
                        sv[tk][:, 2 * hh + 1, :].unsqueeze(1).to_broadcast([P, 16, 16]), ALU.add))
                top16(pair, tv[tk][:, hh, :], tp[tk][:, here], 256)
                step(V_.tensor_copy(small[:, 16:48], si[tk][:, 2 * hh * SEL:(2 * hh + 2) * SEL]))
                step(V_.tensor_scalar(half_i[:, 0:16], tp[tk][:, here], 4, None, ALU.logical_shift_right))
                step(V_.tensor_scalar(half_i[:, 16:32], tp[tk][:, here], 15, None, ALU.bitwise_and))
                step(V_.tensor_copy(half_f, half_i))
                for s in range(2):
                    step(tt(pair3, half_f[:, s * 16:(s + 1) * 16].unsqueeze(2).to_broadcast([P, 16, 16]), iota,
                            ALU.is_equal))
                    step(tt(pair3, pair3, sif[:, s, :].unsqueeze(1).to_broadcast([P, 16, 16]), ALU.mult))
                    step(V_.tensor_reduce(chosen[:, s * 128 + hh * SEL:s * 128 + (hh + 1) * SEL], pair3, AX, ALU.add))
                step(V_.scalar_tensor_tensor(out=chosen[:, here], in0=chosen[:, here], scalar=128.0,
                                             in1=chosen[:, 128 + hh * SEL:128 + (hh + 1) * SEL], op0=ALU.mult, op1=ALU.add))
                at = tk * P + hh * SEL
                step(V_.tensor_copy(tile(38).bitcast(U32)[:, at:at + SEL], chosen[:, here]))

            def top_keys(tk, r):
                top16(proj[:, 16 + r, tk * P:(tk + 1) * P], sv[tk][:, r, :], si[tk][:, r * SEL:(r + 1) * SEL], P)

            def weigh_picks(tk):
                gw = tile(39)[:, tk * P:(tk + 1) * P]
                gw3 = gw.rearrange("p (h k) -> p h k", h=8)
                step(tt(gw3, tv[tk], tv[tk][:, :, 0:1].to_broadcast([P, 8, 16]), ALU.subtract), on=gexp_in)
                dve.wait_ge(gexp_out, tk + 1)
                step(V_.tensor_reduce(gsum[:, 0:8], gw3, AX, ALU.add))
                step(V_.reciprocal(gsum[:, 8:16], gsum[:, 0:8]))
                step(tt(gw3, gw3, gsum[:, 8:16].unsqueeze(2).to_broadcast([P, 8, 16]), ALU.mult), on=picks_ready)

            for hh in range(HEADS):
                dve.wait_ge(sc_copied, 2 * hh + 1)
                for tk in range(2):
                    top_keys(tk, 2 * hh)
                dve.wait_ge(sc_copied, 2 * hh + 2)
                top_keys(0, 2 * hh + 1)
                if hh < HEADS - 1:
                    top_keys(1, 2 * hh + 1)
                pick_experts(0, hh)
            weigh_picks(0)
            top_keys(1, 2 * HEADS - 1)

            dve.wait_ge(unit_done, NUNIT)
            dve.wait_ge(ht_copied, 4)
            step(V_.memset(flat(h[:, :, :]), 0.0))
            dve.wait_ge(sc_done, 16)
            unused = flat(proj[:, 0:8, :])
            for tk in range(2):
                total = flat(h[:, :, :])[:, tk * D:(tk + 1) * D]
                tokens = sq[:, tk * D:(tk + 1) * D]

                def dot(i, s):
                    n = NSLOT * tk + s
                    dve.wait_ge(u_in[s], 16 * (NSLOT // SLOTS * tk + 1) + 16 * i)
                    if not (isinstance(i, int) and n + i == 0):
                        dve.wait_ge(dot_done, n + SLOTS * i)
                    V_.tensor_tensor_reduce(out=unused, in0=tokens, in1=ring[:, s, :], scale=1.0, scalar=0.0,
                                            op0=ALU.mult, op1=ALU.add, accum_out=dots[:, s:s + 1]).then_inc(dot_done, 1)

                def add(i, s):
                    n = NSLOT * tk + s
                    dve.wait_ge(v_in[s], 16 * (NSLOT // SLOTS * tk + 1) + 16 * i)
                    dve.wait_ge(coef_ready, n + 1 + SLOTS * i)
                    if not (isinstance(i, int) and n + i == 0):
                        dve.wait_ge(v_added, n + SLOTS * i)
                    V_.scalar_tensor_tensor(out=total, in0=aring[:, s, :], scalar=dots[:, 2 * SLOTS + s:2 * SLOTS + s + 1],
                                            in1=total, op0=ALU.mult, op1=ALU.add).then_inc(v_added, 1)

                def round_of(i):
                    for s in range(SLOTS):
                        dot(i, s)
                        if s > 0:
                            add(i, s - 1)
                    add(i, SLOTS - 1)

                if tk == 0:
                    for hh in range(HEADS):
                        round_of(hh)
                        pick_experts(1, hh)
                    weigh_picks(1)
                with dve.Fori(HEADS if tk == 0 else 0, NSLOT // SLOTS) as i:
                    round_of(i)
                dve.wait_ge(v_added, NSLOT * (tk + 1))
                step(tt(total, total, att[:, 0:D], ALU.mult))
                dve.wait_ge(ht_copied, 8)
                step(tt(total, total, acc[:, tk, :], ALU.add), on=out_ready)


def kernel(**inputs):
    import concourse.bacc as bacc
    from concourse.bass_utils import run_bass_kernel_spmd as run

    a = {k: np.asarray(v) for k, v in inputs.items()}

    def feature_major(v):
        return v.reshape(-1, P).T

    def tokens_last(m):
        return np.ascontiguousarray(m.T.reshape(-1, P, TOK).transpose(1, 0, 2)).reshape(P, -1)

    def chunks(w):
        k, n = w.shape
        per = D // k
        t = w.reshape(k // P, P, n // (P * per), per, P).transpose(2, 1, 3, 0, 4)
        return t.reshape(n // (P * per), P, CHUNK)

    ev = a["ev_w_in"][0]
    kv, q, za, ga, gb, zb = np.split(ev, [512, 1536, 2560, 3584, 4608], axis=1)
    u_, v_, z_ = np.split(a["od_w_in"][0], 3, axis=1)
    q2, k2, v2, f2, s2, gs2, ga2 = np.split(a["w_in_2"][0], [1024, 2048, 3072, 3080, 3592, 5640], axis=1)
    parts = [kv, ga, gb, q, za, zb, a["ev_w_out"][0], v_, u_, z_, a["od_w_out"][0], s2, k2, q2, v2, a["w_glu_2"][0],
             a["w_ssm_up_2"][0], a["w_attn_up_2"][0], gs2, ga2, a["w_out_2"][0], a["w_peer_q_2"][0]]
    weights = np.concatenate([chunks(w) for w in parts])
    assert len(weights) == NCHUNK

    a0, a1, a2 = a["ada_w"][0], a["ada_w"][1], a["w_ada_2"][0]
    groups = [(a0, 0), (a0, 1), (a0, 2), (a1, 0), (a1, 1), (a1, 2)] + [(a2, i) for i in range(6)]
    ada = np.concatenate([w[:, D * i:D * (i + 1)].reshape(DT, P, D) for w, i in groups])
    biases = np.concatenate([a["ada_b"][0], a["ada_b"][1], a["b_ada_2"][0]])

    vecs = np.zeros((P, NVEC), np.float32)

    def put(name, v):
        at, w = VEC[name]
        vecs[:, at:at + w] = v

    conds = np.ascontiguousarray(np.concatenate([feature_major(a["c"]), feature_major(a["c_ctx"]), feature_major(a["c_2"])], axis=1))
    put("ada_b", feature_major(biases))
    for name, v in (("norm_g0", a["norm_g"][0]), ("norm_g1", a["norm_g"][1]), ("final_g", a["final_g"]),
                    ("norm1_w", a["norm1_w_2"]), ("norm2_w", a["norm2_w_2"]), ("q_norm", a["ev_q_norm"]),
                    ("k_norm", a["ev_k_norm"]), ("q_norm_2", a["q_norm_w_2"]), ("k_norm_2", a["k_norm_w_2"]),
                    ("dw_b", a["ev_dw_b"]), ("ln_g", a["ev_ln_g"]), ("ln_b", a["ev_ln_b"]), ("od_g", a["od_ln_g"]),
                    ("od_b", a["od_ln_b"]), ("A_re", a["ssm_A_re_2"]), ("A_im", a["ssm_A_im_2"]),
                    ("log_dt", np.repeat(a["ssm_log_dt_2"][0], 64)), ("ssm_D", a["ssm_D_2"]), ("b_glu", a["b_glu_2"])):
        put(name, feature_major(v))
    put("dw_w", a["ev_dw_w"][0].reshape(CONV_W, CONV_T, P).transpose(2, 1, 0).reshape(P, -1))
    vecs[0:8, VEC["b_forget"][0]] = a["b_forget_2"][0]
    for name in ("B_re", "B_im"):
        put(name, a[f"ssm_{name}_2"][0].reshape(16, P, 16).transpose(1, 0, 2).reshape(P, -1))
    for name in ("C_re", "C_im"):
        put(name, a[f"ssm_{name}_2"][0].transpose(0, 2, 1).reshape(16, P, 16).transpose(1, 0, 2).reshape(P, -1))
    put("w_f", f2.reshape(DT, P, 8).transpose(1, 0, 2).reshape(P, -1))

    arrays = {
        "xT": tokens_last(a["x"][0]), "ctxT": tokens_last(a["ctx"][0]), "consts": constants(), "conds": conds, "vecs": vecs,
        "weights": weights, "ada": ada,
        "keysT": np.ascontiguousarray(a["peer_sub_keys_2"][0].reshape(16, P, P).transpose(2, 0, 1)).reshape(P, -1),
        "wsT": np.ascontiguousarray(a["od_ws"][0].transpose(2, 0, 1)).reshape(P, -1),
        "bs": np.ascontiguousarray(a["od_bs"][0]).reshape(-1),
        "g3_bias": np.ascontiguousarray(a["b_ada_2"][0][5 * D:]),
        "peer_u": np.ascontiguousarray(a["peer_u_2"][0]), "peer_v": np.ascontiguousarray(a["peer_v_2"][0]),
    }
    nc = bacc.Bacc("TRN2", target_bir_lowering=False, num_devices=1)
    args = [nc.dram_tensor(n, v.shape, F32, kind="ExternalInput").ap() for n, v in arrays.items()]
    out = nc.dram_tensor("out", (TOK, D), F32, kind="ExternalOutput").ap()
    build(nc, *args, out)
    r = run(nc, [arrays], core_ids=[0])
    return r.results[0]["out"].reshape(1, TOK, D)
```
